# Optimizing a Trainium2 kernel written in Bass

```python
import math
import jax, jax.numpy as jnp
from jax import lax
import numpy as np

D_MODEL = 1024
BATCH = 1
SEQ = 1024
DEPTH = 2

CTX_LEN = 256
GRID_W = 64
Q_BLOCK = 128
ROPE_BASE = 10000.0
EPS = 1e-6

GQA_HEADS = 8
GQA_KV_HEADS = 2
GQA_HEAD_DIM = 64
MLA_HEADS = 8
MLA_Q_RANK = 256
MLA_KV_RANK = 128
MLA_NOPE_DIM = 64
MLA_ROPE_DIM = 32
MLA_V_DIM = 64
ATTN_WIDTH = GQA_HEADS * GQA_HEAD_DIM + MLA_HEADS * MLA_V_DIM
ATTN_SPLITS = (GQA_HEADS * GQA_HEAD_DIM, GQA_KV_HEADS * GQA_HEAD_DIM, GQA_KV_HEADS * GQA_HEAD_DIM,
               MLA_Q_RANK, MLA_KV_RANK, MLA_ROPE_DIM, ATTN_WIDTH)
ATTN_IN = (GQA_HEADS + 2 * GQA_KV_HEADS) * GQA_HEAD_DIM + MLA_Q_RANK + MLA_KV_RANK + MLA_ROPE_DIM + ATTN_WIDTH
HY_WIDTH = D_MODEL
HY_ORDER = 2
HY_SHORT = 3
HY_BANDS = 16
HY_EMB = 1 + 2 * HY_BANDS
HY_FFN = 64
HY_FAST_DECAY = 0.3
HY_SLOW_DECAY = 1.5
HY_DECAY_TARGET = 1e-2


def _f32(a):
    return a.astype(jnp.float32)

def split_cols(p, sizes):
    out, start = [], 0
    for n in sizes:
        out.append(p[..., start:start + n])
        start += n
    return out

def rms_norm(x, w):
    xf = _f32(x)
    y = xf * lax.rsqrt(jnp.mean(xf * xf, axis=-1, keepdims=True) + EPS)
    return (y * _f32(w)).astype(x.dtype)

def modulate(x, norm_w, shift, scale):
    return rms_norm(x, norm_w) * (1 + scale) + shift

def axial_rope_tables(n_tokens, rot_dim):
    n_rows = n_tokens // GRID_W
    rows = jnp.repeat(jnp.arange(n_rows, dtype=jnp.int32), GRID_W)
    cols = jnp.tile(jnp.arange(GRID_W, dtype=jnp.int32), n_rows)
    quarter = rot_dim // 4
    inv_freq = ROPE_BASE ** (-jnp.arange(quarter, dtype=jnp.float32) / quarter)
    ang_r = _f32(rows)[:, None] * inv_freq
    ang_c = _f32(cols)[:, None] * inv_freq
    return (jnp.cos(ang_r), jnp.sin(ang_r), jnp.cos(ang_c), jnp.sin(ang_c))

def rotate_pairs(x, cos, sin):
    a, b = jnp.split(x, 2, axis=-1)
    return jnp.concatenate([a * cos - b * sin, b * cos + a * sin], axis=-1)

def apply_axial_rope(x, tables):
    cr, sr, cc, sc = (t[:, None, :].astype(x.dtype) for t in tables)
    xr, xc = jnp.split(x, 2, axis=-1)
    return jnp.concatenate([rotate_pairs(xr, cr, sr), rotate_pairs(xc, cc, sc)], axis=-1)

def block_attention(q, k, v, scale):
    B, Lq, Hkv, G, d = q.shape
    nb = Lq // Q_BLOCK
    kf, vf = _f32(k), _f32(v)
    qb = jnp.moveaxis(q.reshape(B, nb, Q_BLOCK, Hkv, G, d), 1, 0)

    def one_block(qi):
        s = jnp.einsum("bqhgd,bkhd->bhgqk", _f32(qi), kf) * scale
        p = jax.nn.softmax(s, axis=-1)
        return jnp.einsum("bhgqk,bkhe->bqhge", p, vf)

    o = lax.map(one_block, qb)
    return jnp.moveaxis(o, 0, 1).reshape(B, Lq, Hkv * G, v.shape[-1]).astype(v.dtype)

def attn_project(h, w_in, q_norm_w, k_norm_w, cq_norm_w, ckv_norm_w, w_uq, w_ukv, rope_a, rope_m):
    B, L, _ = h.shape
    q_a, k_a, v_a, c_q, c_kv, k_pe, gate = split_cols(h @ w_in, ATTN_SPLITS)
    q_a = rms_norm(q_a.reshape(B, L, GQA_HEADS, GQA_HEAD_DIM), q_norm_w)
    k_a = rms_norm(k_a.reshape(B, L, GQA_KV_HEADS, GQA_HEAD_DIM), k_norm_w)
    v_a = v_a.reshape(B, L, GQA_KV_HEADS, GQA_HEAD_DIM)
    q_m = (rms_norm(c_q, cq_norm_w) @ w_uq).reshape(B, L, MLA_HEADS, MLA_NOPE_DIM + MLA_ROPE_DIM)
    kv_m = (rms_norm(c_kv, ckv_norm_w) @ w_ukv).reshape(B, L, MLA_HEADS, MLA_NOPE_DIM + MLA_V_DIM)
    q_nope, q_pe = q_m[..., :MLA_NOPE_DIM], q_m[..., MLA_NOPE_DIM:]
    k_nope, v_m = kv_m[..., :MLA_NOPE_DIM], kv_m[..., MLA_NOPE_DIM:]
    k_pe = k_pe.reshape(B, L, 1, MLA_ROPE_DIM)
    if rope_a is not None:
        q_a = apply_axial_rope(q_a, rope_a)
        k_a = apply_axial_rope(k_a, rope_a)
        q_pe = apply_axial_rope(q_pe, rope_m)
        k_pe = apply_axial_rope(k_pe, rope_m)
    q_m = jnp.concatenate([q_nope, q_pe], axis=-1)
    k_m = jnp.concatenate([k_nope, jnp.broadcast_to(k_pe, (B, L, MLA_HEADS, MLA_ROPE_DIM))], axis=-1)
    return q_a, k_a, v_a, q_m, k_m, v_m, gate

def attn_mixer(h_lat, h_ctx, w_in, q_norm_w, k_norm_w, cq_norm_w, ckv_norm_w, w_uq, w_ukv, w_out, with_ctx_out):
    L = h_lat.shape[1]
    rope_a = axial_rope_tables(L, GQA_HEAD_DIM)
    rope_m = axial_rope_tables(L, MLA_ROPE_DIM)
    lq_a, lk_a, lv_a, lq_m, lk_m, lv_m, l_gate = attn_project(
        h_lat, w_in, q_norm_w, k_norm_w, cq_norm_w, ckv_norm_w, w_uq, w_ukv, rope_a, rope_m)
    cq_a, ck_a, cv_a, cq_m, ck_m, cv_m, c_gate = attn_project(
        h_ctx, w_in, q_norm_w, k_norm_w, cq_norm_w, ckv_norm_w, w_uq, w_ukv, None, None)

    def mix(q_a, q_m, gate, k_a, v_a, k_m, v_m):
        B, Lq = q_a.shape[:2]
        o_a = block_attention(q_a.reshape(B, Lq, GQA_KV_HEADS, GQA_HEADS // GQA_KV_HEADS, GQA_HEAD_DIM),
                              k_a, v_a, GQA_HEAD_DIM ** -0.5)
        o_m = block_attention(q_m[:, :, :, None, :], k_m, v_m, (MLA_NOPE_DIM + MLA_ROPE_DIM) ** -0.5)
        o = jnp.concatenate([o_a.reshape(B, Lq, -1), o_m.reshape(B, Lq, -1)], axis=-1)
        return (o * jax.nn.silu(gate)) @ w_out

    y_lat = mix(lq_a, lq_m, l_gate,
                jnp.concatenate([ck_a, lk_a], axis=1), jnp.concatenate([cv_a, lv_a], axis=1),
                jnp.concatenate([ck_m, lk_m], axis=1), jnp.concatenate([cv_m, lv_m], axis=1))
    y_ctx = mix(cq_a, cq_m, c_gate, ck_a, cv_a, ck_m, cv_m) if with_ctx_out else None
    return y_lat, y_ctx

def hyena_filters(L, w1, b1, w2, b2, w3, b3, freq):
    t = jnp.linspace(0.0, 1.0, L, dtype=jnp.float32)[:, None]
    w = (2.0 * math.pi / L) * jnp.arange(L, dtype=jnp.float32)[:, None]
    bands = jnp.linspace(1e-4, HY_BANDS - 1, HY_BANDS, dtype=jnp.float32)
    emb = jnp.concatenate([t, jnp.cos(w * bands), -jnp.sin(w * bands)], axis=-1)
    hid = jnp.sin(_f32(freq) * (emb @ _f32(w1) + _f32(b1)))
    hid = jnp.sin(_f32(freq) * (hid @ _f32(w2) + _f32(b2)))
    h = (hid @ _f32(w3) + _f32(b3)).reshape(L, HY_ORDER, 2, HY_WIDTH)
    max_decay = math.log(HY_DECAY_TARGET) / HY_FAST_DECAY
    min_decay = math.log(HY_DECAY_TARGET) / HY_SLOW_DECAY
    deltas = jnp.linspace(min_decay, max_decay, HY_WIDTH, dtype=jnp.float32)
    h = h * jnp.exp(-t * jnp.abs(deltas))[:, None, None, :]
    fwd, bwd = h[:, :, 0], h[:, :, 1]
    kern = jnp.concatenate([fwd, jnp.zeros((1, HY_ORDER, HY_WIDTH), jnp.float32), bwd[:0:-1]], axis=0)
    kern = kern / jnp.sum(jnp.abs(kern), axis=0, keepdims=True)
    return jnp.fft.rfft(kern, axis=0)

def long_conv(u, k_f, skip):
    L = u.shape[1]
    uf = _f32(u)
    y = jnp.fft.irfft(jnp.fft.rfft(uf, n=2 * L, axis=1) * k_f, n=2 * L, axis=1)[:, :L]
    return (y + uf * _f32(skip)).astype(u.dtype)

def short_conv(u, w, b):
    L = u.shape[1]
    pad = HY_SHORT // 2
    up = jnp.pad(u, ((0, 0), (pad, pad), (0, 0)))
    return sum(up[:, j:j + L] * w[j] for j in range(HY_SHORT)) + b

def hyena_mixer(h, w_in, conv_w, conv_b, f_w1, f_b1, f_w2, f_b2, f_w3, f_b3, freq, skip, w_out):
    L = h.shape[1]
    p = h @ w_in
    u = short_conv(p[..., :(HY_ORDER + 1) * HY_WIDTH], conv_w, conv_b)
    gate = p[..., (HY_ORDER + 1) * HY_WIDTH:]
    parts = jnp.split(u, HY_ORDER + 1, axis=-1)
    k_f = hyena_filters(L, f_w1, f_b1, f_w2, f_b2, f_w3, f_b3, freq)
    z = parts[0]
    for o in range(HY_ORDER):
        z = parts[o + 1] * long_conv(z, k_f[:, o], skip[o])
    return (z * jax.nn.silu(gate)) @ w_out

def first_inputs(seed: int = 0) -> dict:
    key = jax.random.key(seed)
    ks = jax.random.split(key, 32)
    n_attn = (DEPTH + 1) // 2
    n_hy = DEPTH // 2
    f32 = jnp.float32

    def nrm(k, shape, fan_in):
        return jax.random.normal(k, shape, f32) * fan_in ** -0.5

    def gain(k, shape):
        return 1.0 + 0.05 * jax.random.normal(k, shape, f32)

    def small(k, shape, s=0.02):
        return s * jax.random.normal(k, shape, f32)

    return {
        "x": jax.random.normal(ks[0], (BATCH, SEQ, D_MODEL), f32),
        "c": jax.random.normal(ks[1], (BATCH, D_MODEL), f32),
        "ctx": jax.random.normal(ks[2], (BATCH, CTX_LEN, D_MODEL), f32),
        "c_ctx": jax.random.normal(ks[3], (D_MODEL,), f32),
        "ada_w": nrm(ks[4], (DEPTH, D_MODEL, 3 * D_MODEL), D_MODEL),
        "ada_b": small(ks[5], (DEPTH, 3 * D_MODEL)),
        "norm_w": gain(ks[6], (DEPTH, D_MODEL)),
        "attn_w_in": nrm(ks[7], (n_attn, D_MODEL, ATTN_IN), D_MODEL),
        "attn_q_norm": gain(ks[8], (n_attn, GQA_HEAD_DIM)),
        "attn_k_norm": gain(ks[9], (n_attn, GQA_HEAD_DIM)),
        "mla_q_norm": gain(ks[10], (n_attn, MLA_Q_RANK)),
        "mla_kv_norm": gain(ks[11], (n_attn, MLA_KV_RANK)),
        "mla_w_uq": nrm(ks[12], (n_attn, MLA_Q_RANK, MLA_HEADS * (MLA_NOPE_DIM + MLA_ROPE_DIM)), MLA_Q_RANK),
        "mla_w_ukv": nrm(ks[13], (n_attn, MLA_KV_RANK, MLA_HEADS * (MLA_NOPE_DIM + MLA_V_DIM)), MLA_KV_RANK),
        "attn_w_out": nrm(ks[14], (n_attn, ATTN_WIDTH, D_MODEL), ATTN_WIDTH),
        "hy_w_in": nrm(ks[15], (n_hy, D_MODEL, (HY_ORDER + 2) * HY_WIDTH), D_MODEL),
        "hy_conv_w": nrm(ks[16], (n_hy, HY_SHORT, (HY_ORDER + 1) * HY_WIDTH), HY_SHORT),
        "hy_conv_b": small(ks[17], (n_hy, (HY_ORDER + 1) * HY_WIDTH)),
        "hy_ffn_w1": nrm(ks[18], (n_hy, HY_EMB, HY_FFN), HY_EMB),
        "hy_ffn_b1": small(ks[19], (n_hy, HY_FFN), 0.1),
        "hy_ffn_w2": nrm(ks[20], (n_hy, HY_FFN, HY_FFN), HY_FFN),
        "hy_ffn_b2": small(ks[21], (n_hy, HY_FFN), 0.1),
        "hy_ffn_w3": nrm(ks[22], (n_hy, HY_FFN, HY_ORDER * 2 * HY_WIDTH), HY_FFN),
        "hy_ffn_b3": small(ks[23], (n_hy, HY_ORDER * 2 * HY_WIDTH), 0.1),
        "hy_freq": gain(ks[24], (n_hy, HY_FFN)),
        "hy_skip": small(ks[25], (n_hy, HY_ORDER, HY_WIDTH), 0.1),
        "hy_w_out": nrm(ks[26], (n_hy, HY_WIDTH, D_MODEL), HY_WIDTH),
        "final_norm_w": gain(ks[27], (D_MODEL,)),
    }

def first_block(x, c, ctx, c_ctx, ada_w, ada_b, norm_w, attn_w_in, attn_q_norm, attn_k_norm,
              mla_q_norm, mla_kv_norm, mla_w_uq, mla_w_ukv, attn_w_out, hy_w_in, hy_conv_w, hy_conv_b,
              hy_ffn_w1, hy_ffn_b1, hy_ffn_w2, hy_ffn_b2, hy_ffn_w3, hy_ffn_b3, hy_freq, hy_skip,
              hy_w_out, final_norm_w):
    last_attn = (DEPTH - 1) - ((DEPTH - 1) % 2)
    s_lat = jax.nn.silu(c)
    s_ctx = jax.nn.silu(c_ctx)
    x_lat, x_ctx = x, ctx
    for i in range(DEPTH):
        j = i // 2
        ctx_update = i < last_attn
        shift, scale, gate = jnp.split(s_lat @ ada_w[i] + ada_b[i], 3, axis=-1)
        h_lat = modulate(x_lat, norm_w[i], shift[:, None], scale[:, None])
        need_ctx = (i % 2 == 0) or ctx_update
        if need_ctx:
            shift_c, scale_c, gate_c = jnp.split(s_ctx @ ada_w[i] + ada_b[i], 3, axis=-1)
            h_ctx = modulate(x_ctx, norm_w[i], shift_c, scale_c)
        if i % 2 == 0:
            y_lat, y_ctx = attn_mixer(h_lat, h_ctx, attn_w_in[j], attn_q_norm[j], attn_k_norm[j],
                                      mla_q_norm[j], mla_kv_norm[j], mla_w_uq[j], mla_w_ukv[j],
                                      attn_w_out[j], ctx_update)
        else:
            hy_args = (hy_w_in[j], hy_conv_w[j], hy_conv_b[j], hy_ffn_w1[j], hy_ffn_b1[j], hy_ffn_w2[j],
                       hy_ffn_b2[j], hy_ffn_w3[j], hy_ffn_b3[j], hy_freq[j], hy_skip[j], hy_w_out[j])
            y_lat = hyena_mixer(h_lat, *hy_args)
            y_ctx = hyena_mixer(h_ctx, *hy_args) if ctx_update else None
        x_lat = x_lat + gate[:, None] * y_lat
        if ctx_update:
            x_ctx = x_ctx + gate_c * y_ctx
    return rms_norm(x_lat, final_norm_w)


DEPTH_2 = 1

BRANCH_WIDTH = D_MODEL // 2
N_BRANCHES = 4
CHUNK = 64
CONV_WIDTH = 4
NORM_EPS = 1e-6

HGRN_HEADS = 4
HGRN_EXPAND = BRANCH_WIDTH // HGRN_HEADS
HGRN_FDIM = HGRN_HEADS * HGRN_EXPAND
HGRN_VDIM = BRANCH_WIDTH
HGRN_VHEAD = HGRN_VDIM // HGRN_HEADS
SSD_DINNER = BRANCH_WIDTH
SSD_HEADDIM = 64
SSD_HEADS = SSD_DINNER // SSD_HEADDIM
SSD_GROUPS = 2
SSD_HPG = SSD_HEADS // SSD_GROUPS
SSD_STATE = 64
SSD_CONV_DIM = SSD_DINNER + 2 * SSD_GROUPS * SSD_STATE
GLA_HEADS = 4
GLA_KDIM = BRANCH_WIDTH // 2
GLA_VDIM = BRANCH_WIDTH
GLA_HEAD_K = GLA_KDIM // GLA_HEADS
GLA_HEAD_V = GLA_VDIM // GLA_HEADS
GLA_GATE_RANK = 16
GLA_GATE_NORMALIZER = 16.0
LRU_WIDTH = BRANCH_WIDTH
LRU_BLOCKS = 8
LRU_BLOCK = LRU_WIDTH // LRU_BLOCKS
LRU_C = 8.0
D_FF = ((8 * D_MODEL // 3 + 255) // 256) * 256

IN_SPLITS = (
    HGRN_FDIM, HGRN_FDIM, HGRN_VDIM, HGRN_VDIM,
    SSD_DINNER, SSD_CONV_DIM, SSD_HEADS,
    GLA_KDIM, GLA_KDIM, GLA_VDIM, GLA_VDIM, GLA_GATE_RANK,
    LRU_WIDTH, LRU_WIDTH,
    N_BRANCHES * D_MODEL,
)
D_IN = sum(IN_SPLITS)


F32 = jnp.float32

def rmsnorm(x, w):
    xf = x.astype(F32)
    y = xf * lax.rsqrt(jnp.mean(xf * xf, axis=-1, keepdims=True) + NORM_EPS)
    return (y * w.astype(F32)).astype(x.dtype)

def causal_dwconv(x, w, b):
    c = x.shape[-1]
    y = lax.conv_general_dilated(
        x, w[:, None, :].astype(x.dtype), window_strides=(1,),
        padding=[(w.shape[0] - 1, 0)], dimension_numbers=("NWC", "WIO", "NWC"),
        feature_group_count=c)
    return y + b.astype(x.dtype)

def chunk_gated_linear_attn(q, k, v, log_f):
    bsz, seqlen, nh, dk = q.shape
    dv = v.shape[-1]
    n = seqlen // CHUNK

    def to_chunks(t):
        return jnp.moveaxis(t.astype(F32).reshape(bsz, n, CHUNK, nh, t.shape[-1]), 1, 0)

    qc, kc, vc, gc = to_chunks(q), to_chunks(k), to_chunks(v), to_chunks(log_f)
    causal = jnp.tril(jnp.ones((CHUNK, CHUNK), bool))

    def step(state, inp):
        qi, ki, vi, gi = inp
        bcum = jnp.cumsum(gi, axis=1)
        rel = bcum[:, :, None] - bcum[:, None, :]
        rel = jnp.where(causal[None, :, :, None, None], rel, -jnp.inf)
        scores = jnp.einsum('bihd,bjhd,bijhd->bhij', qi, ki, jnp.exp(rel))
        o_intra = jnp.einsum('bhij,bjhv->bihv', scores, vi)
        o_inter = jnp.einsum('bihd,bhdv->bihv', qi * jnp.exp(bcum), state)
        b_last = bcum[:, -1:]
        k_dec = ki * jnp.exp(b_last - bcum)
        new_state = state * jnp.exp(b_last[:, 0])[..., None] + jnp.einsum('bjhd,bjhv->bhdv', k_dec, vi)
        return new_state, o_intra + o_inter

    s0 = jnp.zeros((bsz, nh, dk, dv), F32)
    _, o = lax.scan(step, s0, (qc, kc, vc, gc))
    return jnp.moveaxis(o, 0, 1).reshape(bsz, seqlen, nh, dv)

def hgrn2_branch(q, f_pre, i, g, lb, norm_w):
    bsz, seqlen, _ = q.shape
    lbf = lb.astype(F32)
    log_f = jnp.logaddexp(jnp.log(lbf), jnp.log1p(-lbf) + jax.nn.log_sigmoid(f_pre.astype(F32)))
    key = -jnp.expm1(log_f)
    qf = jax.nn.silu(q.astype(F32))
    hk = lambda t: t.reshape(bsz, seqlen, HGRN_HEADS, HGRN_EXPAND)
    hv = lambda t: t.reshape(bsz, seqlen, HGRN_HEADS, HGRN_VHEAD)
    o = chunk_gated_linear_attn(hk(qf), hk(key), hv(i.astype(F32)), hk(log_f))
    o = rmsnorm(o, norm_w) * jax.nn.silu(hv(g.astype(F32)))
    return o.reshape(bsz, seqlen, HGRN_VDIM)

def gla_branch(q, k, v, g, gate_lr, gate_w, gate_b, norm_w):
    bsz, seqlen, _ = q.shape
    log_a = jax.nn.log_sigmoid(gate_lr.astype(F32) @ gate_w.astype(F32) + gate_b.astype(F32)) / GLA_GATE_NORMALIZER
    hk = lambda t: t.astype(F32).reshape(bsz, seqlen, GLA_HEADS, GLA_HEAD_K)
    hv = lambda t: t.astype(F32).reshape(bsz, seqlen, GLA_HEADS, GLA_HEAD_V)
    o = chunk_gated_linear_attn(hk(q) * (GLA_HEAD_K ** -0.5), hk(k), hv(v), hk(log_a))
    o = rmsnorm(o, norm_w) * jax.nn.silu(hv(g))
    return o.reshape(bsz, seqlen, GLA_VDIM)

def ssd_branch(z, xbc, dt_raw, conv_w, conv_b, dt_bias, a_log, d_skip, norm_w):
    bsz, seqlen, _ = z.shape
    n = seqlen // CHUNK
    xbc = jax.nn.silu(causal_dwconv(xbc, conv_w, conv_b).astype(F32))
    xs, bm, cm = jnp.split(xbc, [SSD_DINNER, SSD_DINNER + SSD_GROUPS * SSD_STATE], axis=-1)
    dt = jax.nn.softplus(dt_raw.astype(F32) + dt_bias.astype(F32))
    a_neg = -jnp.exp(a_log.astype(F32)).reshape(SSD_GROUPS, SSD_HPG)
    x_c = xs.reshape(bsz, n, CHUNK, SSD_GROUPS, SSD_HPG, SSD_HEADDIM)
    dt_c = dt.reshape(bsz, n, CHUNK, SSD_GROUPS, SSD_HPG)
    b_c = bm.reshape(bsz, n, CHUNK, SSD_GROUPS, SSD_STATE)
    c_c = cm.reshape(bsz, n, CHUNK, SSD_GROUPS, SSD_STATE)
    a_cs = jnp.cumsum(dt_c * a_neg, axis=2)
    xdt = x_c * dt_c[..., None]
    causal = jnp.tril(jnp.ones((CHUNK, CHUNK), bool))
    seg = a_cs[:, :, :, None] - a_cs[:, :, None, :]
    lmat = jnp.exp(jnp.where(causal[None, None, :, :, None, None], seg, -jnp.inf))
    y_diag = jnp.einsum('bcigs,bcjgs,bcijgh,bcjghp->bcighp', c_c, b_c, lmat, xdt)
    decay_states = jnp.exp(a_cs[:, :, -1:] - a_cs)
    states = jnp.einsum('bcjgs,bcjgh,bcjghp->bcghps', b_c, decay_states, xdt)
    cs = jnp.cumsum(a_cs[:, :, -1], axis=1)
    rel = cs[:, :, None] - cs[:, None, :]
    ctril = jnp.tril(jnp.ones((n, n), bool))
    carried = jnp.einsum('bzcgh,bcghps->bzghps',
                         jnp.exp(jnp.where(ctril[None, :, :, None, None], rel, -jnp.inf)), states)
    prev = jnp.concatenate([jnp.zeros_like(carried[:, :1]), carried[:, :-1]], axis=1)
    y_off = jnp.einsum('bcigs,bcghps,bcigh->bcighp', c_c, prev, jnp.exp(a_cs))
    y = y_diag + y_off + x_c * d_skip.astype(F32).reshape(SSD_GROUPS, SSD_HPG)[..., None]
    y = y.reshape(bsz, seqlen, SSD_DINNER) * jax.nn.silu(z.astype(F32))
    yg = y.reshape(bsz, seqlen, SSD_GROUPS, SSD_DINNER // SSD_GROUPS)
    yg = yg * lax.rsqrt(jnp.mean(yg * yg, axis=-1, keepdims=True) + NORM_EPS)
    return yg.reshape(bsz, seqlen, SSD_DINNER) * norm_w.astype(F32)

def rglru_branch(xb, gate, conv_w, conv_b, wa, ba, wx, bx, lam):
    bsz, seqlen, _ = xb.shape
    u = causal_dwconv(xb, conv_w, conv_b).astype(F32)
    ub = u.reshape(bsz, seqlen, LRU_BLOCKS, LRU_BLOCK)
    r = jax.nn.sigmoid(jnp.einsum('blkd,kde->blke', ub, wa.astype(F32)).reshape(bsz, seqlen, LRU_WIDTH) + ba.astype(F32))
    i = jax.nn.sigmoid(jnp.einsum('blkd,kde->blke', ub, wx.astype(F32)).reshape(bsz, seqlen, LRU_WIDTH) + bx.astype(F32))
    log_a = -LRU_C * r * jax.nn.softplus(-lam.astype(F32))
    a = jnp.exp(log_a)
    bterm = jnp.sqrt(-jnp.expm1(2.0 * log_a)) * (i * u)

    def combine(e1, e2):
        a1, b1 = e1
        a2, b2 = e2
        return a1 * a2, a2 * b1 + b2

    _, h = lax.associative_scan(combine, (a, bterm), axis=1)
    return h * jax.nn.gelu(gate.astype(F32), approximate=True)

def second_inputs(seed: int = 0) -> dict:
    key = jax.random.key(seed)
    ks = jax.random.split(key, 32)
    nrm = lambda k, shape, scale: jax.random.normal(k, shape, F32) * scale
    gain = lambda k, shape: 1.0 + 0.02 * jax.random.normal(k, shape, F32)
    dt = jnp.exp(jax.random.uniform(ks[8], (DEPTH_2, SSD_HEADS), F32, math.log(1e-3), math.log(1e-1)))
    lam_u = jax.random.uniform(ks[19], (DEPTH_2, LRU_WIDTH), F32, 0.9, 0.999) ** (1.0 / LRU_C)
    return {
        "x": nrm(ks[0], (BATCH, SEQ, D_MODEL), 1.0),
        "norm_mix_w": gain(ks[1], (DEPTH_2, D_MODEL)),
        "w_in": nrm(ks[2], (DEPTH_2, D_MODEL, D_IN), D_MODEL ** -0.5),
        "hgrn_lower_bounds": nrm(ks[3], (DEPTH_2, HGRN_FDIM), 0.1),
        "hgrn_norm_w": gain(ks[4], (DEPTH_2, HGRN_VHEAD)),
        "ssd_conv_w": nrm(ks[5], (DEPTH_2, CONV_WIDTH, SSD_CONV_DIM), CONV_WIDTH ** -0.5),
        "ssd_conv_b": nrm(ks[6], (DEPTH_2, SSD_CONV_DIM), 0.01),
        "ssd_dt_bias": dt + jnp.log(-jnp.expm1(-dt)),
        "ssd_a_log": jnp.log(jax.random.uniform(ks[9], (DEPTH_2, SSD_HEADS), F32, 1.0, 16.0)),
        "ssd_d": gain(ks[10], (DEPTH_2, SSD_HEADS)),
        "ssd_norm_w": gain(ks[11], (DEPTH_2, SSD_DINNER)),
        "gla_gate_w": nrm(ks[12], (DEPTH_2, GLA_GATE_RANK, GLA_KDIM), GLA_GATE_RANK ** -0.5),
        "gla_gate_b": nrm(ks[13], (DEPTH_2, GLA_KDIM), 0.01),
        "gla_norm_w": gain(ks[14], (DEPTH_2, GLA_HEAD_V)),
        "lru_conv_w": nrm(ks[15], (DEPTH_2, CONV_WIDTH, LRU_WIDTH), CONV_WIDTH ** -0.5),
        "lru_conv_b": nrm(ks[16], (DEPTH_2, LRU_WIDTH), 0.01),
        "lru_wa": nrm(ks[17], (DEPTH_2, LRU_BLOCKS, LRU_BLOCK, LRU_BLOCK), LRU_BLOCK ** -0.5),
        "lru_ba": nrm(ks[18], (DEPTH_2, LRU_WIDTH), 0.01),
        "lru_wx": nrm(ks[20], (DEPTH_2, LRU_BLOCKS, LRU_BLOCK, LRU_BLOCK), LRU_BLOCK ** -0.5),
        "lru_bx": nrm(ks[21], (DEPTH_2, LRU_WIDTH), 0.01),
        "lru_lambda": jnp.log(lam_u) - jnp.log1p(-lam_u),
        "w_branch": nrm(ks[22], (DEPTH_2, N_BRANCHES, BRANCH_WIDTH, D_MODEL), BRANCH_WIDTH ** -0.5),
        "w_out": nrm(ks[23], (DEPTH_2, D_MODEL, D_MODEL), D_MODEL ** -0.5),
        "norm_ffn_w": gain(ks[24], (DEPTH_2, D_MODEL)),
        "w_ffn_in": nrm(ks[25], (DEPTH_2, D_MODEL, 2 * D_FF), D_MODEL ** -0.5),
        "w_ffn_out": nrm(ks[26], (DEPTH_2, D_FF, D_MODEL), D_FF ** -0.5),
        "norm_f_w": gain(ks[27], (D_MODEL,)),
    }

def second_block(x, norm_mix_w, w_in, hgrn_lower_bounds, hgrn_norm_w, ssd_conv_w, ssd_conv_b, ssd_dt_bias,
              ssd_a_log, ssd_d, ssd_norm_w, gla_gate_w, gla_gate_b, gla_norm_w, lru_conv_w, lru_conv_b,
              lru_wa, lru_ba, lru_wx, lru_bx, lru_lambda, w_branch, w_out, norm_ffn_w, w_ffn_in,
              w_ffn_out, norm_f_w):
    bsz, seqlen, _ = x.shape
    split_idx = np.cumsum(IN_SPLITS)[:-1].tolist()
    lb_all = jnp.cumsum(jax.nn.softmax(hgrn_lower_bounds.astype(F32), axis=0), axis=0)
    lb_all = lb_all - lb_all[0:1]
    h = x
    for l in range(DEPTH_2):
        xn = rmsnorm(h, norm_mix_w[l])
        proj = xn @ w_in[l]
        (hq, hf, hi, hg, sz, sxbc, sdt, gq, gk, gv, gg, glr, lx, lg, mg) = jnp.split(proj, split_idx, axis=-1)
        ya = hgrn2_branch(hq, hf, hi, hg, lb_all[l], hgrn_norm_w[l])
        yb = ssd_branch(sz, sxbc, sdt, ssd_conv_w[l], ssd_conv_b[l], ssd_dt_bias[l], ssd_a_log[l],
                        ssd_d[l], ssd_norm_w[l])
        yc = gla_branch(gq, gk, gv, gg, glr, gla_gate_w[l], gla_gate_b[l], gla_norm_w[l])
        yd = rglru_branch(lx, lg, lru_conv_w[l], lru_conv_b[l], lru_wa[l], lru_ba[l], lru_wx[l], lru_bx[l],
                          lru_lambda[l])
        ys = jnp.stack([ya, yb, yc, yd], axis=2).astype(h.dtype)
        branch_out = jnp.einsum('blnw,nwd->blnd', ys, w_branch[l])
        gates = jax.nn.sigmoid(mg.astype(F32)).reshape(bsz, seqlen, N_BRANCHES, D_MODEL)
        merged = jnp.sum(gates * branch_out.astype(F32), axis=2).astype(h.dtype)
        h = h + (merged @ w_out[l]).astype(h.dtype)
        xn = rmsnorm(h, norm_ffn_w[l])
        gate_up = xn @ w_ffn_in[l]
        g_ff, u_ff = jnp.split(gate_up, [D_FF], axis=-1)
        h = h + ((jax.nn.silu(g_ff) * u_ff) @ w_ffn_out[l]).astype(h.dtype)
    return rmsnorm(h, norm_f_w)


_first_inputs = second_inputs


def second_inputs(seed=0):
    import zlib

    import numpy as np

    out = dict(_first_inputs(seed))
    spreads = {}
    factors = {}
    for name, (base, spread) in spreads.items():
        noise = np.random.default_rng([zlib.crc32(name.encode()), seed]).standard_normal(out[name].shape)
        drawn = base * np.exp(spread * noise) if base else spread * noise
        out[name] = __import__('jax').numpy.asarray(drawn.astype(out[name].dtype))
    for name, factor in factors.items():
        out[name] = (out[name] * factor).astype(out[name].dtype)
    return out


_narrow_inputs = second_inputs


def second_inputs(seed=0):

    out = dict(_narrow_inputs(seed))
    wider = {'hgrn_norm_w': 11.03,
     'ssd_conv_b': 10.14,
     'ssd_d': 12.0,
     'ssd_norm_w': 6.61,
     'gla_gate_b': 12.0,
     'gla_norm_w': 11.38,
     'lru_conv_b': 3.99,
     'lru_ba': 12.0,
     'lru_bx': 12.0,
     'norm_ffn_w': 5.16,
     'norm_f_w': 3.51}
    for name, times in wider.items():
        mean = out[name].mean()
        out[name] = (mean + times * (out[name] - mean)).astype(out[name].dtype)
    return out


def setup_inputs(seed=0):
    out = dict(first_inputs(seed))
    for name, value in second_inputs(seed + 1).items():
        if name != "x":
            out[name + "_2"] = value
    return out


def reference(
    x, c, ctx, c_ctx, ada_w, ada_b, norm_w, attn_w_in, attn_q_norm, attn_k_norm, mla_q_norm,
    mla_kv_norm, mla_w_uq, mla_w_ukv, attn_w_out, hy_w_in, hy_conv_w, hy_conv_b, hy_ffn_w1,
    hy_ffn_b1, hy_ffn_w2, hy_ffn_b2, hy_ffn_w3, hy_ffn_b3, hy_freq, hy_skip, hy_w_out,
    final_norm_w, norm_mix_w_2, w_in_2, hgrn_lower_bounds_2, hgrn_norm_w_2, ssd_conv_w_2,
    ssd_conv_b_2, ssd_dt_bias_2, ssd_a_log_2, ssd_d_2, ssd_norm_w_2, gla_gate_w_2, gla_gate_b_2,
    gla_norm_w_2, lru_conv_w_2, lru_conv_b_2, lru_wa_2, lru_ba_2, lru_wx_2, lru_bx_2,
    lru_lambda_2, w_branch_2, w_out_2, norm_ffn_w_2, w_ffn_in_2, w_ffn_out_2, norm_f_w_2,
):
    x = first_block(
        x, c, ctx, c_ctx, ada_w, ada_b, norm_w, attn_w_in, attn_q_norm, attn_k_norm, mla_q_norm,
        mla_kv_norm, mla_w_uq, mla_w_ukv, attn_w_out, hy_w_in, hy_conv_w, hy_conv_b, hy_ffn_w1,
        hy_ffn_b1, hy_ffn_w2, hy_ffn_b2, hy_ffn_w3, hy_ffn_b3, hy_freq, hy_skip, hy_w_out,
        final_norm_w,
    )
    return second_block(
        x, norm_mix_w_2, w_in_2, hgrn_lower_bounds_2, hgrn_norm_w_2, ssd_conv_w_2, ssd_conv_b_2,
        ssd_dt_bias_2, ssd_a_log_2, ssd_d_2, ssd_norm_w_2, gla_gate_w_2, gla_gate_b_2,
        gla_norm_w_2, lru_conv_w_2, lru_conv_b_2, lru_wa_2, lru_ba_2, lru_wx_2, lru_bx_2,
        lru_lambda_2, w_branch_2, w_out_2, norm_ffn_w_2, w_ffn_in_2, w_ffn_out_2, norm_f_w_2,
    )


_drawn_inputs = setup_inputs


def setup_inputs(seed=0):
    import zlib

    import numpy as np

    out = dict(_drawn_inputs(seed))
    spreads = {}
    factors = {'ctx': 2.894,
     'norm_w': 3.517,
     'attn_q_norm': 8.0,
     'attn_k_norm': 8.0,
     'mla_q_norm': 8.0,
     'mla_kv_norm': 4.165,
     'hy_conv_b': 8.0,
     'hy_freq': 8.0,
     'gla_gate_b_2': 3.535,
     'lru_ba_2': 8.0,
     'lru_bx_2': 4.441}
    for name, (base, spread) in spreads.items():
        noise = np.random.default_rng([zlib.crc32(name.encode()), seed]).standard_normal(out[name].shape)
        drawn = base * np.exp(spread * noise) if base else spread * noise
        out[name] = __import__('jax').numpy.asarray(drawn.astype(out[name].dtype))
    for name, factor in factors.items():
        out[name] = (out[name] * factor).astype(out[name].dtype)
    return out
```

```python
from contextlib import ExitStack
import math

import numpy as np
import concourse.bass as bass
from concourse import mybir
from concourse.alu_op_type import AluOpType as ALU

ACT = mybir.ActivationFunctionType
F32 = mybir.dt.float32
AX_X = mybir.AxisListType.X

P = 128
D = 1024
DT = D // P
L = 1024
LT = L // P
C = 256
N = L + C
NT = N // P
BANK = 512
EPS = 1e-6
QH = 8
HD = 64
ROPE = 32
GRID = 64
HALF = 512


class Phase:

    def __init__(self, nc, tag):
        self.nc, self.tag, self.ctx, self.sems = nc, tag, ExitStack(), []

    def __enter__(self):
        return self

    def __exit__(self, *e):
        self.ctx.close()
        if e[0] is None:
            self.nc.clear_and_free_semaphores(self.sems)
            self.nc.all_engine_barrier(sem_only=True)

    def sb(self, name, shape):
        return self.ctx.enter_context(self.nc.sbuf_tensor(f"{self.tag}_{name}", shape, F32))

    def psum(self, name, shape):
        return self.ctx.enter_context(self.nc.psum_tensor(f"{self.tag}_{name}", shape, F32))

    def sem(self, name):
        s = self.nc.alloc_semaphore(f"{self.tag}_{name}")
        self.sems.append(s)
        return s

    def block(self):
        return self.nc.Block(no_gpsimd_drain=True)


def segments(cols):
    return [(a, min(a + BANK, cols)) for a in range(0, cols, BANK)]


def banked(cols):
    return -(-cols // BANK) * BANK


def chained(eng, ins, sem, count):
    count[0] += 1
    ins.then_inc(sem, 1)
    eng.wait_ge(sem, count[0])


def load_weight_tiles(sp, w, wbuf, tiles, loaded, multiplied):
    with sp.Fori(0, tiles // 2) as pair:
        for b in range(2):
            sp.wait_ge(multiplied, pair * 2 + (b + 1))
            sp.dma_start(wbuf[:, b], w[pair * 2 + b]).then_inc(loaded[b], 16)


def multiply_weight_tiles(pe, wbuf, ps, rhs, cols, tiles, loaded, multiplied, emptied):
    kt = wbuf.shape[2]
    pe.sem_inc(multiplied, 2)
    pe.sem_inc(emptied, 2)
    with pe.Fori(0, tiles // 2) as pair:
        for b in range(2):
            pe.wait_ge(loaded[b], pair * 16 + 16)
            pe.wait_ge(emptied, pair * 2 + (b + 1))
            for k in range(kt):
                for lo, hi in segments(cols):
                    mm = pe.matmul(ps[:, b, lo:hi], wbuf[:, b, k], rhs[:, k, lo:hi],
                                   start=(k == 0), stop=(k == kt - 1))
            mm.then_inc(multiplied, 1)


def load(nc, tag, pairs):
    with Phase(nc, tag) as ph:
        landed = ph.sem("landed")
        with ph.block() as block:
            @block.sync
            def _(sp):
                for dst, src in pairs:
                    sp.dma_start(dst, src).then_inc(landed, 16)
                sp.wait_ge(landed, 16 * len(pairs))


def store(nc, tag, dst, src):
    with Phase(nc, tag) as ph:
        stored = ph.sem("stored")
        with ph.block() as block:
            @block.sync
            def _(sp):
                sp.dma_start(dst, src[:]).then_inc(stored, 16)
                sp.wait_ge(stored, 16)


def project(nc, tag, w, rhs, out, tiles, cols, func=ACT.Copy):
    with Phase(nc, tag) as ph:
        kt = w.shape[2]
        wbuf = ph.sb("wbuf", [P, 2, kt, P])
        ps = ph.psum("ps", [P, 2, banked(cols)])
        loaded = [ph.sem(f"loaded{b}") for b in range(2)]
        multiplied, emptied = ph.sem("multiplied"), ph.sem("emptied")
        with ph.block() as block:
            @block.sync
            def _(sp):
                load_weight_tiles(sp, w, wbuf, tiles, loaded, multiplied)

            @block.tensor
            def _(pe):
                multiply_weight_tiles(pe, wbuf, ps, rhs, cols, tiles, loaded, multiplied, emptied)

            @block.scalar
            def _(act):
                with act.Fori(0, tiles // 2) as pair:
                    for b in range(2):
                        act.wait_ge(multiplied, pair * 2 + (b + 3))
                        act.activation(out[:, pair * 2 + b, 0:cols], ps[:, b, 0:cols], func).then_inc(emptied, 1)


def rms_norm(nc, tag, x, out, groups, per, width, summing, weight, shift, cols):
    with Phase(nc, tag) as ph:
        squares = ph.sb("squares", [P, 2, cols])
        mean = ph.sb("mean", [P, cols])
        root = ph.sb("root", [P, cols])
        inverse = ph.sb("inverse", [P, cols])
        ps = ph.psum("ps", [P, 2, banked(cols)])
        squared, summed, mean_ready, rooted = (ph.sem(s) for s in ("squared", "summed", "mean_ready", "rooted"))
        inverse_ready, scaled = ph.sem("inverse_ready"), ph.sem("scaled")
        with ph.block() as block:
            @block.scalar
            def _(act):
                for g in range(groups):
                    for n in range(g * per, (g + 1) * per):
                        if n >= 2:
                            act.wait_ge(summed, n - 1)
                        act.activation(squares[:, n % 2], x[:, n], ACT.Square).then_inc(squared, 1)
                    act.wait_ge(mean_ready, g + 1)
                    act.activation(root[:], mean[:], ACT.Sqrt).then_inc(rooted, 1)
                    if shift is not None:
                        for n in range(g * per, (g + 1) * per):
                            act.wait_ge(scaled, n + 1)
                            act.activation(out[:, n], out[:, n], ACT.Identity, bias=shift[:, n:n + 1])

            @block.tensor
            def _(pe):
                for g in range(groups):
                    if g >= 2:
                        pe.wait_ge(mean_ready, g - 1)
                    for t in range(per):
                        pe.wait_ge(squared, g * per + t + 1)
                        for lo, hi in segments(cols):
                            mm = pe.matmul(ps[:, g % 2, lo:hi], summing, squares[:, (g * per + t) % 2, lo:hi],
                                           start=(t == 0), stop=(t == per - 1))
                        mm.then_inc(summed, 1)

            @block.vector
            def _(dve):
                for g in range(groups):
                    dve.wait_ge(summed, (g + 1) * per)
                    dve.tensor_scalar(mean[:], ps[:, g % 2, 0:cols], 1.0 / width, EPS, ALU.mult,
                                      ALU.add).then_inc(mean_ready, 1)
                    dve.wait_ge(rooted, g + 1)
                    dve.reciprocal(inverse[:], root[:]).then_inc(inverse_ready, 1)
                    dve.wait_ge(inverse_ready, g + 1)
                    for n in range(g * per, (g + 1) * per):
                        if weight is None:
                            ins = dve.tensor_tensor(out[:, n], x[:, n], inverse[:], ALU.mult)
                        else:
                            ins = dve.scalar_tensor_tensor(out[:, n], x[:, n], weight[:, n:n + 1], inverse[:],
                                                           ALU.mult, ALU.mult)
                        ins.then_inc(scaled, 1)


def modulation(nc, A, mod, one_plus):
    tiles = 2 * 3 * DT
    with ExitStack() as ctx:
        cs = ctx.enter_context(nc.sbuf_tensor("ada_c", [P, DT, 2], F32))
        bias = ctx.enter_context(nc.sbuf_tensor("ada_bias", [P, tiles], F32))
        normw = ctx.enter_context(nc.sbuf_tensor("ada_normw", [P, 2, DT], F32))
        load(nc, "ada_load", [(cs[:], A["c2"]), (bias[:], A["ada_b"]), (normw[:], A["norm_w"])])
        with Phase(nc, "ada_silu") as ph:
            done = ph.sem("silu_done")
            with ph.block() as block:
                @block.scalar
                def _(act):
                    act.activation(cs[:], cs[:], ACT.Silu).then_inc(done, 1)
        project(nc, "ada", A["ada_w"], cs, mod, tiles, 2)
        with Phase(nc, "ada_bias") as ph:
            done = ph.sem("bias_added")
            with ph.block() as block:
                @block.vector
                def _(dve):
                    for s in range(2):
                        dve.tensor_tensor(mod[:, :, s], mod[:, :, s], bias[:], ALU.add).then_inc(done, 1)
                    dve.wait_ge(done, 2)
                    for layer in range(2):
                        for s in range(2):
                            first = (3 * layer + 1) * DT
                            dve.scalar_tensor_tensor(one_plus[:, layer, s], mod[:, first:first + DT, s], 1.0,
                                                     normw[:, layer], ALU.add, ALU.mult)


def rotate(nc, tag, x, tiles, swap, cos, sin, cols):
    with Phase(nc, tag) as ph:
        ps = ph.psum("ps", [P, 2, banked(cols)])
        turned = ph.sb("turned", [P, cols])
        swapped, straight, crossed, added = (ph.sem(s) for s in ("swapped", "straight", "crossed", "added"))
        with ph.block() as block:
            @block.tensor
            def _(pe):
                for t in range(tiles):
                    if t >= 2:
                        pe.wait_ge(crossed, t - 1)
                    for lo, hi in segments(cols):
                        mm = pe.matmul(ps[:, t % 2, lo:hi], swap, x[:, t, lo:hi], start=True, stop=True)
                    mm.then_inc(swapped, 1)

            @block.vector
            def _(dve):
                for t in range(tiles):
                    dve.wait_ge(swapped, t + 1)
                    dve.tensor_tensor(turned[:], ps[:, t % 2, 0:cols], sin[:, 0:cols], ALU.mult).then_inc(crossed, 1)
                    dve.tensor_tensor(x[:, t], x[:, t], cos[:, 0:cols], ALU.mult).then_inc(straight, 1)
                    dve.wait_ge(crossed, t + 1)
                    dve.wait_ge(straight, t + 1)
                    dve.tensor_tensor(x[:, t], x[:, t], turned[:], ALU.add).then_inc(added, 1)
                    dve.wait_ge(added, t + 1)


def mla_keys_values(nc, A, ckv, kpe, k_m, v_m, v_ch, v_a, ident):
    with Phase(nc, "mla_kv") as ph:
        wk = ph.sb("wk", [P, QH, P])
        wv = ph.sb("wv", [P, QH * HD])
        ps = ph.psum("ps", [P, 2, banked(N)])
        landed, keys, keys_read, values, values_read = (
            ph.sem(s) for s in ("landed", "keys", "keys_read", "values", "values_read"))
        with ph.block() as block:
            @block.sync
            def _(sp):
                sp.dma_start(wk[:], A["mla_wk"]).then_inc(landed, 16)
                sp.dma_start(wv[:], A["mla_wv"]).then_inc(landed, 16)

            @block.tensor
            def _(pe):
                pe.wait_ge(landed, 32)
                for h in range(QH):
                    if h >= 2:
                        pe.wait_ge(keys_read, h - 1)
                    for lo, hi in segments(N):
                        mm = pe.matmul(ps[:, h % 2, lo:hi], wk[:, h], ckv[:, 0, lo:hi], start=True, stop=True)
                    mm.then_inc(keys, 1)
                for t in range(NT):
                    if t < 2:
                        pe.wait_ge(keys_read, QH - 1 + t)
                    else:
                        pe.wait_ge(values_read, 2 * (t - 1))
                    pe.matmul(ps[:, t % 2, 0:QH * HD], ckv[:, 0, t * P:(t + 1) * P], wv[:], start=True, stop=True)
                    pe.transpose(ps[:, t % 2, BANK:BANK + P], v_ch[:, t * P:(t + 1) * P],
                                 ident).then_inc(values, 1)

            @block.vector
            def _(dve):
                for h in range(QH):
                    dve.wait_ge(keys, h + 1)
                    dve.tensor_tensor(k_m[:, h], ps[:, h % 2, 0:N], kpe, ALU.add).then_inc(keys_read, 1)
                for t in range(NT):
                    dve.wait_ge(values, t + 1)
                    dve.tensor_copy(v_m[:, t], ps[:, t % 2, 0:QH * HD]).then_inc(values_read, 1)
                    dve.tensor_copy(v_a[:, t], ps[:, t % 2, BANK:BANK + P]).then_inc(values_read, 1)


def attention(nc, q_a, k_a, v_a, q_m, k_m, v_m, ident):
    heads = [("a", i, r) for r in range(2) for i in range(4)] + [("m", h, 0) for h in range(QH)]
    H = len(heads)
    groups = [(0, 4), (4, 8), (8, NT)]
    G = len(groups)
    with Phase(nc, "attn") as ph:
        qa = ph.sb("qa", [P, 4, P])
        qm = ph.sb("qm", [P, QH, P])
        probs = ph.sb("probs", [P, 2, N])
        turned = ph.sb("turned", [P, 2, NT, P])
        top = ph.sb("top", [P, 2])
        minus_top = ph.sb("minus_top", [P, 2])
        total = ph.sb("total", [P, 2])
        share = ph.sb("share", [P, 2])
        scores = ph.psum("scores", [P, 2, banked(N)])
        tp = ph.psum("tp", [P, BANK])
        op = ph.psum("op", [P, BANK])
        queries, scored, topped, negated, exped, turned_up, copied_a, copied_v, weighed, shared, stored = (
            ph.sem(s) for s in ("queries", "scored", "topped", "negated", "exped", "turned_up", "copied_a",
                                "copied_v", "weighed", "shared", "stored"))

        with ph.block() as block:
            @block.gpsimd
            def _(pool):
                with pool.Fori(0, LT) as t:
                    pool.tensor_copy(qa[:], q_a[:, :, bass.ts(t, P)]).then_inc(queries, 1)
                    pool.tensor_copy(qm[:], q_m[:, :, bass.ts(t, P)]).then_inc(queries, 1)
                    pool.wait_ge(scored, t * H + H)

            @block.tensor
            def _(pe):
                pe.sem_inc(turned_up, 2 * G)
                pe.sem_inc(weighed, 2)

                def score(t, n, part):
                    kind, i, r = heads[n]
                    if part == 0:
                        pe.wait_ge(exped, t * H + (n + 1))
                    if kind == "a":
                        rows, q, k = slice(64 * r, 64 * r + 64), qa[:, i], k_a
                    else:
                        rows, q, k = slice(0, HD + ROPE), qm[:, i], k_m[:, i]
                    lo, hi = segments(N)[part]
                    mm = pe.matmul(scores[:, n % 2, lo:hi], q[rows], k[rows, lo:hi], start=True, stop=True)
                    if part == G - 1:
                        mm.then_inc(scored, 1)

                def turn(t, n, g):
                    if g == 0:
                        pe.wait_ge(exped, t * H + (n + 3))
                        pe.wait_ge(copied_v, t * 2 * H + (2 * n + 2))
                    elif g == 1:
                        pe.wait_ge(copied_a, t * H + (n + 2))
                    else:
                        pe.wait_ge(copied_v, t * 2 * H + (2 * n + 3))
                    a, b = groups[g]
                    for k in range(a, b):
                        tr = pe.transpose(tp[:, (k - a) * P:(k - a + 1) * P], probs[:, n % 2, k * P:(k + 1) * P], ident)
                    tr.then_inc(turned_up, 1)

                def weigh(t, n):
                    kind, i, r = heads[n]
                    v, col = (v_a, 64 * r) if kind == "a" else (v_m, 64 * i)
                    pe.wait_ge(stored, t * H + (n + 1))
                    pe.wait_ge(copied_a, t * H + (n + 2))
                    for k in range(NT):
                        if k == groups[1][0]:
                            pe.wait_ge(copied_v, t * 2 * H + (2 * n + 3))
                        if k == groups[2][0]:
                            pe.wait_ge(copied_v, t * 2 * H + (2 * n + 4))
                        mm = pe.matmul(op[:, 0:HD], turned[:, n % 2, k], v[:, k, col:col + HD],
                                       start=(k == 0), stop=(k == NT - 1))
                    mm.then_inc(weighed, 1)

                with pe.Fori(0, LT) as t:
                    pe.wait_ge(queries, t * 2 + 2)
                    for n in range(2):
                        for g in range(G):
                            score(t, n, g)
                    for n in range(H):
                        for g in range(G):
                            if n + 2 < H:
                                score(t, n + 2, g)
                            turn(t, n, g)
                        weigh(t, n)

            @block.vector
            def _(dve):
                dve.sem_inc(copied_v, 2)
                dve.sem_inc(stored, 1)
                dve.sem_inc(shared, 2)

                def maximum(t, n):
                    scale = (HD if heads[n][0] == "a" else HD + ROPE) ** -0.5
                    dve.wait_ge(scored, t * H + (n + 1))
                    dve.wait_ge(exped, t * H + (n + 1))
                    dve.reduce_max(top[:, n % 2:n % 2 + 1], scores[:, n % 2, 0:N],
                                   AX_X).then_inc(topped, 1)
                    dve.wait_ge(topped, t * H + (n + 1))
                    dve.tensor_scalar(minus_top[:, n % 2:n % 2 + 1], top[:, n % 2:n % 2 + 1], -scale, None,
                                      ALU.mult).then_inc(negated, 1)

                with dve.Fori(0, LT) as t:
                    maximum(t, 0)
                    for n in range(H):
                        if n + 1 < H:
                            maximum(t, n + 1)
                        dve.wait_ge(exped, t * H + (n + 3))
                        dve.reciprocal(share[:, n % 2:n % 2 + 1], total[:, n % 2:n % 2 + 1]).then_inc(shared, 1)
                        for g in (1, 2):
                            a, b = groups[g]
                            dve.wait_ge(turned_up, t * H * G + (n * G + g + 1 + 2 * G))
                            dve.tensor_copy(turned[:, n % 2, a:b], tp[:, 0:(b - a) * P]
                                            .rearrange("p (k c) -> p k c", c=P)).then_inc(copied_v, 1)
                        dve.wait_ge(weighed, t * H + (n + 3))
                        dve.wait_ge(shared, t * H + (n + 3))
                        dve.tensor_scalar(q_m[:, n // 2, bass.ds(t * P + n % 2 * HD, HD)], op[:, 0:HD], share[:, n % 2:n % 2 + 1], None,
                                          ALU.mult).then_inc(stored, 1)

            @block.scalar
            def _(act):
                act.sem_inc(exped, 2)
                act.sem_inc(copied_a, 1)

                def soften(t, n):
                    scale = (HD if heads[n][0] == "a" else HD + ROPE) ** -0.5
                    act.wait_ge(negated, t * H + (n + 1))
                    act.wait_ge(turned_up, t * H * G + (n + 1) * G)
                    act.wait_ge(shared, t * H + (n + 1))
                    act.activation(probs[:, n % 2], scores[:, n % 2, 0:N], ACT.Exp,
                                   bias=minus_top[:, n % 2:n % 2 + 1], scale=scale,
                                   accum_out=total[:, n % 2:n % 2 + 1]).then_inc(exped, 1)

                with act.Fori(0, LT) as t:
                    soften(t, 0)
                    for n in range(H):
                        act.wait_ge(turned_up, t * H * G + (n * G + 1 + 2 * G))
                        act.wait_ge(weighed, t * H + (n + 1))
                        a, b = groups[0]
                        act.activation(turned[:, n % 2, a:b], tp[:, 0:(b - a) * P]
                                       .rearrange("p (k c) -> p k c", c=P), ACT.Copy).then_inc(copied_a, 1)
                        if n + 1 < H:
                            soften(t, n + 1)


def turn_and_gate(nc, tag, o, gate, out, ident):
    with Phase(nc, tag) as ph:
        ps = ph.psum("ps", [P, 2, L])
        turned, gated, used = (ph.sem(s) for s in ("turned", "gated", "used"))
        with ph.block() as block:
            @block.scalar
            def _(act):
                for c in range(DT):
                    act.activation(gate[:, c], gate[:, c], ACT.Silu).then_inc(gated, 1)

            @block.tensor
            def _(pe):
                for c in range(DT):
                    if c >= 2:
                        pe.wait_ge(used, c - 1)
                    for t in range(LT):
                        tr = pe.transpose(ps[:, c % 2, t * P:(t + 1) * P], o[:, c, t * P:(t + 1) * P], ident)
                    tr.then_inc(turned, 1)

            @block.vector
            def _(dve):
                for c in range(DT):
                    dve.wait_ge(turned, c + 1)
                    dve.wait_ge(gated, c + 1)
                    dve.tensor_tensor(out[:, c], ps[:, c % 2], gate[:, c], ALU.mult).then_inc(used, 1)


def project_residual(nc, tag, w, rhs, gate, x):
    with Phase(nc, tag) as ph:
        kt = w.shape[2]
        wbuf = ph.sb("wbuf", [P, 2, kt, P])
        ps = ph.psum("ps", [P, 2, L])
        loaded = [ph.sem(f"loaded{b}") for b in range(2)]
        multiplied, emptied = ph.sem("multiplied"), ph.sem("emptied")
        with ph.block() as block:
            @block.sync
            def _(sp):
                load_weight_tiles(sp, w, wbuf, DT, loaded, multiplied)

            @block.tensor
            def _(pe):
                multiply_weight_tiles(pe, wbuf, ps, rhs, L, DT, loaded, multiplied, emptied)

            @block.vector
            def _(dve):
                for m in range(DT):
                    dve.wait_ge(multiplied, m + 3)
                    if gate is None:
                        ins = dve.tensor_tensor(x[:, m], ps[:, m % 2], x[:, m], ALU.add)
                    else:
                        ins = dve.scalar_tensor_tensor(x[:, m], ps[:, m % 2], gate[:, m:m + 1], x[:, m],
                                                       ALU.mult, ALU.add)
                    ins.then_inc(emptied, 1)


def attention_layer(nc, A, x_out, mod, one_plus, K):
    ones, halves, ident, swap_a, swap_m = (K[:, i] for i in range(5))
    with ExitStack() as ctx:
        def sb(name, shape):
            return ctx.enter_context(nc.sbuf_tensor(name, shape, F32))
        lat = sb("a_lat", [P, 14, L])
        both = sb("a_both", [P, 4, N])
        with ExitStack() as inner:
            x = inner.enter_context(nc.sbuf_tensor("a_x", [P, DT, L], F32))
            h = inner.enter_context(nc.sbuf_tensor("a_h", [P, DT, N], F32))
            load(nc, "a_ctx", [(x[:], A["x"]), (h[:, :, L:N], A["ctx"])])
            rms_norm(nc, "an0", x, h[:, :, 0:L], 1, DT, D, ones, one_plus[:, 0, 0], mod[:, 0:DT, 0], L)
            rms_norm(nc, "an1", h[:, :, L:N], h[:, :, L:N], 1, DT, D, ones, one_plus[:, 0, 1], mod[:, 0:DT, 1], C)
            project(nc, "ap0", A["attn_w_lat"], h, lat, 14, L)
            project(nc, "ap1", A["attn_w_both"], h, both, 4, N)
        ctx2 = ctx.enter_context(ExitStack())
        q_m = ctx2.enter_context(nc.sbuf_tensor("a_qm", [P, QH, L], F32))
        with ExitStack() as inner:
            small = inner.enter_context(nc.sbuf_tensor("a_small", [P, 8], F32))
            cos = inner.enter_context(nc.sbuf_tensor("a_cos", [P, N], F32))
            sin = inner.enter_context(nc.sbuf_tensor("a_sin", [P, N], F32))
            load(nc, "a_load", [(small[:], A["attn_small"]), (cos[:], A["rope"][0]), (sin[:], A["rope"][1])])
            rms_norm(nc, "an2", lat[:, 0:4], lat[:, 0:4], 4, 1, HD, halves, small[:, 0:4], None, L)
            rms_norm(nc, "an3", both[:, 0:1], both[:, 0:1], 1, 1, HD, halves, small[:, 4:5], None, N)
            rms_norm(nc, "an4", lat[:, 4:6], lat[:, 4:6], 1, 2, 256, ones, small[:, 5:7], None, L)
            rms_norm(nc, "an5", both[:, 1:2], both[:, 1:2], 1, 1, 128, ones, small[:, 7:8], None, N)
            rotate(nc, "ar0", lat[:, 0:4], 4, swap_a, cos, sin, L)
            rotate(nc, "ar1", both[:, 0:1], 1, swap_a, cos, sin, N)
            project(nc, "ap2", A["mla_w_uq"], lat[:, 4:6], q_m, QH, L)
            load(nc, "a_load2", [(cos[:], A["rope"][2]), (sin[:], A["rope"][3])])
            rotate(nc, "ar2", q_m, QH, swap_m, cos, sin, L)
            rotate(nc, "ar3", both[:, 2:3], 1, swap_m, cos, sin, N)
        k_m = ctx2.enter_context(nc.sbuf_tensor("a_km", [P, QH, N], F32))
        v_m = ctx2.enter_context(nc.sbuf_tensor("a_vm", [P, NT, QH * HD], F32))
        v_a = ctx2.enter_context(nc.sbuf_tensor("a_va", [P, NT, P], F32))
        mla_keys_values(nc, A, both[:, 1:2], both[:, 2], k_m, v_m, both[:, 3], v_a, ident)
        attention(nc, lat[:, 0:4], both[:, 0], v_a, q_m, k_m, v_m, ident)
        turn_and_gate(nc, "a_gate", q_m, lat[:, 6:14], lat[:, 6:14], ident)
        ctx2.close()
        x = sb("a_x2", [P, DT, L])
        load(nc, "a_x2l", [(x[:], A["x"])])
        project_residual(nc, "a_out", A["attn_w_out"], lat[:, 6:14], mod[:, 2 * DT:3 * DT, 0], x)
        store(nc, "a_store", x_out, x)


FFN = 64
EMB = 33


def filter_network(nc, A, hid):
    ROUND = 1.5 * 2.0 ** 23
    HIGH = 6.28125
    LOW = 2 * math.pi - HIGH
    with Phase(nc, "filter_net") as ph:
        emb, w1, w2, small = ph.sb("emb", [EMB, L]), ph.sb("w1", [EMB, FFN]), ph.sb("w2", [FFN, FFN]), ph.sb("small", [FFN, 3])
        arg, turns, first = ph.sb("arg", [FFN, L]), ph.sb("turns", [FFN, L]), ph.sb("first", [FFN, L])
        ps = ph.psum("ps", [P, 2, L])
        landed, multiplied, step, reduced, sined = (
            ph.sem(s) for s in ("landed", "multiplied", "step", "reduced", "sined"))
        with ph.block() as block:
            @block.sync
            def _(sp):
                for dst, src in ((emb, A["hy_emb"]), (w1, A["hy_w1"]), (w2, A["hy_w2"]), (small, A["hy_small"])):
                    sp.dma_start(dst[:], src).then_inc(landed, 16)

            @block.tensor
            def _(pe):
                pe.wait_ge(landed, 64)
                for lo, hi in segments(L):
                    mm = pe.matmul(ps[0:FFN, 0, lo:hi], w1[:], emb[:, lo:hi], start=True, stop=True)
                mm.then_inc(multiplied, 1)
                pe.wait_ge(sined, 1)
                for lo, hi in segments(L):
                    mm = pe.matmul(ps[0:FFN, 1, lo:hi], w2[:], first[:, lo:hi], start=True, stop=True)
                mm.then_inc(multiplied, 1)

            @block.vector
            def _(dve):
                count = [0]
                dve.wait_ge(landed, 64)
                dve.memset(hid[FFN:FFN + 1, :], 1.0)
                for layer in range(2):
                    dve.wait_ge(multiplied, layer + 1)
                    if layer:
                        dve.wait_ge(sined, 1)
                    chained(dve, dve.tensor_scalar(arg[:], ps[0:FFN, layer], small[:, layer:layer + 1], small[:, 2:3],
                                                   ALU.add, ALU.mult), step, count)
                    chained(dve, dve.tensor_scalar(turns[:], arg[:], 1 / (2 * math.pi), ROUND, ALU.mult, ALU.add),
                            step, count)
                    chained(dve, dve.tensor_scalar(turns[:], turns[:], ROUND, None, ALU.subtract), step, count)
                    chained(dve, dve.scalar_tensor_tensor(arg[:], turns[:], -HIGH, arg[:], ALU.mult, ALU.add),
                            step, count)
                    chained(dve, dve.scalar_tensor_tensor(arg[:], turns[:], -LOW, arg[:], ALU.mult, ALU.add),
                            step, count)
                    dve.tensor_scalar(arg[:], arg[:], 3.1415925, -3.1415925, ALU.min, ALU.max).then_inc(reduced, 1)

            @block.scalar
            def _(act):
                act.wait_ge(reduced, 1)
                act.activation(first[:], arg[:], ACT.Sin).then_inc(sined, 1)
                act.wait_ge(reduced, 2)
                act.activation(hid[0:FFN, :], arg[:], ACT.Sin).then_inc(sined, 1)


def filter_taps(nc, A, hid, order, even, odd, inverse):
    with Phase(nc, f"taps{order}") as ph:
        w3 = ph.sb("w3", [FFN + 1, 2, D])
        decay = ph.sb("decay", [P, 2, D])
        fwd, bwd = ph.sb("fwd", [P, 2, D]), ph.sb("bwd", [P, 2, D])
        mag = ph.sb("mag", [P, 2, D])
        size = ph.sb("size", [P, D])
        magnitudes = ph.sem("magnitudes")
        ps = ph.psum("ps", [P, 2, 2, D])
        landed, made, decayed, sized, combined, total, scaled = (
            ph.sem(s) for s in ("landed", "made", "decayed", "sized", "combined", "total", "scaled"))
        table = [ph.sem(f"table{b}") for b in range(2)]
        with ph.block() as block:
            @block.sync
            def _(sp):
                sp.dma_start(w3[:], A["hy_w3"][order]).then_inc(landed, 16)
                for t in range(LT):
                    if t >= 2:
                        sp.wait_ge(decayed, 2 * (t - 1))
                    sp.dma_start(decay[:, t % 2], A["hy_decay"][t]).then_inc(table[t % 2], 16)

            @block.tensor
            def _(pe):
                pe.wait_ge(landed, 16)
                for t in range(LT):
                    if t >= 2:
                        pe.wait_ge(decayed, 2 * (t - 1))
                    for way in range(2):
                        for lo, hi in segments(D):
                            mm = pe.matmul(ps[:, t % 2, way, lo:hi], hid[:, t * P:(t + 1) * P], w3[:, way, lo:hi],
                                           start=True, stop=True)
                    mm.then_inc(made, 1)
                pe.wait_ge(decayed, 2 * LT)
                pe.wait_ge(sized, 2 * LT + 1)
                for lo, hi in segments(D):
                    mm = pe.matmul(ps[:, 0, 0, lo:hi], A["ones"], size[:, lo:hi], start=True, stop=True)
                mm.then_inc(total, 1)

            @block.vector
            def _(dve):
                dve.memset(size[:], 0.0).then_inc(sized, 1)
                for t in range(LT):
                    dve.wait_ge(made, t + 1)
                    dve.wait_ge(table[t % 2], 16 * (t // 2 + 1))
                    if t >= 2:
                        dve.wait_ge(magnitudes, 2 * (t - 1))
                        dve.wait_ge(combined, 2 * (t - 1))
                    dve.tensor_tensor(fwd[:, t % 2], ps[:, t % 2, 0], decay[:, t % 2], ALU.mult).then_inc(decayed, 1)
                    dve.tensor_tensor(bwd[:, t % 2], ps[:, t % 2, 1], decay[:, t % 2], ALU.mult).then_inc(decayed, 1)
                    dve.wait_ge(decayed, 2 * t + 2)
                    if t == 0:
                        dve.memset(bwd[0:1, 0], 0.0).then_inc(scaled, 1)
                        dve.wait_ge(scaled, 1)
                    for way in range(2):
                        dve.wait_ge(magnitudes, 2 * t + way + 1)
                        dve.wait_ge(sized, 2 * t + way + 1)
                        dve.tensor_tensor(size[:], size[:], mag[:, way], ALU.add).then_inc(sized, 1)
                dve.wait_ge(total, 1)
                dve.tensor_scalar(inverse[:], ps[:, 0, 0], float(L), None, ALU.mult).then_inc(scaled, 1)
                dve.wait_ge(scaled, 2)
                dve.reciprocal(inverse[:], inverse[:])

            @block.scalar
            def _(act):
                for t in range(LT):
                    act.wait_ge(decayed, 2 * t + 2)
                    act.wait_ge(scaled, 1)
                    for way, tap in enumerate((fwd, bwd)):
                        if t:
                            act.wait_ge(sized, 2 * t + way)
                        act.activation(mag[:, way], tap[:, t % 2], ACT.Abs).then_inc(magnitudes, 1)

            @block.gpsimd
            def _(pool):
                pool.wait_ge(scaled, 1)
                for t in range(LT):
                    pool.wait_ge(decayed, 2 * t + 2)
                    pool.tensor_tensor(even[:, t], fwd[:, t % 2], bwd[:, t % 2], ALU.add).then_inc(combined, 1)
                    pool.tensor_tensor(odd[:, t], fwd[:, t % 2], bwd[:, t % 2], ALU.subtract).then_inc(combined, 1)


def transform(pe, wbuf, ps, rhs_cos, rhs_sin, loaded, multiplied, emptied, apart):
    pe.sem_inc(multiplied, 2)
    pe.sem_inc(emptied, 2)
    with pe.Fori(0, DT // 2) as pair:
        for b in range(2):
            pe.wait_ge(loaded[b], pair * 16 + 16)
            pe.wait_ge(emptied, pair * 2 + (b + 1))
            for part, rhs in enumerate((rhs_cos, rhs_sin)):
                out = ps[:, b, part] if apart else ps[:, b]
                for k in range(LT):
                    for lo, hi in segments(D):
                        mm = pe.matmul(out[:, lo:hi], wbuf[:, b, part * LT + k], rhs[:, k, lo:hi],
                                       start=(k == 0 and (apart or part == 0)),
                                       stop=(k == LT - 1 and (apart or part == 1)))
            mm.then_inc(multiplied, 1)


def filter_spectrum(nc, A, order, even, odd, inverse):
    with Phase(nc, f"spec{order}") as ph:
        wbuf = ph.sb("wbuf", [P, 2, 2 * LT, P])
        skip = ph.sb("skip", [P, D])
        out = ph.sb("out", [P, 2, 2, D])
        ps = ph.psum("ps", [P, 2, 2, D])
        loaded = [ph.sem(f"loaded{b}") for b in range(2)]
        stored = [ph.sem(f"stored{b}") for b in range(2)]
        multiplied, emptied, landed, finished, small = (ph.sem(s) for s in ("multiplied", "emptied", "landed", "finished", "small"))
        with ph.block() as block:
            @block.sync
            def _(sp):
                sp.dma_start(skip[:], A["hy_skip"][order]).then_inc(landed, 16)
                load_weight_tiles(sp, A["hy_lag_tables"], wbuf, DT, loaded, multiplied)

            @block.tensor
            def _(pe):
                transform(pe, wbuf, ps, even, odd, loaded, multiplied, emptied, True)

            @block.vector
            def _(dve):
                dve.wait_ge(landed, 16)
                dve.tensor_scalar(skip[:], skip[:], 1.0 / L, None, ALU.mult).then_inc(small, 1)
                for b in range(2):
                    dve.sem_inc(stored[b], 16)
                dve.wait_ge(small, 1)
                with dve.Fori(0, DT // 2) as pair:
                    for b in range(2):
                        dve.wait_ge(multiplied, pair * 2 + (b + 3))
                        dve.wait_ge(stored[b], pair * 16 + 16)
                        dve.tensor_tensor(out[:, b, 0], ps[:, b, 0], inverse[:], ALU.mult).then_inc(small, 1)
                        dve.tensor_tensor(out[:, b, 1], ps[:, b, 1], inverse[:], ALU.mult).then_inc(emptied, 1)
                        dve.wait_ge(small, pair * 2 + (b + 2))
                        dve.tensor_tensor(out[:, b, 0], out[:, b, 0], skip[:], ALU.add).then_inc(finished, 1)

            @block.scalar
            def _(act):
                with act.Fori(0, DT // 2) as pair:
                    for b in range(2):
                        act.wait_ge(finished, pair * 2 + (b + 1))
                        act.wait_ge(emptied, pair * 2 + (b + 3))
                        act.dma_start(A["spectrum"][order * DT + pair * 2 + b], out[:, b]).then_inc(stored[b], 16)
                for b in range(2):
                    act.wait_ge(stored[b], 16 * (DT // 2 + 1))


def hyena_filters(nc, A):
    with ExitStack() as ctx:
        hid = ctx.enter_context(nc.sbuf_tensor("hy_hid", [FFN + 1, L], F32))
        even = ctx.enter_context(nc.sbuf_tensor("hy_even", [P, LT, D], F32))
        odd = ctx.enter_context(nc.sbuf_tensor("hy_odd", [P, LT, D], F32))
        inverse = ctx.enter_context(nc.sbuf_tensor("hy_inverse", [P, D], F32))
        filter_network(nc, A, hid)
        for order in range(2):
            filter_taps(nc, A, hid, order, even, odd, inverse)
            filter_spectrum(nc, A, order, even, odd, inverse)


def project_conv(nc, tag, w, rhs, out, tiles, taps, first, before, after, func):
    width = before + 1 + after
    with Phase(nc, tag) as ph:
        kt = w.shape[2]
        wbuf = ph.sb("wbuf", [P, 2, kt, P])
        raw = ph.sb("raw", [P, 2, before + L + after])
        ps = ph.psum("ps", [P, 2, L])
        loaded = [ph.sem(f"loaded{b}") for b in range(2)]
        multiplied, emptied, padded, step, convolved = (
            ph.sem(s) for s in ("multiplied", "emptied", "padded", "step", "convolved"))
        with ph.block() as block:
            @block.sync
            def _(sp):
                load_weight_tiles(sp, w, wbuf, tiles, loaded, multiplied)

            @block.tensor
            def _(pe):
                multiply_weight_tiles(pe, wbuf, ps, rhs, L, tiles, loaded, multiplied, emptied)

            @block.scalar
            def _(act):
                act.wait_ge(padded, 1)
                for m in range(tiles):
                    act.wait_ge(multiplied, m + 3)
                    if m >= 2:
                        act.wait_ge(step, width * (m - 1))
                    act.activation(raw[:, m % 2, before:before + L], ps[:, m % 2], ACT.Copy).then_inc(emptied, 1)
                    if func is not None and m >= 1:
                        act.wait_ge(step, width * m)
                        act.activation(out[:, m - 1], out[:, m - 1], func)
                if func is not None:
                    act.wait_ge(step, width * tiles)
                    act.activation(out[:, tiles - 1], out[:, tiles - 1], func)

            @block.vector
            def _(dve):
                dve.memset(raw[:], 0.0).then_inc(padded, 1)
                for m in range(tiles):
                    t = taps[:, first + m]
                    dve.wait_ge(emptied, m + 3)
                    dve.tensor_scalar(out[:, m], raw[:, m % 2, 0:L], t[:, 0:1], t[:, width:width + 1],
                                      ALU.mult, ALU.add).then_inc(step, 1)
                    for j in range(1, width):
                        dve.wait_ge(step, width * m + j)
                        dve.scalar_tensor_tensor(out[:, m], raw[:, m % 2, j:j + L], t[:, j:j + 1], out[:, m],
                                                 ALU.mult, ALU.add).then_inc(step, 1)


def turn_tiles(nc, tag, src, dst, ident, factor=None):
    with Phase(nc, tag) as ph:
        ps = ph.psum("ps", [P, 2, L])
        turned, used = ph.sem("turned"), ph.sem("used")
        with ph.block() as block:
            @block.tensor
            def _(pe):
                for t in range(LT):
                    if t >= 2:
                        pe.wait_ge(used, t - 1)
                    for c in range(DT):
                        tr = pe.transpose(ps[:, t % 2, c * P:(c + 1) * P], src[:, c, t * P:(t + 1) * P], ident)
                    tr.then_inc(turned, 1)

            @block.vector
            def _(dve):
                for t in range(LT):
                    dve.wait_ge(turned, t + 1)
                    if factor is None:
                        dve.tensor_copy(dst[:, t], ps[:, t % 2]).then_inc(used, 1)
                    else:
                        dve.tensor_tensor(dst[:, t], ps[:, t % 2], factor[:, t], ALU.mult).then_inc(used, 1)


def long_conv(nc, A, order, z, spec, factor):
    with Phase(nc, f"fwd{order}") as ph:
        wbuf = ph.sb("wbuf", [P, 2, 2 * LT, P])
        filt = ph.sb("filt", [P, 2, 2, D])
        cross = ph.sb("cross", [P, D])
        ps = ph.psum("ps", [P, 2, 2, D])
        loaded = [ph.sem(f"loaded{b}") for b in range(2)]
        filt_in = [ph.sem(f"filt_in{b}") for b in range(2)]
        multiplied, emptied, step = (ph.sem(s) for s in ("multiplied", "emptied", "step"))
        with ph.block() as block:
            @block.sync
            def _(sp):
                load_weight_tiles(sp, A["hy_tables"], wbuf, DT, loaded, multiplied)

            @block.scalar
            def _(act):
                with act.Fori(0, DT // 2) as pair:
                    for b in range(2):
                        act.wait_ge(emptied, pair * 2 + (b + 1))
                        act.dma_start(filt[:, b], A["spectrum"][order * DT + pair * 2 + b]).then_inc(filt_in[b], 16)

            @block.tensor
            def _(pe):
                transform(pe, wbuf, ps, z, z, loaded, multiplied, emptied, True)

            @block.vector
            def _(dve):
                count = [0]
                for f in range(DT):
                    b = f % 2
                    dve.wait_ge(multiplied, f + 3)
                    dve.wait_ge(filt_in[b], 16 * (f // 2 + 1))
                    re, im, k_re, k_im = ps[:, b, 0], ps[:, b, 1], filt[:, b, 0], filt[:, b, 1]
                    chained(dve, dve.tensor_tensor(spec[:, 0, f], re, k_re, ALU.mult), step, count)
                    chained(dve, dve.tensor_tensor(cross[:], im, k_im, ALU.mult), step, count)
                    chained(dve, dve.tensor_tensor(spec[:, 0, f], spec[:, 0, f], cross[:], ALU.subtract), step, count)
                    chained(dve, dve.tensor_tensor(spec[:, 1, f], re, k_im, ALU.mult), step, count)
                    dve.tensor_tensor(cross[:], im, k_re, ALU.mult).then_inc(emptied, 1)
                    dve.wait_ge(emptied, f + 3)
                    chained(dve, dve.tensor_tensor(spec[:, 1, f], spec[:, 1, f], cross[:], ALU.add), step, count)
    with Phase(nc, f"inv{order}") as ph:
        wbuf = ph.sb("wbuf", [P, 2, 2 * LT, P])
        ps = ph.psum("ps", [P, 2, D])
        loaded = [ph.sem(f"loaded{b}") for b in range(2)]
        multiplied, emptied = (ph.sem(s) for s in ("multiplied", "emptied"))
        with ph.block() as block:
            @block.sync
            def _(sp):
                load_weight_tiles(sp, A["hy_tables"], wbuf, DT, loaded, multiplied)

            @block.tensor
            def _(pe):
                transform(pe, wbuf, ps, spec[:, 0], spec[:, 1], loaded, multiplied, emptied, False)

            @block.vector
            def _(dve):
                for t in range(LT):
                    dve.wait_ge(multiplied, t + 3)
                    if factor is None:
                        dve.tensor_copy(z[:, t], ps[:, t % 2]).then_inc(emptied, 1)
                    else:
                        dve.tensor_tensor(z[:, t], ps[:, t % 2], factor[:, t], ALU.mult).then_inc(emptied, 1)


def multiply(nc, tag, out, a, b, tiles):
    with Phase(nc, tag) as ph:
        with ph.block() as block:
            @block.vector
            def _(dve):
                for t in range(tiles):
                    dve.tensor_tensor(out[:, t], a[:, t], b[:, t], ALU.mult)


def hyena_layer(nc, A, x_in, x_out, mod, one_plus, K):
    ones, ident = K[:, 0], K[:, 2]
    A["ones"] = ones
    hyena_filters(nc, A)
    with ExitStack() as ctx:
        def sb(name, shape):
            return ctx.enter_context(nc.sbuf_tensor(name, shape, F32))
        last = sb("hy_last", [P, DT, L])
        final_w = sb("hy_final_w", [P, DT])
        with ExitStack() as mid:
            z = mid.enter_context(nc.sbuf_tensor("hy_z", [P, LT, D], F32))
            part1 = mid.enter_context(nc.sbuf_tensor("hy_part1", [P, LT, D], F32))
            with ExitStack() as inner:
                u = inner.enter_context(nc.sbuf_tensor("hy_u", [P, DT, L], F32))
                h = inner.enter_context(nc.sbuf_tensor("hy_h", [P, DT, L], F32))
                taps = inner.enter_context(nc.sbuf_tensor("hy_taps", [P, 24, 4], F32))
                load(nc, "hy_load", [(u[:], x_in), (taps[:], A["hy_taps"]), (final_w[:], A["final_norm_w"])])
                rms_norm(nc, "hy_n", u, h, 1, DT, D, ones, one_plus[:, 1, 0], mod[:, 3 * DT:4 * DT, 0], L)
                w = A["hy_w_in"]
                project_conv(nc, "hy_c0", w[0:8], h, u, DT, taps, 0, 1, 1, None)
                turn_tiles(nc, "hy_t0", u, z, ident)
                project_conv(nc, "hy_c1", w[8:16], h, u, DT, taps, 8, 1, 1, None)
                turn_tiles(nc, "hy_t1", u, part1, ident)
                project_conv(nc, "hy_c2", w[16:24], h, u, DT, taps, 16, 1, 1, None)
                project(nc, "hy_g", w[24:32], h, last, DT, L, ACT.Silu)
                multiply(nc, "hy_m", last, last, u, DT)
            spec = mid.enter_context(nc.sbuf_tensor("hy_spec", [P, 2, DT, D], F32))
            long_conv(nc, A, 0, z, spec, part1)
            long_conv(nc, A, 1, z, spec, None)
            turn_tiles(nc, "hy_t2", z, last, ident, last)
        x = sb("hy_x", [P, DT, L])
        load(nc, "hy_load2", [(x[:], x_in)])
        project_residual(nc, "hy_out", A["hy_w_out"], last, mod[:, 5 * DT:6 * DT, 0], x)
        rms_norm(nc, "hy_fn", x, x, 1, DT, D, ones, final_w, None, L)
        store(nc, "hy_store", x_out, x)


KEY = 128
LEVELS = 7
SH = 8


def spread(ap, shape):
    return ap.broadcast_to(shape)


def gated_tile(nc, tag, q, k, log_f, values, outs, scratch, masks, ident):
    H = len(values)
    rows = [slice(h * (P // H), (h + 1) * (P // H)) for h in range(H)]
    units = [(n, h) for n in range(LEVELS + 1) for h in range(H)]
    with Phase(nc, tag) as ph:
        cum = ph.sb("cum", [P, L])
        keep = ph.sb("keep", [P, LT, P])
        edge = ph.sb("edge", [P, 2, L])
        near_q, near_k = scratch[:, 0:2], scratch[:, 2:4]
        score = ph.sb("score", [P, H, L])
        masked_part = ph.sb("masked_part", [P, L])
        key_tok = ph.sb("key_tok", [P, LT, P])
        state = ph.sb("state", [P, LT, P])
        ps = ph.psum("ps", [P, 2, L])
        ps_a = ph.psum("ps_a", [P, L])
        ps_b = ph.psum("ps_b", [P, L])
        setup, summed, edges, exped, factored, products, masked, added, turned, copied, updates, states, out_ready, out_copied = (
            ph.sem(s) for s in ("setup", "summed", "edges", "exped", "factored", "products", "masked", "added", "turned",
                                "copied", "updates", "states", "out_ready", "out_copied"))

        def halves(ap, level):
            half = 2 ** level
            a = ap.rearrange("p (b s) -> p b s", s=2 * half)
            mid = a[:, :, half - 1:half]
            return a[:, :, 0:half], a[:, :, half:2 * half], spread(mid, [P, L // (2 * half), half])

        with ph.block() as block:
            @block.vector
            def _(dve):
                dve.memset(near_q, 0.0).then_inc(setup, 1)
                dve.memset(near_k, 0.0).then_inc(setup, 1)
                dve.memset(keep[:], 1.0).then_inc(setup, 1)
                dve.memset(state[:, 0], 0.0).then_inc(setup, 1)
                dve.wait_ge(setup, 4)
                dve.memset(keep[:, :, 0:1], 0.0).then_inc(setup, 1)
                dve.wait_ge(setup, 5)
                dve.tensor_tensor_scan(cum[:], keep[:].rearrange("p c t -> p (c t)"), log_f, 0.0, ALU.mult,
                                       ALU.add).then_inc(summed, 1)
                dve.wait_ge(summed, 1)

                def exponents(level):
                    b_left, b_right, mid = halves(cum[:], level)
                    left, right, _ = halves(edge[:, level % 2], level)
                    if level >= 2:
                        dve.wait_ge(factored, 2 * (level - 1))
                    dve.tensor_tensor(right, b_right, mid, ALU.subtract).then_inc(edges, 1)
                    dve.tensor_tensor(left, mid, b_left, ALU.subtract).then_inc(edges, 1)

                def factors(level):
                    left, right, _ = halves(edge[:, level % 2], level)
                    q_right, k_left = halves(q, level)[1], halves(k, level)[0]
                    if level >= 2:
                        dve.wait_ge(products, H * (level - 2 + 2))
                    dve.wait_ge(exped, level + 1)
                    dve.tensor_tensor(halves(near_q[:, level % 2], level)[1], q_right, right, ALU.mult).then_inc(factored, 1)
                    dve.tensor_tensor(halves(near_k[:, level % 2], level)[0], k_left, left, ALU.mult).then_inc(factored, 1)

                def accumulate(u):
                    n, h = units[u]
                    mask = spread(masks[:, n].unsqueeze(1), [P, LT, P])
                    part = ps[:, u % 2].rearrange("p (c t) -> p c t", t=P)
                    dve.wait_ge(products, u + 1)
                    if n == 0:
                        dve.tensor_tensor(score[:, h].rearrange("p (c t) -> p c t", t=P), part, mask,
                                          ALU.mult).then_inc(masked, 1)
                    else:
                        if u > H:
                            dve.wait_ge(added, u - H)
                        dve.tensor_tensor(masked_part[:].rearrange("p (c t) -> p c t", t=P), part, mask,
                                          ALU.mult).then_inc(masked, 1)
                        dve.wait_ge(masked, u + 1)
                        dve.tensor_tensor(score[:, h], score[:, h], masked_part[:], ALU.add).then_inc(added, 1)

                exponents(0)
                for level in range(LEVELS):
                    if level + 1 < LEVELS:
                        exponents(level + 1)
                    factors(level)
                    for h in range(H):
                        accumulate(level * H + h)
                chunks = cum[:].rearrange("p (c t) -> p c t", t=P)
                last = spread(chunks[:, :, P - 1:P], [P, LT, P])
                dve.wait_ge(factored, 2 * LEVELS)
                dve.wait_ge(products, H * (LEVELS - 1))
                dve.tensor_tensor(edge[:, 1].rearrange("p (c t) -> p c t", t=P), last, chunks, ALU.subtract).then_inc(edges, 1)
                dve.wait_ge(exped, LEVELS + 2)
                dve.tensor_tensor(near_k[:, 1], k, edge[:, 1], ALU.mult).then_inc(factored, 1)
                dve.tensor_tensor(near_q[:, 1], q, edge[:, 0], ALU.mult).then_inc(factored, 1)
                for h in range(H):
                    accumulate(LEVELS * H + h)
                dve.wait_ge(updates, 1)
                for c in range(LT - 1):
                    if c:
                        dve.wait_ge(states, c)
                    dve.scalar_tensor_tensor(state[:, c + 1], state[:, c], edge[:, 0, (c + 1) * P - 1:(c + 1) * P],
                                             ps_b[:, c * P:(c + 1) * P], ALU.mult, ALU.add).then_inc(states, 1)

            @block.scalar
            def _(act):
                for level in range(LEVELS):
                    act.wait_ge(edges, 2 * (level + 1))
                    act.activation(edge[:, level % 2], edge[:, level % 2], ACT.Exp).then_inc(exped, 1)
                act.wait_ge(factored, 2 * LEVELS)
                act.activation(edge[:, 0], cum[:], ACT.Exp).then_inc(exped, 1)
                act.wait_ge(edges, 2 * LEVELS + 1)
                act.activation(edge[:, 1], edge[:, 1], ACT.Exp).then_inc(exped, 1)
                act.wait_ge(turned, 1)
                act.activation(key_tok[:].rearrange("p c t -> p (c t)"), ps_a[:], ACT.Copy).then_inc(copied, 1)
                for h in range(H):
                    act.wait_ge(out_ready, h + 1)
                    act.activation(outs[h], (ps_a if h == 0 else ps_b)[:], ACT.Copy).then_inc(out_copied, 1)

            @block.tensor
            def _(pe):
                for u, (n, h) in enumerate(units):
                    if n == 0:
                        left, right = k, q
                        pe.wait_ge(setup, 1)
                    else:
                        left, right = near_k[:, (n - 1) % 2], near_q[:, (n - 1) % 2]
                        pe.wait_ge(factored, 2 * n)
                    if u >= 2:
                        pe.wait_ge(masked, u - 1)
                    for c in range(LT):
                        mm = pe.matmul(ps[:, u % 2, c * P:(c + 1) * P], left[rows[h], c * P:(c + 1) * P],
                                       right[rows[h], c * P:(c + 1) * P], start=True, stop=True)
                    mm.then_inc(products, 1)
                pe.wait_ge(factored, 2 * LEVELS + 2)
                for c in range(LT):
                    tr = pe.transpose(ps_a[:, c * P:(c + 1) * P], near_k[:, 1, c * P:(c + 1) * P], ident)
                tr.then_inc(turned, 1)
                pe.wait_ge(copied, 1)
                for h in range(H):
                    for c in range(LT):
                        mm = pe.matmul(ps_b[rows[h], c * P:(c + 1) * P], key_tok[:, c, rows[h]], values[h][:, c],
                                       start=True, stop=True)
                mm.then_inc(updates, 1)
                pe.wait_ge(states, LT - 1)
                pe.wait_ge(added, len(units) - H)
                for h in range(H):
                    out = (ps_a if h == 0 else ps_b)
                    for c in range(LT):
                        mm = pe.matmul(out[:, c * P:(c + 1) * P], values[h][:, c], score[:, h, c * P:(c + 1) * P],
                                       start=True, stop=(c == 0))
                        if c:
                            mm = pe.matmul(out[:, c * P:(c + 1) * P], state[rows[h], c],
                                           near_q[rows[h], 1, c * P:(c + 1) * P], start=False, stop=True)
                    mm.then_inc(out_ready, 1)


def soft(nc, tag, x, tmp, tiles, bias, scale, sign, rows=P):
    with Phase(nc, tag) as ph:
        biased, logged, done = (ph.sem(s) for s in ("biased", "logged", "done"))
        with ph.block() as block:
            @block.vector
            def _(dve):
                for t in range(tiles):
                    if bias is not None:
                        dve.tensor_scalar(x[:, t], x[:, t], bias[:, t:t + 1], None, ALU.add).then_inc(biased, 1)
                for t in range(tiles):
                    dve.wait_ge(logged, 3 * t + 3)
                    dve.scalar_tensor_tensor(x[:, t], x[:, t], 0.0, tmp[:, t], ALU.max if sign > 0 else ALU.min,
                                             ALU.add if sign > 0 else ALU.subtract).then_inc(done, 1)
                    if scale * sign != 1:
                        dve.wait_ge(done, t + 1)
                        dve.tensor_scalar(x[:, t], x[:, t], scale * sign, None, ALU.mult)

            @block.scalar
            def _(act):
                for t in range(tiles):
                    if bias is not None:
                        act.wait_ge(biased, t + 1)
                    for j, (src, func, s, b) in enumerate(((x, ACT.Abs, 1.0, 0.0), (tmp, ACT.Exp, -1.0, 0.0),
                                                           (tmp, ACT.Ln, 1.0, 1.0))):
                        act.activation(tmp[:, t], src[:, t], func, scale=s, bias=b).then_inc(logged, 1)
                        act.wait_ge(logged, 3 * t + j + 1)


def activate(nc, tag, out, x, tiles, func, scale=1.0):
    with Phase(nc, tag) as ph:
        with ph.block() as block:
            @block.scalar
            def _(act):
                for t in range(tiles):
                    act.activation(out[:, t], x[:, t], func, scale=scale)


def turn_rows(nc, tag, src, dst, tiles, ident):
    with Phase(nc, tag) as ph:
        ps = ph.psum("ps", [P, 2, BANK])
        turned, used = ph.sem("turned"), ph.sem("used")
        with ph.block() as block:
            @block.tensor
            def _(pe):
                for t in range(LT):
                    if t >= 2:
                        pe.wait_ge(used, t - 1)
                    for c in range(tiles):
                        tr = pe.transpose(ps[:, t % 2, c * P:(c + 1) * P], src[:, c, t * P:(t + 1) * P], ident)
                    tr.then_inc(turned, 1)

            @block.vector
            def _(dve):
                for t in range(LT):
                    dve.wait_ge(turned, t + 1)
                    dve.tensor_copy(dst[:, t, 0:tiles * P], ps[:, t % 2, 0:tiles * P]).then_inc(used, 1)


def hgrn_branch(nc, A, xn, out, work, small, masks, K):
    ones, ident = K[:, 0], K[:, 2]
    w = A["w_in_2"]
    with ExitStack() as ctx:
        q, f, key, v = (ctx.enter_context(nc.sbuf_tensor(f"hg_{n}", [P, 4, L], F32)) for n in ("q", "f", "key", "v"))
        v_tok = v[:].rearrange("p a (b c) -> p (a b) c", c=4 * P)
        project(nc, "hg_q", w["hq"], xn, q, 4, L, ACT.Silu)
        project(nc, "hg_f", w["hf"], xn, f, 4, L)
        project(nc, "hg_i", w["hi"], xn, work, 4, L)
        turn_rows(nc, "hg_t", work, v_tok, 4, ident)
        activate(nc, "hg_k", key, f, 4, ACT.Sigmoid, -1.0)
        soft(nc, "hg_s", f, work, 4, None, -1.0, -1)
        for h in range(4):
            gated_tile(nc, f"hg{h}", q[:, h], key[:, h], f[:, h], [v_tok[:, :, h * P:(h + 1) * P]], [out[:, h]], work,
                       masks, ident)
        project(nc, "hg_g", w["hg"], xn, q, 4, L, ACT.Silu)
        rms_norm(nc, "hg_n", out, out, 4, 1, KEY, ones, small[:, 0:4], None, L)
        multiply(nc, "hg_m", out, out, q, 4)


def gla_branch(nc, A, xn, out, small, masks, K):
    ones, ident = K[:, 0], K[:, 2]
    w = A["w_in_2"]
    with ExitStack() as ctx:
        def sb(name, shape):
            return ctx.enter_context(nc.sbuf_tensor(name, shape, F32))
        q, k, f, tmp = (sb(f"gl_{n}", [P, 2, L]) for n in ("q", "k", "f", "tmp"))
        work, v = sb("gl_work", [P, 4, L]), sb("gl_v", [P, 4, L])
        gate_w = sb("gl_gate_w", [P, 2, P])
        v_tok = v[:].rearrange("p a (b c) -> p (a b) c", c=4 * P)
        project(nc, "gl_q", w["gq"], xn, q, 2, L)
        project(nc, "gl_k", w["gk"], xn, k, 2, L)
        project(nc, "gl_i", w["gv"], xn, work, 4, L)
        turn_rows(nc, "gl_t", work, v_tok, 4, ident)
        project(nc, "gl_r", w["glr_sdt"], xn, tmp, 2, L)
        load(nc, "gl_load", [(gate_w[:], A["gla_gate_w"])])
        with Phase(nc, "gl_f") as ph:
            ps = ph.psum("ps", [P, 2, L])
            multiplied = ph.sem("multiplied")
            with ph.block() as block:
                @block.tensor
                def _(pe):
                    for m in range(2):
                        for lo, hi in segments(L):
                            mm = pe.matmul(ps[:, m, lo:hi], gate_w[:, m], tmp[:, 0, lo:hi], start=True, stop=True)
                        mm.then_inc(multiplied, 1)

                @block.scalar
                def _(act):
                    for m in range(2):
                        act.wait_ge(multiplied, m + 1)
                        act.activation(f[:, m], ps[:, m], ACT.Copy)
                        act.activation(q[:, m], q[:, m], ACT.Copy, scale=64 ** -0.5)
        soft(nc, "gl_s", f, tmp, 2, small[:, 4:6], -1.0 / 16.0, -1)
        for m in range(2):
            gated_tile(nc, f"gl{m}", q[:, m], k[:, m], f[:, m], [v_tok[:, :, h * P:(h + 1) * P] for h in (2 * m, 2 * m + 1)],
                       [out[:, 2 * m], out[:, 2 * m + 1]], work, masks, ident)
        project(nc, "gl_g", w["gg"], xn, work, 4, L, ACT.Silu)
        rms_norm(nc, "gl_n", out, out, 4, 1, KEY, ones, small[:, 6:10], None, L)
        multiply(nc, "gl_m", out, out, work, 4)


def lru_branch(nc, A, xn, out, small, taps):
    w = A["w_in_2"]
    with ExitStack() as ctx:
        def sb(name, shape):
            return ctx.enter_context(nc.sbuf_tensor(name, shape, F32))
        u, r, i, gate = (sb(f"lr_{n}", [P, 4, L]) for n in ("u", "r", "i", "gate"))
        wa = sb("lr_w", [P, 2, 4, P])
        rate, tmp = sb("lr_rate", [P, 1, 4]), sb("lr_tmp", [P, 1, 4])
        project_conv(nc, "lr_x", w["lx"], xn, u, 4, taps, 6, 3, 0, None)
        project(nc, "lr_g", w["lg"], xn, gate, 4, L, ACT.Gelu_apprx_tanh)
        load(nc, "lr_load", [(wa[:], A["lru_w"]), (rate[:, 0], A["small_2"][:, 18:22])])
        soft(nc, "lr_s", rate, tmp, 1, None, -8.0, -1)
        with Phase(nc, "lr_r") as ph:
            ps = ph.psum("ps", [P, 2, 2, L])
            multiplied, emptied = ph.sem("multiplied"), ph.sem("emptied")
            with ph.block() as block:
                @block.tensor
                def _(pe):
                    for t in range(4):
                        if t >= 2:
                            pe.wait_ge(emptied, 2 * (t - 1))
                        for g in range(2):
                            for lo, hi in segments(L):
                                mm = pe.matmul(ps[:, t % 2, g, lo:hi], wa[:, g, t], u[:, t, lo:hi], start=True, stop=True)
                        mm.then_inc(multiplied, 1)

                @block.scalar
                def _(act):
                    for t in range(4):
                        act.wait_ge(multiplied, t + 1)
                        act.activation(r[:, t], ps[:, t % 2, 0], ACT.Sigmoid, bias=small[:, 10 + t:11 + t]).then_inc(emptied, 1)
                        act.activation(i[:, t], ps[:, t % 2, 1], ACT.Sigmoid, bias=small[:, 14 + t:15 + t]).then_inc(emptied, 1)
        with Phase(nc, "lr_scan") as ph:
            th, inv = ph.sb("th", [P, L]), ph.sb("inv", [P, L])
            step, lane, rooted = ph.sem("step"), ph.sem("lane"), ph.sem("rooted")
            with ph.block() as block:
                @block.vector
                def _(dve):
                    count = [0]
                    for t in range(4):
                        if t:
                            dve.wait_ge(lane, 3 * t)
                        chained(dve, dve.tensor_scalar(r[:, t], r[:, t], rate[:, 0, t:t + 1], None, ALU.mult), step, count)
                        dve.wait_ge(lane, 3 * t + 1)
                        chained(dve, dve.tensor_scalar(inv[:], th[:], -1.0, 1.0, ALU.mult, ALU.add), step, count)
                        chained(dve, dve.reciprocal(inv[:], inv[:]), step, count)
                        chained(dve, dve.scalar_tensor_tensor(inv[:], th[:], -2.0, inv[:], ALU.mult, ALU.mult), step, count)
                        chained(dve, dve.tensor_tensor(i[:, t], i[:, t], u[:, t], ALU.mult), step, count)
                        dve.wait_ge(lane, 3 * t + 3)
                        chained(dve, dve.tensor_tensor(i[:, t], i[:, t], inv[:], ALU.mult), step, count)
                        chained(dve, dve.tensor_tensor_scan(u[:, t], r[:, t], i[:, t], 0.0, ALU.mult, ALU.add), step, count)
                        chained(dve, dve.tensor_tensor(out[:, t], u[:, t], gate[:, t], ALU.mult), step, count)

                @block.scalar
                def _(act):
                    for t in range(4):
                        act.wait_ge(step, 8 * t + 1)
                        act.activation(th[:], r[:, t], ACT.Tanh).then_inc(lane, 1)
                        act.wait_ge(lane, 3 * t + 1)
                        act.activation(r[:, t], r[:, t], ACT.Exp).then_inc(lane, 1)
                        act.wait_ge(step, 8 * t + 4)
                        act.activation(inv[:], inv[:], ACT.Sqrt).then_inc(lane, 1)


def ssd_branch(nc, A, xn, out, scratch, small, taps, masks, K):
    ones, ident = K[:, 0], K[:, 2]
    w = A["w_in_2"]
    with ExitStack() as ctx:
        def sb(name, shape):
            return ctx.enter_context(nc.sbuf_tensor(name, shape, F32))
        xbc = sb("sd_xbc", [P, 6, L])
        dt = sb("sd_dt", [P, 2, L])
        cs, left = sb("sd_cs", [SH, L]), sb("sd_left", [SH, L])
        tok = sb("sd_tok", [P, LT, 5 * P])
        heads = sb("sd_heads", [P, LT, 2, SH])
        picks = sb("sd_picks", [SH, 2 * SH + 4, P])
        project_conv(nc, "sd_x", w["sxbc"], xn, xbc, 6, taps, 0, 3, 0, ACT.Silu)
        project(nc, "sd_d", w["glr_sdt"], xn, dt, 2, L)
        load(nc, "sd_load", [(picks[:], A["ssd_picks"])])
        with ExitStack() as inner:
            tmp = inner.enter_context(nc.sbuf_tensor("sd_tmp", [SH, 1, L], F32))
            soft(nc, "sd_s", dt[0:SH, 1:2], tmp, 1, small[0:SH, 22:23], 1.0, 1)
        with Phase(nc, "sd_cum") as ph:
            keep = ph.sb("keep", [SH, LT, P])
            rate = ph.sb("rate", [SH, 1])
            da = ph.sb("da", [SH, L])
            ps = ph.psum("ps", [P, LT, 2, SH])
            step, exped, turned = ph.sem("step"), ph.sem("exped"), ph.sem("turned")
            with ph.block() as block:
                @block.scalar
                def _(act):
                    act.activation(rate[:], small[0:SH, 23:24], ACT.Exp).then_inc(exped, 1)
                    act.wait_ge(step, 5)
                    act.activation(left[:], left[:], ACT.Exp).then_inc(exped, 1)

                @block.vector
                def _(dve):
                    count = [0]
                    chained(dve, dve.memset(keep[:], 1.0), step, count)
                    chained(dve, dve.memset(keep[:, :, 0:1], 0.0), step, count)
                    dve.wait_ge(exped, 1)
                    chained(dve, dve.tensor_scalar(da[:], dt[0:SH, 1], rate[:], -1.0, ALU.mult, ALU.mult), step, count)
                    chained(dve, dve.tensor_tensor_scan(cs[:], keep[:].rearrange("p c t -> p (c t)"), da[:], 0.0,
                                                        ALU.mult, ALU.add), step, count)
                    chunks = cs[:].rearrange("p (c t) -> p c t", t=P)
                    chained(dve, dve.tensor_tensor(left[:].rearrange("p (c t) -> p c t", t=P),
                                                   spread(chunks[:, :, P - 1:P], [SH, LT, P]), chunks, ALU.subtract),
                            step, count)
                    dve.wait_ge(exped, 2)
                    chained(dve, dve.tensor_tensor(left[:], left[:], dt[0:SH, 1], ALU.mult), step, count)
                    dve.wait_ge(turned, 1)
                    dve.tensor_copy(heads[:], ps[:])

                @block.tensor
                def _(pe):
                    pe.wait_ge(step, 6)
                    for c in range(LT):
                        pe.transpose(ps[:, c, 0], dt[0:SH, 1, c * P:(c + 1) * P], ident[0:SH, 0:SH])
                        tr = pe.transpose(ps[:, c, 1], left[:, c * P:(c + 1) * P], ident[0:SH, 0:SH])
                    tr.then_inc(turned, 1)
        turn_rows(nc, "sd_t", xbc, tok[:, :, 0:4 * P], 4, ident)
        turn_rows(nc, "sd_tb", xbc[:, 4:5], tok[:, :, 4 * P:5 * P], 1, ident)
        ssd_heads(nc, A, xbc, cs, tok, heads, picks, out, scratch, masks)
        skip_gate(nc, A, xn, xbc, out, small)
    rms_norm(nc, "sd_n", out, out, 2, 2, 256, ones, small[:, 28:32], None, L)


def ssd_heads(nc, A, xbc, cs, tok, heads, picks, out, scratch, masks):
    with Phase(nc, "sd_heads") as ph:
        both = scratch[:, 0:2]
        xdt, xw = ph.sb("xdt", [P, 2, LT, HD]), ph.sb("xw", [P, 2, LT, HD])
        score = scratch[:, 2:4]
        decay = ph.sb("decay", [P, L])
        c_dec = ph.sb("c_dec", [P, L])
        state = ph.sb("state", [P, LT, HD])
        causal = ph.sb("causal", [P, P])
        seg = ph.psum("seg", [P, 2, L])
        wide = ph.psum("wide", [P, L])
        upd = ph.psum("upd", [P, LT, HD])
        yp = ph.psum("yp", [P, BANK])
        landed, products, grouped, segs, low, exped, scored, widened, wide_exped, queried, xs, updates, states, outs, copied = (
            ph.sem(s) for s in ("landed", "products", "grouped", "segs", "low", "exped", "scored", "widened", "wide_exped",
                                "queried", "xs", "updates", "states", "outs", "copied"))
        with ph.block() as block:
            @block.sync
            def _(sp):
                sp.dma_start(causal[:], A["causal"]).then_inc(landed, 16)

            @block.tensor
            def _(pe):
                for g in range(2):
                    r = slice(64 * g, 64 * g + 64)
                    for c in range(LT):
                        at = slice(c * P, (c + 1) * P)
                        mm = pe.matmul(seg[:, g, at], xbc[r, 4, at], xbc[r, 5, at], start=True, stop=True)
                    mm.then_inc(products, 1)
                pe.wait_ge(grouped, 2)
                for m in range(4):
                    for e in range(2):
                        n, h = 2 * m + e, m + 4 * e
                        if n >= 2:
                            pe.wait_ge(low, n - 1)
                        for c in range(LT):
                            at = slice(c * P, (c + 1) * P)
                            pe.matmul(seg[:, e, at], picks[:, h], cs[:, at], start=True, stop=False)
                            mm = pe.matmul(seg[:, e, at], cs[:, at], picks[:, SH + h], start=False, stop=True)
                        mm.then_inc(segs, 1)
                    if m:
                        pe.wait_ge(wide_exped, m)
                    for lo, hi in segments(L):
                        mm = pe.matmul(wide[:, lo:hi], picks[:, 2 * SH + m], cs[:, lo:hi], start=True, stop=True)
                    mm.then_inc(widened, 1)
                    pe.wait_ge(xs, 4 * m + 4)
                    if m:
                        pe.wait_ge(states, (LT - 1) * m)
                    for e in range(2):
                        for c in range(LT):
                            mm = pe.matmul(upd[64 * e:64 * e + 64, c], tok[:, c, 4 * P + 64 * e:4 * P + 64 * e + 64],
                                           xw[:, e, c], start=True, stop=True)
                    mm.then_inc(updates, 1)
                    pe.wait_ge(queried, m + 1)
                    pe.wait_ge(states, (LT - 1) * (m + 1))
                    for e in range(2):
                        n, h = 2 * m + e, m + 4 * e
                        pe.wait_ge(scored, n + 1)
                        o = slice(64 * (h % 2), 64 * (h % 2) + 64)
                        r = slice(64 * e, 64 * e + 64)
                        for part in range(2):
                            if 2 * n + part:
                                pe.wait_ge(copied, 2 * n + part)
                            for c in range(4 * part, 4 * part + 4):
                                at, to = slice(c * P, (c + 1) * P), slice((c % 4) * P, (c % 4 + 1) * P)
                                mm = pe.matmul(yp[o, to], xdt[:, e, c], score[:, e, at], start=True, stop=(c == 0))
                                if c:
                                    mm = pe.matmul(yp[o, to], state[r, c], c_dec[r, at], start=False, stop=True)
                            mm.then_inc(outs, 1)

            @block.vector
            def _(dve):
                dve.wait_ge(landed, 16)
                dve.memset(state[:, 0], 0.0)
                for g in range(2):
                    dve.wait_ge(products, g + 1)
                    dve.tensor_tensor(both[:, g].rearrange("p (c t) -> p c t", t=P),
                                      seg[:, g].rearrange("p (c t) -> p c t", t=P),
                                      spread(causal[:].unsqueeze(1), [P, LT, P]), ALU.mult).then_inc(grouped, 1)
                dve.wait_ge(grouped, 2)
                for m in range(4):
                    if m:
                        dve.wait_ge(outs, 4 * m)
                    for e in range(2):
                        n, h = 2 * m + e, m + 4 * e
                        x = tok[:, :, h * HD:(h + 1) * HD]
                        for dst, which in ((xdt, 0), (xw, 1)):
                            dve.tensor_tensor(dst[:, e], x, spread(heads[:, :, which, h:h + 1], [P, LT, HD]),
                                              ALU.mult).then_inc(xs, 1)
                        dve.wait_ge(segs, n + 1)
                        dve.tensor_scalar(score[:, e], seg[:, e], 0.0, None, ALU.min).then_inc(low, 1)
                    dve.wait_ge(wide_exped, m + 1)
                    dve.tensor_tensor(c_dec[:], xbc[:, 5], decay[:], ALU.mult).then_inc(queried, 1)
                    for e in range(2):
                        dve.wait_ge(exped, 2 * m + e + 1)
                        dve.tensor_tensor(score[:, e], score[:, e], both[:, e], ALU.mult).then_inc(scored, 1)
                    dve.wait_ge(updates, m + 1)
                    for c in range(LT - 1):
                        if c or m:
                            dve.wait_ge(states, (LT - 1) * m + c)
                        dve.scalar_tensor_tensor(state[:, c + 1], state[:, c], decay[:, (c + 1) * P - 1:(c + 1) * P],
                                                 upd[:, c], ALU.mult, ALU.add).then_inc(states, 1)

            @block.scalar
            def _(act):
                for m in range(4):
                    for e in range(2):
                        act.wait_ge(low, 2 * m + e + 1)
                        act.activation(score[:, e], score[:, e], ACT.Exp).then_inc(exped, 1)
                    act.wait_ge(widened, m + 1)
                    if m:
                        act.wait_ge(queried, m)
                        act.wait_ge(states, (LT - 1) * m)
                    act.activation(decay[:], wide[:], ACT.Exp).then_inc(wide_exped, 1)
                    for e in range(2):
                        n, h = 2 * m + e, m + 4 * e
                        o = slice(64 * (h % 2), 64 * (h % 2) + 64)
                        for part in range(2):
                            act.wait_ge(outs, 2 * n + part + 1)
                            act.activation(out[o, h // 2, part * BANK:(part + 1) * BANK], yp[o, :],
                                           ACT.Copy).then_inc(copied, 1)


def skip_gate(nc, A, xn, xbc, out, small):
    z = xbc[:, 0:4]
    with Phase(nc, "sd_skip") as ph:
        with ph.block() as block:
            @block.vector
            def _(dve):
                for t in range(4):
                    dve.scalar_tensor_tensor(out[:, t], xbc[:, t], small[:, 24 + t:25 + t], out[:, t], ALU.mult, ALU.add)
    project(nc, "sd_z", A["w_in_2"]["sz"], xn, z, 4, L, ACT.Silu)
    multiply(nc, "sd_m", out, out, z, 4)


def merge(nc, A, xn, ys, merged):
    B = 4
    with Phase(nc, "merge") as ph:
        wgate = ph.sb("wgate", [P, 2, DT, P])
        wbr = ph.sb("wbr", [P, 2, 4, P])
        gates, part = ph.sb("gates", [P, 2, L]), ph.sb("part", [P, L])
        ps = ph.psum("ps", [P, 2, 2, L])
        gate_in = [ph.sem(f"gate_in{b}") for b in range(2)]
        branch_in = [ph.sem(f"branch_in{b}") for b in range(2)]
        gate_mul, branch_mul, gated, emptied, step = (ph.sem(s) for s in ("gate_mul", "branch_mul", "gated", "emptied", "step"))
        with ph.block() as block:
            @block.sync
            def _(sp):
                with sp.Fori(0, DT) as m:
                    for n in range(B):
                        b = n % 2
                        sp.wait_ge(gate_mul, m * B + (n + 1))
                        sp.dma_start(wgate[:, b], A["w_gates"][m * B + n]).then_inc(gate_in[b], 16)
                        sp.wait_ge(branch_mul, m * B + (n + 1))
                        sp.dma_start(wbr[:, b], A["w_branches"][m * B + n]).then_inc(branch_in[b], 16)

            @block.tensor
            def _(pe):
                pe.sem_inc(gate_mul, 2)
                pe.sem_inc(branch_mul, 2)
                pe.sem_inc(emptied, 2)
                pe.sem_inc(gated, 2)
                with pe.Fori(0, DT) as m:
                    for n in range(B):
                        b = n % 2
                        pe.wait_ge(gate_in[b], m * 32 + (16 * (n // 2) + 16))
                        pe.wait_ge(gated, m * B + (n + 1))
                        for k in range(DT):
                            for lo, hi in segments(L):
                                mm = pe.matmul(ps[:, b, 0, lo:hi], wgate[:, b, k], xn[:, k, lo:hi],
                                               start=(k == 0), stop=(k == DT - 1))
                        mm.then_inc(gate_mul, 1)
                        pe.wait_ge(branch_in[b], m * 32 + (16 * (n // 2) + 16))
                        pe.wait_ge(emptied, m * B + (n + 1))
                        for k in range(4):
                            for lo, hi in segments(L):
                                mm = pe.matmul(ps[:, b, 1, lo:hi], wbr[:, b, k], ys[:, 4 * n + k, lo:hi],
                                               start=(k == 0), stop=(k == 3))
                        mm.then_inc(branch_mul, 1)

            @block.scalar
            def _(act):
                with act.Fori(0, DT) as m:
                    for n in range(B):
                        act.wait_ge(gate_mul, m * B + (n + 3))
                        act.wait_ge(emptied, m * B + (n + 1))
                        act.activation(gates[:, n % 2], ps[:, n % 2, 0], ACT.Sigmoid).then_inc(gated, 1)

            @block.vector
            def _(dve):
                with dve.Fori(0, DT) as m:
                    for n in range(B):
                        dve.wait_ge(gated, m * B + (n + 3))
                        dve.wait_ge(branch_mul, m * B + (n + 3))
                        if n == 0:
                            dve.tensor_tensor(merged[:, m], ps[:, 0, 1], gates[:, 0], ALU.mult).then_inc(emptied, 1)
                        else:
                            dve.tensor_tensor(part[:], ps[:, n % 2, 1], gates[:, n % 2], ALU.mult).then_inc(emptied, 1)
                            dve.wait_ge(emptied, m * B + (n + 3))
                            dve.tensor_tensor(merged[:, m], merged[:, m], part[:], ALU.add).then_inc(step, 1)
                            dve.wait_ge(step, m * (B - 1) + n)


def mixer_layer(nc, A, x_in, x_out, K):
    ones = K[:, 0]
    with ExitStack() as ctx:
        def sb(name, shape):
            return ctx.enter_context(nc.sbuf_tensor(name, shape, F32))
        small = sb("m_small", [P, 48])
        taps = sb("m_taps", [P, 10, 5])
        masks = sb("m_masks", [P, LEVELS + 1, P])
        ys = sb("m_ys", [P, 16, L])
        xn = sb("m_xn", [P, DT, L])
        load(nc, "m_load", [(small[:], A["small_2"]), (taps[:], A["taps_2"]), (masks[:], A["level_masks"]),
                            (xn[:], x_in)])
        rms_norm(nc, "m_n", xn, xn, 1, DT, D, ones, small[:, 32:40], None, L)
        hgrn_branch(nc, A, xn, ys[:, 0:4], ys[:, 4:8], small, masks, K)
        ssd_branch(nc, A, xn, ys[:, 4:8], ys[:, 8:12], small, taps, masks, K)
        gla_branch(nc, A, xn, ys[:, 8:12], small, masks, K)
        lru_branch(nc, A, xn, ys[:, 12:16], small, taps)
        merged = sb("m_merged", [P, DT, L])
        merge(nc, A, xn, ys, merged)
        x = xn
        load(nc, "m_load2", [(x[:], x_in)])
        project_residual(nc, "m_out", A["w_out_2"], merged, None, x)
        store(nc, "m_store", x_out, x)


def ffn_layer(nc, A, x_in, out, K):
    FT = 22
    ones = K[:, 0]
    with ExitStack() as ctx:
        def sb(name, shape):
            return ctx.enter_context(nc.sbuf_tensor(name, shape, F32))
        small = sb("f_small", [P, 2, DT])
        x = sb("f_x", [P, DT, L])
        hidden = sb("f_hidden", [P, FT, L])
        with ExitStack() as inner:
            xn = inner.enter_context(nc.sbuf_tensor("f_xn", [P, DT, L], F32))
            load(nc, "f_load", [(x[:], x_in), (small[:], A["norms_2"])])
            rms_norm(nc, "f_n", x, xn, 1, DT, D, ones, small[:, 0], None, L)
            with Phase(nc, "f_in") as ph:
                wbuf = ph.sb("wbuf", [P, 2, 2 * DT, P])
                ps = ph.psum("ps", [P, 2, 2, L])
                act_out = ph.sb("act_out", [P, 2, L])
                loaded = [ph.sem(f"loaded{b}") for b in range(2)]
                multiplied, emptied, silued = (ph.sem(s) for s in ("multiplied", "emptied", "silued"))
                with ph.block() as block:
                    @block.sync
                    def _(sp):
                        load_weight_tiles(sp, A["w_ffn_in_2"], wbuf, FT, loaded, multiplied)

                    @block.tensor
                    def _(pe):
                        pe.sem_inc(multiplied, 2)
                        pe.sem_inc(emptied, 2)
                        with pe.Fori(0, FT // 2) as pair:
                            for b in range(2):
                                pe.wait_ge(loaded[b], pair * 16 + 16)
                                pe.wait_ge(emptied, pair * 2 + (b + 1))
                                for part in range(2):
                                    for k in range(DT):
                                        for lo, hi in segments(L):
                                            mm = pe.matmul(ps[:, b, part, lo:hi], wbuf[:, b, part * DT + k],
                                                           xn[:, k, lo:hi], start=(k == 0), stop=(k == DT - 1))
                                mm.then_inc(multiplied, 1)

                    @block.scalar
                    def _(act):
                        with act.Fori(0, FT // 2) as pair:
                            for b in range(2):
                                act.wait_ge(multiplied, pair * 2 + (b + 3))
                                act.wait_ge(emptied, pair * 2 + (b + 1))
                                act.activation(act_out[:, b], ps[:, b, 0], ACT.Silu).then_inc(silued, 1)

                    @block.vector
                    def _(dve):
                        with dve.Fori(0, FT // 2) as pair:
                            for b in range(2):
                                dve.wait_ge(silued, pair * 2 + (b + 1))
                                dve.tensor_tensor(hidden[:, pair * 2 + b], ps[:, b, 1], act_out[:, b],
                                                  ALU.mult).then_inc(emptied, 1)
        project_residual(nc, "f_out", A["w_ffn_out_2"], hidden, None, x)
        rms_norm(nc, "f_fn", x, x, 1, DT, D, ones, small[:, 1], None, L)
        store(nc, "f_store", out, x)


def weight_tiles(w):
    k, m = w.shape
    w = np.concatenate([w, np.zeros((k, -m % P), w.dtype)], axis=1)
    return w.reshape(k // P, P, -1, P).transpose(2, 1, 0, 3)


def channels(x):
    return x.T.reshape(-1, P, x.shape[0]).transpose(1, 0, 2)


def columns(v):
    return np.moveaxis(v.reshape(*v.shape[:-1], -1, P), -1, 0)


def swap_matrix(blocks):
    m = np.zeros((P, P), np.float32)
    for first, w in blocks:
        for half in range(2):
            for j in range(w):
                a = first + half * 2 * w + j
                m[a + w, a] = -1.0
                m[a, a + w] = 1.0
    return m


def rope_tables(blocks):
    cos, sin = np.ones((P, N), np.float32), np.zeros((P, N), np.float32)
    t = np.arange(L)
    for first, w in blocks:
        inv = np.float32(10000.0) ** (-np.arange(w, dtype=np.float32) / np.float32(w))
        for half, pos in enumerate((t // GRID, t % GRID)):
            angle = (pos.astype(np.float32)[None] * inv[:, None]).astype(np.float64)
            for part in range(2):
                rows = slice(first + half * 2 * w + part * w, first + half * 2 * w + (part + 1) * w)
                cos[rows, :L], sin[rows, :L] = np.cos(angle), np.sin(angle)
    return cos, sin


def attention_arrays(i):
    w = i["attn_w_in"][0]
    q, k, v, cq, ckv, kpe, gate = np.split(w, np.cumsum([512, 128, 128, 256, 128, 32]), axis=1)
    q = q.reshape(D, 2, 4, HD).transpose(0, 2, 1, 3).reshape(D, 512)
    kpe = np.concatenate([np.zeros((D, HD), w.dtype), kpe, np.zeros((D, P - HD - ROPE), w.dtype)], axis=1)
    uq = i["mla_w_uq"][0].reshape(256, QH, HD + ROPE)
    uq = np.concatenate([uq, np.zeros((256, QH, P - HD - ROPE), w.dtype)], axis=2).reshape(256, QH * P)
    ukv = i["mla_w_ukv"][0].reshape(P, QH, 2 * HD)
    wk = np.concatenate([ukv[:, :, :HD], np.zeros((P, QH, HD), w.dtype)], axis=2)
    qn, kn = i["attn_q_norm"][0], i["attn_k_norm"][0]
    qk = np.stack([np.tile(qn, 2)] * 4 + [np.tile(kn, 2)], axis=1)
    small = np.concatenate([qk, columns(i["mla_q_norm"][0]), columns(i["mla_kv_norm"][0])], axis=1)
    a_blocks, m_blocks = [(0, 16), (HD, 16)], [(HD, 8)]
    half = np.kron(np.eye(2), np.ones((HD, HD)))
    return {
        "x": channels(i["x"][0]), "ctx": channels(i["ctx"][0]),
        "c2": columns(np.stack([i["c"][0], i["c_ctx"]])).transpose(0, 2, 1),
        "ada_w": np.concatenate([weight_tiles(i["ada_w"][0]), weight_tiles(i["ada_w"][1])]),
        "ada_b": columns(i["ada_b"]).reshape(P, -1), "norm_w": columns(i["norm_w"]),
        "attn_w_lat": weight_tiles(np.concatenate([q, cq, gate], axis=1)),
        "attn_w_both": weight_tiles(np.concatenate([k, ckv, kpe, v], axis=1)),
        "attn_small": small, "mla_w_uq": weight_tiles(uq), "mla_wk": wk,
        "mla_wv": ukv[:, :, HD:].reshape(P, QH * HD), "attn_w_out": weight_tiles(i["attn_w_out"][0]),
        "rope": np.stack(rope_tables(a_blocks) + rope_tables(m_blocks)),
        "matrices": np.stack([np.ones((P, P)), half, np.eye(P), swap_matrix(a_blocks), swap_matrix(m_blocks)],
                             axis=1).astype(np.float32),
    }


def hyena_arrays(i):
    t = np.linspace(0.0, 1.0, L, dtype=np.float32)[:, None]
    w = (np.float32(2.0 * math.pi / L)) * np.arange(L, dtype=np.float32)[:, None]
    bands = np.linspace(1e-4, 15, 16, dtype=np.float32)
    angle = (w * bands).astype(np.float64)
    emb = np.concatenate([t, np.cos(angle), -np.sin(angle)], axis=-1).astype(np.float32)
    deltas = np.abs(np.linspace(math.log(1e-2) / 1.5, math.log(1e-2) / 0.3, D))
    decay = np.exp(-t.astype(np.float64) * deltas).astype(np.float32)
    k, n = np.arange(L) + 0.5, np.arange(L)
    lag = 2 * np.pi / (2 * L) * np.outer(n, k)
    pos = 2 * np.pi / (2 * L) * np.outer(n + 0.5, k)

    def tables(a):
        return np.concatenate([weight_tiles(np.cos(a)), weight_tiles(np.sin(a))], axis=2).astype(np.float32)

    w3 = np.concatenate([i["hy_ffn_w3"][0], i["hy_ffn_b3"]], axis=0).reshape(65, 2, 2, D).transpose(1, 0, 2, 3)
    taps = np.concatenate([i["hy_conv_w"][0], i["hy_conv_b"]], axis=0)
    return {
        "hy_emb": emb.T, "hy_w1": i["hy_ffn_w1"][0], "hy_w2": i["hy_ffn_w2"][0],
        "hy_small": np.stack([i["hy_ffn_b1"][0], i["hy_ffn_b2"][0], i["hy_freq"][0]], axis=1),
        "hy_w3": w3, "hy_decay": decay.reshape(LT, P, D), "hy_lag_tables": tables(lag), "hy_tables": tables(pos),
        "hy_skip": np.broadcast_to(i["hy_skip"][0][:, None], (2, P, D)),
        "hy_taps": columns(taps).transpose(0, 2, 1), "hy_w_in": weight_tiles(i["hy_w_in"][0]),
        "hy_w_out": weight_tiles(i["hy_w_out"][0]), "final_norm_w": columns(i["final_norm_w"]),
    }


def block_arrays(i):
    i = {k[:-2]: v for k, v in i.items() if k.endswith("_2")}
    w = i["w_in"][0]
    sizes = [512, 512, 512, 512, 512, 768, 8, 256, 256, 512, 512, 16, 512, 512, 4096]
    names = ["hq", "hf", "hi", "hg", "sz", "sxbc", "sdt", "gq", "gk", "gv", "gg", "glr", "lx", "lg", "mg"]
    parts = {n: weight_tiles(p) for n, p in zip(names, np.split(w, np.cumsum(sizes)[:-1], axis=1))}
    parts["glr_sdt"] = np.concatenate([parts.pop("glr"), parts.pop("sdt")])
    gates = parts.pop("mg").reshape(4, DT, P, DT, P).transpose(1, 0, 2, 3, 4).reshape(4 * DT, P, DT, P)
    branches = np.stack([weight_tiles(b) for b in i["w_branch"][0]], axis=1).reshape(4 * DT, P, 4, P)
    small = np.zeros((P, 48), np.float32)

    def put(at, cols):
        small[:cols.shape[0], at:at + cols.shape[1]] = cols

    put(0, np.tile(i["hgrn_norm_w"][0][:, None], (1, 4)))
    put(4, columns(i["gla_gate_b"][0]))
    put(6, np.tile(i["gla_norm_w"][0][:, None], (1, 4)))
    put(10, columns(i["lru_ba"][0]))
    put(14, columns(i["lru_bx"][0]))
    put(18, columns(i["lru_lambda"][0]))
    put(22, i["ssd_dt_bias"][0][:, None])
    put(23, i["ssd_a_log"][0][:, None])
    put(24, columns(np.repeat(i["ssd_d"][0], HD)))
    put(28, columns(i["ssd_norm_w"][0]))
    put(32, columns(i["norm_mix_w"][0]))
    taps = np.concatenate([np.concatenate([i["ssd_conv_w"][0], i["ssd_conv_b"]]),
                           np.concatenate([i["lru_conv_w"][0], i["lru_conv_b"]])], axis=1)
    gate_w = np.zeros((P, 2 * P), np.float32)
    gate_w[:16] = i["gla_gate_w"][0]
    lru = np.zeros((P, 2, 4, P), np.float32)
    for n, name in enumerate(("lru_wa", "lru_wx")):
        for b in range(8):
            r = slice(64 * (b % 2), 64 * (b % 2) + 64)
            lru[r, n, b // 2, r] = i[name][0][b]
    j, k = np.arange(P)[:, None], np.arange(P)[None]
    masks = [j == k]
    for level in range(LEVELS):
        half = 2 ** level
        masks.append((j // (2 * half) == k // (2 * half)) & (j // half % 2 == 0) & (k // half % 2 == 1))
    picks = np.zeros((SH, 2 * SH + 4, P), np.float32)
    for h in range(SH):
        picks[h, h], picks[h, SH + h] = 1.0, -1.0
    for m in range(4):
        picks[m, 2 * SH + m, :64], picks[4 + m, 2 * SH + m, 64:] = 1.0, 1.0
    ffn = i["w_ffn_in"][0]
    ffn = np.concatenate([weight_tiles(ffn[:, :2816]), weight_tiles(ffn[:, 2816:])], axis=2)
    out = {f"w_in_2_{n}": p for n, p in parts.items()}
    out.update({
        "w_gates": gates, "w_branches": branches, "small_2": small, "taps_2": columns(taps).transpose(0, 2, 1),
        "gla_gate_w": gate_w.reshape(P, 2, P), "lru_w": lru, "level_masks": np.stack(masks, axis=1).astype(np.float32),
        "causal": (j <= k).astype(np.float32), "ssd_picks": picks, "w_out_2": weight_tiles(i["w_out"][0]),
        "w_ffn_in_2": ffn, "w_ffn_out_2": weight_tiles(i["w_ffn_out"][0]),
        "norms_2": columns(np.stack([i["norm_ffn_w"][0], i["norm_f_w"]])),
    })
    return out


def build(nc, A):
    A["w_in_2"] = {name[7:]: ap for name, ap in A.items() if name.startswith("w_in_2_")}
    with ExitStack() as ctx:
        K = ctx.enter_context(nc.sbuf_tensor("matrices", [P, 5, P], F32))
        mod = ctx.enter_context(nc.sbuf_tensor("mod", [P, 6 * DT, 2], F32))
        one_plus = ctx.enter_context(nc.sbuf_tensor("one_plus", [P, 2, 2, DT], F32))
        load(nc, "load_matrices", [(K[:], A["matrices"])])
        modulation(nc, A, mod, one_plus)
        attention_layer(nc, A, A["x1"], mod, one_plus, K)
        hyena_layer(nc, A, A["x1"], A["x2"], mod, one_plus, K)
        mixer_layer(nc, A, A["x2"], A["x3"], K)
        ffn_layer(nc, A, A["x3"], A["out"], K)


def kernel(**inputs):
    import concourse.bacc as bacc
    from concourse.bass_utils import run_bass_kernel_spmd

    nc = bacc.Bacc("TRN2", target_bir_lowering=False, num_devices=1)
    i = {name: np.asarray(value) for name, value in inputs.items()}
    arrays = {**attention_arrays(i), **hyena_arrays(i), **block_arrays(i)}
    arrays = {name: np.ascontiguousarray(a) for name, a in arrays.items()}
    A = {name: nc.dram_tensor(f"in_{name}", a.shape, mybir.dt.from_np(a.dtype), kind="ExternalInput").ap()
         for name, a in arrays.items()}
    for name in ("x1", "x2", "x3"):
        A[name] = nc.dram_tensor(name, (P, DT, L), F32, kind="Internal").ap()
    A["spectrum"] = nc.dram_tensor("spectrum", (2 * DT, P, 2, D), F32, kind="Internal").ap()
    A["out"] = nc.dram_tensor("out", (P, DT, L), F32, kind="ExternalOutput").ap()
    build(nc, A)
    r = run_bass_kernel_spmd(nc, [{f"in_{name}": a for name, a in arrays.items()}], core_ids=[0])
    out = r.results[0]["out"]
    return out.transpose(2, 1, 0).reshape(1, L, D)
```

```python
from contextlib import ExitStack
import math

import numpy as np
import concourse.bass as bass
from concourse import mybir
from concourse.alu_op_type import AluOpType as ALU

ACT = mybir.ActivationFunctionType
F32 = mybir.dt.float32
AX_X = mybir.AxisListType.X

P = 128
D = 1024
DT = D // P
L = 1024
LT = L // P
C = 256
N = L + C
NT = N // P
BANK = 512
EPS = 1e-6
QH = 8
HD = 64
ROPE = 32
GRID = 64
HALF = 512


class Phase:

    def __init__(self, nc, tag):
        self.nc, self.tag, self.ctx, self.sems = nc, tag, ExitStack(), []

    def __enter__(self):
        return self

    def __exit__(self, *e):
        self.ctx.close()
        if e[0] is None:
            self.nc.clear_and_free_semaphores(self.sems)
            self.nc.all_engine_barrier(sem_only=True)

    def sb(self, name, shape):
        return self.ctx.enter_context(self.nc.sbuf_tensor(f"{self.tag}_{name}", shape, F32))

    def psum(self, name, shape):
        return self.ctx.enter_context(self.nc.psum_tensor(f"{self.tag}_{name}", shape, F32))

    def sem(self, name):
        s = self.nc.alloc_semaphore(f"{self.tag}_{name}")
        self.sems.append(s)
        return s

    def block(self):
        return self.nc.Block(no_gpsimd_drain=True)


def segments(cols):
    return [(a, min(a + BANK, cols)) for a in range(0, cols, BANK)]


def banked(cols):
    return -(-cols // BANK) * BANK


def chained(eng, ins, sem, count):
    count[0] += 1
    ins.then_inc(sem, 1)
    eng.wait_ge(sem, count[0])


def load_weight_tiles(sp, w, wbuf, tiles, loaded, multiplied, before=0):
    with sp.Fori(0, tiles // 2) as pair:
        for b in range(2):
            sp.wait_ge(multiplied, pair * 2 + (before + b + 1))
            sp.dma_start(wbuf[:, b], w[pair * 2 + b]).then_inc(loaded[b], 16)


def multiply_weight_tiles(pe, wbuf, ps, rhs, cols, tiles, loaded, multiplied, emptied, before=0):
    kt = wbuf.shape[2]
    if not before:
        pe.sem_inc(multiplied, 2)
        pe.sem_inc(emptied, 2)
    with pe.Fori(0, tiles // 2) as pair:
        for b in range(2):
            pe.wait_ge(loaded[b], pair * 16 + (16 + 8 * before))
            pe.wait_ge(emptied, pair * 2 + (before + b + 1))
            for k in range(kt):
                for lo, hi in segments(cols):
                    mm = pe.matmul(ps[:, b, lo:hi], wbuf[:, b, k], rhs[:, k, lo:hi],
                                   start=(k == 0), stop=(k == kt - 1))
            mm.then_inc(multiplied, 1)


def load(nc, tag, pairs):
    with Phase(nc, tag) as ph:
        landed = ph.sem("landed")
        with ph.block() as block:
            @block.sync
            def _(sp):
                for dst, src in pairs:
                    sp.dma_start(dst, src).then_inc(landed, 16)
                sp.wait_ge(landed, 16 * len(pairs))


def store(nc, tag, dst, src):
    with Phase(nc, tag) as ph:
        stored = ph.sem("stored")
        with ph.block() as block:
            @block.sync
            def _(sp):
                sp.dma_start(dst, src[:]).then_inc(stored, 16)
                sp.wait_ge(stored, 16)


def project(nc, tag, w, rhs, out, tiles, cols, func=ACT.Copy):
    project_each(nc, tag, rhs, cols, [(w, out, tiles, func)])


def project_each(nc, tag, rhs, cols, jobs):
    befores = [sum(job[2] for job in jobs[:n]) for n in range(len(jobs))]
    with Phase(nc, tag) as ph:
        kt = jobs[0][0].shape[2]
        wbuf = ph.sb("wbuf", [P, 2, kt, P])
        ps = ph.psum("ps", [P, 2, banked(cols)])
        loaded = [ph.sem(f"loaded{b}") for b in range(2)]
        multiplied, emptied = ph.sem("multiplied"), ph.sem("emptied")
        with ph.block() as block:
            @block.sync
            def _(sp):
                for (w, out, tiles, func), before in zip(jobs, befores):
                    load_weight_tiles(sp, w, wbuf, tiles, loaded, multiplied, before)

            @block.tensor
            def _(pe):
                for (w, out, tiles, func), before in zip(jobs, befores):
                    multiply_weight_tiles(pe, wbuf, ps, rhs, cols, tiles, loaded, multiplied, emptied, before)

            @block.scalar
            def _(act):
                for (w, out, tiles, func), before in zip(jobs, befores):
                    with act.Fori(0, tiles // 2) as pair:
                        for b in range(2):
                            act.wait_ge(multiplied, pair * 2 + (before + b + 3))
                            act.activation(out[:, pair * 2 + b, 0:cols], ps[:, b, 0:cols], func).then_inc(emptied, 1)


def rms_norm(nc, tag, x, out, groups, per, width, summing, weight, shift, cols):
    with Phase(nc, tag) as ph:
        squares = ph.sb("squares", [P, 2, cols])
        sums = ph.sb("sums", [P, cols]) if per > 1 else None
        mean = ph.sb("mean", [P, cols])
        root = ph.sb("root", [P, cols])
        inverse = ph.sb("inverse", [P, cols])
        ps = ph.psum("ps", [P, 2, banked(cols)])
        squared, summed, mean_ready, rooted = (ph.sem(s) for s in ("squared", "summed", "mean_ready", "rooted"))
        inverse_ready, scaled, added = ph.sem("inverse_ready"), ph.sem("scaled"), ph.sem("added")
        adds = per - 1
        with ph.block() as block:
            @block.scalar
            def _(act):
                for g in range(groups):
                    for n in range(g * per, (g + 1) * per):
                        if n >= 2 and per == 1:
                            act.wait_ge(summed, n - 1)
                        elif n >= 2:
                            act.wait_ge(added, (n - 2) // per * adds + max((n - 2) % per, 1))
                        act.activation(squares[:, n % 2], x[:, n], ACT.Square).then_inc(squared, 1)
                    act.wait_ge(mean_ready, g + 1)
                    act.activation(root[:], mean[:], ACT.Sqrt).then_inc(rooted, 1)
                    if shift is not None:
                        for n in range(g * per, (g + 1) * per):
                            act.wait_ge(scaled, n + 1)
                            act.activation(out[:, n], out[:, n], ACT.Identity, bias=shift[:, n:n + 1])

            @block.tensor
            def _(pe):
                for g in range(groups):
                    if g >= 2:
                        pe.wait_ge(mean_ready, g - 1)
                    if per == 1:
                        pe.wait_ge(squared, g + 1)
                        total = squares[:, g % 2]
                    else:
                        pe.wait_ge(added, (g + 1) * adds)
                        total = sums
                    for lo, hi in segments(cols):
                        mm = pe.matmul(ps[:, g % 2, lo:hi], summing, total[:, lo:hi], start=True, stop=True)
                    mm.then_inc(summed, 1)

            @block.vector
            def _(dve):
                for g in range(groups):
                    for t in range(1, per):
                        n = g * per + t
                        dve.wait_ge(squared, n + 1)
                        if t > 1:
                            dve.wait_ge(added, g * adds + t - 1)
                        dve.tensor_tensor(sums[:], squares[:, (n - 1) % 2] if t == 1 else sums[:], squares[:, n % 2],
                                          ALU.add).then_inc(added, 1)
                    dve.wait_ge(summed, g + 1)
                    dve.tensor_scalar(mean[:], ps[:, g % 2, 0:cols], 1.0 / width, EPS, ALU.mult,
                                      ALU.add).then_inc(mean_ready, 1)
                    dve.wait_ge(rooted, g + 1)
                    dve.reciprocal(inverse[:], root[:]).then_inc(inverse_ready, 1)
                    dve.wait_ge(inverse_ready, g + 1)
                    for n in range(g * per, (g + 1) * per):
                        if weight is None:
                            ins = dve.tensor_tensor(out[:, n], x[:, n], inverse[:], ALU.mult)
                        else:
                            ins = dve.scalar_tensor_tensor(out[:, n], x[:, n], weight[:, n:n + 1], inverse[:],
                                                           ALU.mult, ALU.mult)
                        ins.then_inc(scaled, 1)


def modulation(nc, A, mod, one_plus):
    tiles = 2 * 3 * DT
    by_step = mod[:].rearrange("p (s m) two -> p s (m two)", m=A["ada_w"].shape[2] // DT)
    with ExitStack() as ctx:
        cs = ctx.enter_context(nc.sbuf_tensor("ada_c", [P, DT, 2], F32))
        bias = ctx.enter_context(nc.sbuf_tensor("ada_bias", [P, tiles], F32))
        normw = ctx.enter_context(nc.sbuf_tensor("ada_normw", [P, 2, DT], F32))
        load(nc, "ada_load", [(cs[:], A["c2"]), (bias[:], A["ada_b"]), (normw[:], A["norm_w"])])
        with Phase(nc, "ada_silu") as ph:
            done = ph.sem("silu_done")
            with ph.block() as block:
                @block.scalar
                def _(act):
                    act.activation(cs[:], cs[:], ACT.Silu).then_inc(done, 1)
        per = A["ada_w"].shape[2] // DT
        steps = tiles // per
        with Phase(nc, "ada") as ph:
            wbuf = ph.sb("wbuf", [P, 2, per * DT, P])
            ps = ph.psum("ps", [P, 2, BANK])
            loaded = [ph.sem(f"loaded{b}") for b in range(2)]
            multiplied, emptied = ph.sem("multiplied"), ph.sem("emptied")
            with ph.block() as block:
                @block.sync
                def _(sp):
                    load_weight_tiles(sp, A["ada_w"], wbuf, steps, loaded, multiplied)

                @block.tensor
                def _(pe):
                    pe.sem_inc(multiplied, 2)
                    pe.sem_inc(emptied, 2)
                    with pe.Fori(0, steps // 2) as pair:
                        for b in range(2):
                            pe.wait_ge(loaded[b], pair * 16 + 16)
                            pe.wait_ge(emptied, pair * 2 + (b + 1))
                            for j in range(per):
                                for k in range(DT):
                                    mm = pe.matmul(ps[:, b, 2 * j:2 * j + 2], wbuf[:, b, j * DT + k], cs[:, k],
                                                   start=(k == 0), stop=(k == DT - 1))
                            mm.then_inc(multiplied, 1)

                @block.scalar
                def _(act):
                    with act.Fori(0, steps // 2) as pair:
                        for b in range(2):
                            act.wait_ge(multiplied, pair * 2 + (b + 3))
                            act.activation(by_step[:, pair * 2 + b], ps[:, b, 0:2 * per], ACT.Copy).then_inc(emptied, 1)
        with Phase(nc, "ada_bias") as ph:
            done = ph.sem("bias_added")
            with ph.block() as block:
                @block.vector
                def _(dve):
                    for s in range(2):
                        dve.tensor_tensor(mod[:, :, s], mod[:, :, s], bias[:], ALU.add).then_inc(done, 1)
                    dve.wait_ge(done, 2)
                    for layer in range(2):
                        for s in range(2):
                            first = (3 * layer + 1) * DT
                            dve.scalar_tensor_tensor(one_plus[:, layer, s], mod[:, first:first + DT, s], 1.0,
                                                     normw[:, layer], ALU.add, ALU.mult)


def rotate(nc, tag, x, tiles, swap, cos, sin, cols):
    with Phase(nc, tag) as ph:
        ps = ph.psum("ps", [P, 2, banked(cols)])
        turned = ph.sb("turned", [P, cols])
        swapped, straight, crossed, added = (ph.sem(s) for s in ("swapped", "straight", "crossed", "added"))
        with ph.block() as block:
            @block.tensor
            def _(pe):
                for t in range(tiles):
                    if t >= 2:
                        pe.wait_ge(crossed, t - 1)
                    for lo, hi in segments(cols):
                        mm = pe.matmul(ps[:, t % 2, lo:hi], swap, x[:, t, lo:hi], start=True, stop=True)
                    mm.then_inc(swapped, 1)

            @block.vector
            def _(dve):
                for t in range(tiles):
                    dve.wait_ge(swapped, t + 1)
                    dve.tensor_tensor(turned[:], ps[:, t % 2, 0:cols], sin[:, 0:cols], ALU.mult).then_inc(crossed, 1)
                    dve.tensor_tensor(x[:, t], x[:, t], cos[:, 0:cols], ALU.mult).then_inc(straight, 1)
                    dve.wait_ge(crossed, t + 1)
                    dve.wait_ge(straight, t + 1)
                    dve.tensor_tensor(x[:, t], x[:, t], turned[:], ALU.add).then_inc(added, 1)
                    dve.wait_ge(added, t + 1)


def mla_keys_values(nc, A, ckv, kpe, k_m, v_m, v_ch, v_a, ident):
    with Phase(nc, "mla_kv") as ph:
        wk = ph.sb("wk", [P, QH, P])
        wv = ph.sb("wv", [P, QH * HD])
        ps = ph.psum("ps", [P, 2, banked(N)])
        landed, keys, keys_read, values, values_read = (
            ph.sem(s) for s in ("landed", "keys", "keys_read", "values", "values_read"))
        with ph.block() as block:
            @block.sync
            def _(sp):
                sp.dma_start(wk[:], A["mla_wk"]).then_inc(landed, 16)
                sp.dma_start(wv[:], A["mla_wv"]).then_inc(landed, 16)

            @block.tensor
            def _(pe):
                pe.wait_ge(landed, 32)
                for h in range(QH):
                    if h >= 2:
                        pe.wait_ge(keys_read, h - 1)
                    for lo, hi in segments(N):
                        mm = pe.matmul(ps[:, h % 2, lo:hi], wk[:, h], ckv[:, 0, lo:hi], start=True, stop=True)
                    mm.then_inc(keys, 1)
                for t in range(NT):
                    if t < 2:
                        pe.wait_ge(keys_read, QH - 1 + t)
                    else:
                        pe.wait_ge(values_read, 2 * (t - 1))
                    pe.matmul(ps[:, t % 2, 0:QH * HD], ckv[:, 0, t * P:(t + 1) * P], wv[:], start=True, stop=True)
                    pe.transpose(ps[:, t % 2, BANK:BANK + P], v_ch[:, t * P:(t + 1) * P],
                                 ident).then_inc(values, 1)

            @block.vector
            def _(dve):
                for h in range(QH):
                    dve.wait_ge(keys, h + 1)
                    dve.tensor_tensor(k_m[:, h], ps[:, h % 2, 0:N], kpe, ALU.add).then_inc(keys_read, 1)
                for t in range(NT):
                    dve.wait_ge(values, t + 1)
                    dve.tensor_copy(v_m[:, t], ps[:, t % 2, 0:QH * HD]).then_inc(values_read, 1)
                    dve.tensor_copy(v_a[:, t], ps[:, t % 2, BANK:BANK + P]).then_inc(values_read, 1)


def attention(nc, q_a, k_a, v_a, q_m, k_m, v_m, ident):
    heads = [("m", h, 0) for h in range(QH)] + [("a", i, r) for r in range(2) for i in range(4)]
    H = len(heads)
    groups = [(0, 4), (4, 8), (8, NT)]
    G = len(groups)
    with Phase(nc, "attn") as ph:
        qa = ph.sb("qa", [P, 4, P])
        qm = ph.sb("qm", [P, QH, P])
        probs = ph.sb("probs", [P, 2, N])
        turned = ph.sb("turned", [P, 2, NT, P])
        top = ph.sb("top", [P, 2])
        minus_top = ph.sb("minus_top", [P, 2])
        total = ph.sb("total", [P, 2])
        share = ph.sb("share", [P, 2])
        scores = ph.psum("scores", [P, 2, banked(N)])
        bank_a = ph.psum("bank_a", [P, BANK])
        bank_b = ph.psum("bank_b", [P, BANK])
        queries_a, queries_m, scored, topped, negated, exped, turned_up, copied_a, copied_v, weighed, shared, stored = (
            ph.sem(s) for s in ("queries_a", "queries_m", "scored", "topped", "negated", "exped", "turned_up", "copied_a",
                                "copied_v", "weighed", "shared", "stored"))

        def kind(n):
            return heads[n % H]

        def scale(n):
            return (HD if kind(n)[0] == "a" else HD + ROPE) ** -0.5

        with ph.block() as block:
            @block.gpsimd
            def _(pool):
                pool.tensor_copy(qm[:], q_m[:, :, 0:P]).then_inc(queries_m, 1)
                pool.tensor_copy(qa[:], q_a[:, :, 0:P]).then_inc(queries_a, 1)
                with pool.Fori(0, LT - 1) as t:
                    tokens = bass.ds(t * P + P, P)
                    pool.wait_ge(scored, t * H + QH)
                    pool.tensor_copy(qm[:], q_m[:, :, tokens]).then_inc(queries_m, 1)
                    pool.wait_ge(scored, t * H + H)
                    pool.tensor_copy(qa[:], q_a[:, :, tokens]).then_inc(queries_a, 1)

            @block.tensor
            def _(pe):
                pe.sem_inc(turned_up, 2 * G)
                pe.sem_inc(weighed, 2)

                def score(t, n, part):
                    which, i, r = kind(n)
                    if part == 0:
                        if n % H == 0:
                            pe.wait_ge(queries_m, t + (n // H + 1))
                        if n % H == QH:
                            pe.wait_ge(queries_a, t + 1)
                        pe.wait_ge(exped, t * H + (n + 1))
                    if which == "a":
                        rows, q, k = slice(64 * r, 64 * r + 64), qa[:, i], k_a
                    else:
                        rows, q, k = slice(0, HD + ROPE), qm[:, i], k_m[:, i]
                    lo, hi = segments(N)[part]
                    mm = pe.matmul(scores[:, n % 2, lo:hi], q[rows], k[rows, lo:hi], start=True, stop=True)
                    if part == G - 1:
                        mm.then_inc(scored, 1)

                def turn(t, n, g):
                    if g == 0:
                        pe.wait_ge(exped, t * H + (n + 3))
                        pe.wait_ge(copied_v, t * 2 * H + (2 * n + 2))
                    elif g == 1:
                        pe.wait_ge(stored, t * H + (n + 1))
                    else:
                        pe.wait_ge(copied_a, t * H + (n + 2))
                    bank = bank_b if g == 1 else bank_a
                    a, b = groups[g]
                    for k in range(a, b):
                        tr = pe.transpose(bank[:, (k - a) * P:(k - a + 1) * P], probs[:, n % 2, k * P:(k + 1) * P], ident)
                    tr.then_inc(turned_up, 1)

                def weigh(t, n):
                    which, i, r = kind(n)
                    v, col = (v_a, 64 * r) if which == "a" else (v_m, 64 * i)
                    pe.wait_ge(copied_v, t * 2 * H + (2 * n + 3))
                    for k in range(NT):
                        if k == groups[2][0]:
                            pe.wait_ge(copied_v, t * 2 * H + (2 * n + 4))
                        mm = pe.matmul(bank_b[:, 0:HD], turned[:, n % 2, k], v[:, k, col:col + HD],
                                       start=(k == 0), stop=(k == NT - 1))
                    mm.then_inc(weighed, 1)

                def tile(t, last):
                    for n in range(H):
                        for g in range(G):
                            turn(t, n, g)
                            if n + 2 < H or not last:
                                score(t, n + 2, g)
                        weigh(t, n)

                for n in range(2):
                    for g in range(G):
                        score(0, n, g)
                with pe.Fori(0, LT - 1) as t:
                    tile(t, False)
                tile(LT - 1, True)

            @block.vector
            def _(dve):
                dve.sem_inc(copied_v, 2)
                dve.sem_inc(stored, 1)
                dve.sem_inc(shared, 2)

                def maximum(t, n):
                    dve.wait_ge(scored, t * H + (n + 1))
                    dve.wait_ge(exped, t * H + (n + 1))
                    dve.reduce_max(top[:, n % 2:n % 2 + 1], scores[:, n % 2, 0:N],
                                   AX_X).then_inc(topped, 1)
                    dve.wait_ge(topped, t * H + (n + 1))
                    dve.tensor_scalar(minus_top[:, n % 2:n % 2 + 1], top[:, n % 2:n % 2 + 1], -scale(n), None,
                                      ALU.mult).then_inc(negated, 1)

                def tile(t, last):
                    for n in range(H):
                        if n + 1 < H or not last:
                            maximum(t, n + 1)
                        dve.wait_ge(exped, t * H + (n + 3))
                        dve.reciprocal(share[:, n % 2:n % 2 + 1], total[:, n % 2:n % 2 + 1]).then_inc(shared, 1)
                        for g in (1, 2):
                            a, b = groups[g]
                            bank = bank_b if g == 1 else bank_a
                            dve.wait_ge(turned_up, t * H * G + (n * G + g + 1 + 2 * G))
                            dve.tensor_copy(turned[:, n % 2, a:b], bank[:, 0:(b - a) * P]
                                            .rearrange("p (k c) -> p k c", c=P)).then_inc(copied_v, 1)
                        which, i, r = kind(n)
                        out = i + 4 * r if which == "a" else QH + i
                        dve.wait_ge(weighed, t * H + (n + 3))
                        dve.wait_ge(shared, t * H + (n + 3))
                        dve.tensor_scalar(q_m[:, out // 2, bass.ds(t * P + out % 2 * HD, HD)], bank_b[:, 0:HD],
                                          share[:, n % 2:n % 2 + 1], None, ALU.mult).then_inc(stored, 1)

                maximum(0, 0)
                with dve.Fori(0, LT - 1) as t:
                    tile(t, False)
                tile(LT - 1, True)

            @block.scalar
            def _(act):
                act.sem_inc(exped, 2)
                act.sem_inc(copied_a, 1)

                def soften(t, n):
                    act.wait_ge(negated, t * H + (n + 1))
                    act.wait_ge(turned_up, t * H * G + (n + 1) * G)
                    act.wait_ge(shared, t * H + (n + 1))
                    act.activation(probs[:, n % 2], scores[:, n % 2, 0:N], ACT.Exp,
                                   bias=minus_top[:, n % 2:n % 2 + 1], scale=scale(n),
                                   accum_out=total[:, n % 2:n % 2 + 1]).then_inc(exped, 1)

                def tile(t, last):
                    for n in range(H):
                        act.wait_ge(turned_up, t * H * G + (n * G + 1 + 2 * G))
                        act.wait_ge(weighed, t * H + (n + 1))
                        a, b = groups[0]
                        act.activation(turned[:, n % 2, a:b], bank_a[:, 0:(b - a) * P]
                                       .rearrange("p (k c) -> p k c", c=P), ACT.Copy).then_inc(copied_a, 1)
                        if n + 1 < H or not last:
                            soften(t, n + 1)

                soften(0, 0)
                with act.Fori(0, LT - 1) as t:
                    tile(t, False)
                tile(LT - 1, True)


def turn_and_gate(nc, tag, o, gate, out, ident):
    with Phase(nc, tag) as ph:
        ps = ph.psum("ps", [P, 2, L])
        turned, gated, used = (ph.sem(s) for s in ("turned", "gated", "used"))
        with ph.block() as block:
            @block.scalar
            def _(act):
                for c in range(DT):
                    act.activation(gate[:, c], gate[:, c], ACT.Silu).then_inc(gated, 1)

            @block.tensor
            def _(pe):
                for c in range(DT):
                    if c >= 2:
                        pe.wait_ge(used, c - 1)
                    for t in range(LT):
                        tr = pe.transpose(ps[:, c % 2, t * P:(t + 1) * P], o[:, c, t * P:(t + 1) * P], ident)
                    tr.then_inc(turned, 1)

            @block.vector
            def _(dve):
                for c in range(DT):
                    dve.wait_ge(turned, c + 1)
                    dve.wait_ge(gated, c + 1)
                    dve.tensor_tensor(out[:, c], ps[:, c % 2], gate[:, c], ALU.mult).then_inc(used, 1)


def project_residual(nc, tag, w, rhs, gate, x, x_in=None, x_out=None):
    with Phase(nc, tag) as ph:
        kt = w.shape[2]
        wbuf = ph.sb("wbuf", [P, 2, kt, P])
        ps = ph.psum("ps", [P, 2, L])
        loaded = [ph.sem(f"loaded{b}") for b in range(2)]
        x_here = [ph.sem(f"x_here{b}") for b in range(2)]
        multiplied, emptied, stored = ph.sem("multiplied"), ph.sem("emptied"), ph.sem("stored")
        with ph.block() as block:
            @block.sync
            def _(sp):
                load_weight_tiles(sp, w, wbuf, DT, loaded, multiplied)

            @block.scalar
            def _(act):
                if x_in is not None:
                    for part in range(2):
                        act.dma_start(x[:, part * 4:part * 4 + 4], x_in[:, part * 4:part * 4 + 4]).then_inc(x_here[part], 16)
                if x_out is not None:
                    for m in range(DT):
                        act.wait_ge(emptied, m + 3)
                        act.dma_start(x_out[:, m], x[:, m]).then_inc(stored, 16)
                    act.wait_ge(stored, 16 * DT)

            @block.tensor
            def _(pe):
                multiply_weight_tiles(pe, wbuf, ps, rhs, L, DT, loaded, multiplied, emptied)

            @block.vector
            def _(dve):
                for m in range(DT):
                    dve.wait_ge(multiplied, m + 3)
                    if x_in is not None and m % 4 == 0:
                        dve.wait_ge(x_here[m // 4], 16)
                    if gate is None:
                        ins = dve.tensor_tensor(x[:, m], ps[:, m % 2], x[:, m], ALU.add)
                    else:
                        ins = dve.scalar_tensor_tensor(x[:, m], ps[:, m % 2], gate[:, m:m + 1], x[:, m],
                                                       ALU.mult, ALU.add)
                    ins.then_inc(emptied, 1)


def attention_layer(nc, A, x_out, mod, one_plus, K):
    ones, halves, ident, swap_a, swap_m = (K[:, i] for i in range(5))
    with ExitStack() as ctx:
        def sb(name, shape):
            return ctx.enter_context(nc.sbuf_tensor(name, shape, F32))
        lat = sb("a_lat", [P, 14, L])
        both = sb("a_both", [P, 4, N])
        with ExitStack() as inner:
            x = inner.enter_context(nc.sbuf_tensor("a_x", [P, DT, L], F32))
            h = inner.enter_context(nc.sbuf_tensor("a_h", [P, DT, N], F32))
            load(nc, "a_ctx", [(x[:], A["x"]), (h[:, :, L:N], A["ctx"])])
            rms_norm(nc, "an0", x, h[:, :, 0:L], 1, DT, D, ones, one_plus[:, 0, 0], mod[:, 0:DT, 0], L)
            rms_norm(nc, "an1", h[:, :, L:N], h[:, :, L:N], 1, DT, D, ones, one_plus[:, 0, 1], mod[:, 0:DT, 1], C)
            project(nc, "ap0", A["attn_w_lat"], h, lat, 14, L)
            project(nc, "ap1", A["attn_w_both"], h, both, 4, N)
        ctx2 = ctx.enter_context(ExitStack())
        q_m = ctx2.enter_context(nc.sbuf_tensor("a_qm", [P, QH, L], F32))
        with ExitStack() as inner:
            small = inner.enter_context(nc.sbuf_tensor("a_small", [P, 8], F32))
            cos = inner.enter_context(nc.sbuf_tensor("a_cos", [P, N], F32))
            sin = inner.enter_context(nc.sbuf_tensor("a_sin", [P, N], F32))
            load(nc, "a_load", [(small[:], A["attn_small"]), (cos[:], A["rope"][0]), (sin[:], A["rope"][1])])
            rms_norm(nc, "an2", lat[:, 0:4], lat[:, 0:4], 4, 1, HD, halves, small[:, 0:4], None, L)
            rms_norm(nc, "an3", both[:, 0:1], both[:, 0:1], 1, 1, HD, halves, small[:, 4:5], None, N)
            rms_norm(nc, "an4", lat[:, 4:6], lat[:, 4:6], 1, 2, 256, ones, small[:, 5:7], None, L)
            rms_norm(nc, "an5", both[:, 1:2], both[:, 1:2], 1, 1, 128, ones, small[:, 7:8], None, N)
            rotate(nc, "ar0", lat[:, 0:4], 4, swap_a, cos, sin, L)
            rotate(nc, "ar1", both[:, 0:1], 1, swap_a, cos, sin, N)
            project(nc, "ap2", A["mla_w_uq"], lat[:, 4:6], q_m, QH, L)
            load(nc, "a_load2", [(cos[:], A["rope"][2]), (sin[:], A["rope"][3])])
            rotate(nc, "ar2", q_m, QH, swap_m, cos, sin, L)
            rotate(nc, "ar3", both[:, 2:3], 1, swap_m, cos, sin, N)
        k_m = ctx2.enter_context(nc.sbuf_tensor("a_km", [P, QH, N], F32))
        v_m = ctx2.enter_context(nc.sbuf_tensor("a_vm", [P, NT, QH * HD], F32))
        v_a = ctx2.enter_context(nc.sbuf_tensor("a_va", [P, NT, P], F32))
        mla_keys_values(nc, A, both[:, 1:2], both[:, 2], k_m, v_m, both[:, 3], v_a, ident)
        attention(nc, lat[:, 0:4], both[:, 0], v_a, q_m, k_m, v_m, ident)
        turn_and_gate(nc, "a_gate", q_m, lat[:, 6:14], lat[:, 6:14], ident)
        ctx2.close()
        x = sb("a_x2", [P, DT, L])
        project_residual(nc, "a_out", A["attn_w_out"], lat[:, 6:14], mod[:, 2 * DT:3 * DT, 0], x, A["x"], x_out)


def spread(ap, shape):
    return ap.broadcast_to(shape)


PAIRS = 4
FFN = 64
EMB = 33


def filter_network(nc, A, hid):
    ROUND = 1.5 * 2.0 ** 23
    HIGH = 6.28125
    LOW = 2 * math.pi - HIGH
    with Phase(nc, "filter_net") as ph:
        emb, w1, w2, small = ph.sb("emb", [EMB, L]), ph.sb("w1", [EMB, FFN]), ph.sb("w2", [FFN, FFN]), ph.sb("small", [FFN, 3])
        arg, turns, first = ph.sb("arg", [FFN, L]), ph.sb("turns", [FFN, L]), ph.sb("first", [FFN, L])
        ps = ph.psum("ps", [P, 2, L])
        landed, multiplied, step, reduced, sined = (
            ph.sem(s) for s in ("landed", "multiplied", "step", "reduced", "sined"))
        with ph.block() as block:
            @block.sync
            def _(sp):
                for dst, src in ((emb, A["hy_emb"]), (w1, A["hy_w1"]), (w2, A["hy_w2"]), (small, A["hy_small"])):
                    sp.dma_start(dst[:], src).then_inc(landed, 16)

            @block.tensor
            def _(pe):
                pe.wait_ge(landed, 64)
                for lo, hi in segments(L):
                    mm = pe.matmul(ps[0:FFN, 0, lo:hi], w1[:], emb[:, lo:hi], start=True, stop=True)
                mm.then_inc(multiplied, 1)
                pe.wait_ge(sined, 1)
                for lo, hi in segments(L):
                    mm = pe.matmul(ps[0:FFN, 1, lo:hi], w2[:], first[:, lo:hi], start=True, stop=True)
                mm.then_inc(multiplied, 1)

            @block.vector
            def _(dve):
                count = [0]
                dve.wait_ge(landed, 64)
                dve.memset(hid[FFN:FFN + 1, :], 1.0)
                for layer in range(2):
                    dve.wait_ge(multiplied, layer + 1)
                    if layer:
                        dve.wait_ge(sined, 1)
                    chained(dve, dve.tensor_scalar(arg[:], ps[0:FFN, layer], small[:, layer:layer + 1], small[:, 2:3],
                                                   ALU.add, ALU.mult), step, count)
                    chained(dve, dve.tensor_scalar(turns[:], arg[:], 1 / (2 * math.pi), ROUND, ALU.mult, ALU.add),
                            step, count)
                    chained(dve, dve.tensor_scalar(turns[:], turns[:], ROUND, None, ALU.subtract), step, count)
                    chained(dve, dve.scalar_tensor_tensor(arg[:], turns[:], -HIGH, arg[:], ALU.mult, ALU.add),
                            step, count)
                    chained(dve, dve.scalar_tensor_tensor(arg[:], turns[:], -LOW, arg[:], ALU.mult, ALU.add),
                            step, count)
                    dve.tensor_scalar(arg[:], arg[:], 3.1415925, -3.1415925, ALU.min, ALU.max).then_inc(reduced, 1)

            @block.scalar
            def _(act):
                act.wait_ge(reduced, 1)
                act.activation(first[:], arg[:], ACT.Sin).then_inc(sined, 1)
                act.wait_ge(reduced, 2)
                act.activation(hid[0:FFN, :], arg[:], ACT.Sin).then_inc(sined, 1)


def filter_taps(nc, A, hid, order, plus, minus, inverse, ones):
    with Phase(nc, f"taps{order}") as ph:
        w3 = ph.sb("w3", [FFN + 1, 2, D])
        decay = ph.sb("decay", [P, 2, D])
        fwd, bwd = ph.sb("fwd", [P, 2, D]), ph.sb("bwd", [P, 2, D])
        mag = ph.sb("mag", [P, 2, D])
        size = ph.sb("size", [P, D])
        magnitudes = ph.sem("magnitudes")
        ps = ph.psum("ps", [P, 2, 2, D])
        landed, made, decayed, sized, combined, total, scaled = (
            ph.sem(s) for s in ("landed", "made", "decayed", "sized", "combined", "total", "scaled"))
        table = [ph.sem(f"table{b}") for b in range(2)]
        with ph.block() as block:
            @block.sync
            def _(sp):
                sp.dma_start(w3[:], A["hy_w3"][order]).then_inc(landed, 16)
                for t in range(LT):
                    if t >= 2:
                        sp.wait_ge(decayed, 2 * (t - 1))
                    sp.dma_start(decay[:, t % 2], A["hy_decay"][t]).then_inc(table[t % 2], 16)

            @block.tensor
            def _(pe):
                pe.wait_ge(landed, 16)
                for t in range(LT):
                    if t >= 2:
                        pe.wait_ge(decayed, 2 * (t - 1))
                    for way in range(2):
                        for lo, hi in segments(D):
                            mm = pe.matmul(ps[:, t % 2, way, lo:hi], hid[:, t * P:(t + 1) * P], w3[:, way, lo:hi],
                                           start=True, stop=True)
                    mm.then_inc(made, 1)
                pe.wait_ge(decayed, 2 * LT)
                pe.wait_ge(sized, 2 * LT + 1)
                for lo, hi in segments(D):
                    mm = pe.matmul(ps[:, 0, 0, lo:hi], ones, size[:, lo:hi], start=True, stop=True)
                mm.then_inc(total, 1)

            @block.vector
            def _(dve):
                dve.memset(size[:], 0.0).then_inc(sized, 1)
                for t in range(LT):
                    dve.wait_ge(made, t + 1)
                    dve.wait_ge(table[t % 2], 16 * (t // 2 + 1))
                    if t >= 2:
                        dve.wait_ge(magnitudes, 2 * (t - 1))
                        dve.wait_ge(combined, 2 * (t - 1))
                    dve.tensor_tensor(fwd[:, t % 2], ps[:, t % 2, 0], decay[:, t % 2], ALU.mult).then_inc(decayed, 1)
                    dve.tensor_tensor(bwd[:, t % 2], ps[:, t % 2, 1], decay[:, t % 2], ALU.mult).then_inc(decayed, 1)
                    dve.wait_ge(decayed, 2 * t + 2)
                    if t == 0:
                        dve.memset(bwd[0:1, 0], 0.0).then_inc(scaled, 1)
                        dve.wait_ge(scaled, 1)
                    for way in range(2):
                        dve.wait_ge(magnitudes, 2 * t + way + 1)
                        dve.wait_ge(sized, 2 * t + way + 1)
                        dve.tensor_tensor(size[:], size[:], mag[:, way], ALU.add).then_inc(sized, 1)
                dve.wait_ge(total, 1)
                dve.tensor_scalar(inverse[:], ps[:, 0, 0], float(L), None, ALU.mult).then_inc(scaled, 1)
                dve.wait_ge(scaled, 2)
                dve.reciprocal(inverse[:], inverse[:])

            @block.scalar
            def _(act):
                for t in range(LT):
                    act.wait_ge(decayed, 2 * t + 2)
                    act.wait_ge(scaled, 1)
                    for way, tap in enumerate((fwd, bwd)):
                        if t:
                            act.wait_ge(sized, 2 * t + way)
                        act.activation(mag[:, way], tap[:, t % 2], ACT.Abs).then_inc(magnitudes, 1)

            @block.gpsimd
            def _(pool):
                pool.wait_ge(scaled, 1)
                for t in range(LT):
                    pool.wait_ge(decayed, 2 * t + 2)
                    pool.tensor_tensor(plus[:, t], fwd[:, t % 2], bwd[:, t % 2], ALU.add).then_inc(combined, 1)
                    pool.tensor_tensor(minus[:, t], fwd[:, t % 2], bwd[:, t % 2], ALU.subtract).then_inc(combined, 1)


def transform(pe, wbuf, ps, first, second, loaded, multiplied, emptied):
    pe.sem_inc(multiplied, 2)
    pe.sem_inc(emptied, 2)
    with pe.Fori(0, PAIRS // 2) as f2:
        for b in range(2):
            pe.wait_ge(loaded[b], f2 * 16 + 16)
            for half in range(2):
                pe.wait_ge(emptied, f2 * 4 + (2 * b + half + 1))
                for part in range(4):
                    rhs = (first, second)[part // 2]
                    for k in range(4):
                        mm = pe.matmul(ps[:, half, part], wbuf[:, b, part * 4 + k],
                                       rhs[:, (part % 2) * 4 + k, half * BANK:(half + 1) * BANK],
                                       start=(k == 0), stop=(k == 3))
                mm.then_inc(multiplied, 1)


def load_tables(sp, tables, wbuf, loaded, multiplied):
    with sp.Fori(0, PAIRS // 2) as f2:
        for b in range(2):
            sp.wait_ge(multiplied, f2 * 4 + (2 * b)) if b else sp.wait_ge(multiplied, f2 * 4 + 1)
            sp.dma_start(wbuf[:, b], tables[f2 * 2 + b]).then_inc(loaded[b], 16)


def filter_spectrum(nc, A, order, plus, minus, inverse):
    with Phase(nc, f"spec{order}") as ph:
        wbuf = ph.sb("wbuf", [P, 2, 4 * 4, P])
        skip = ph.sb("skip", [P, D])
        odd_lags = ph.sb("odd_lags", [P, 2, 2, BANK])
        out = ph.sb("out", [P, 2, 4, BANK])
        ps = ph.psum("ps", [P, 2, 4, BANK])
        loaded = [ph.sem(f"loaded{b}") for b in range(2)]
        stored = [ph.sem(f"stored{b}") for b in range(2)]
        multiplied, emptied, landed, finished, step, copied, ready = (
            ph.sem(s) for s in ("multiplied", "emptied", "landed", "finished", "step", "copied", "ready"))
        with ph.block() as block:
            @block.sync
            def _(sp):
                sp.dma_start(skip[:], A["hy_skip"][order]).then_inc(landed, 16)
                load_tables(sp, A["hy_lag_tables"], wbuf, loaded, multiplied)

            @block.tensor
            def _(pe):
                transform(pe, wbuf, ps, plus, minus, loaded, multiplied, emptied)

            @block.scalar
            def _(act):
                for n in range(2 * PAIRS):
                    act.wait_ge(multiplied, n + 3)
                    if n >= 2:
                        act.wait_ge(emptied, n + 1)
                    act.activation(odd_lags[:, n % 2], ps[:, n % 2, 1::2], ACT.Copy).then_inc(copied, 1)
                    if n >= 1:
                        act.wait_ge(finished, n)
                        act.dma_start(A["spectrum"][order * 2 * PAIRS + n - 1], out[:, (n - 1) % 2])\
                           .then_inc(stored[(n - 1) % 2], 16)
                act.wait_ge(finished, 2 * PAIRS)
                act.dma_start(A["spectrum"][(order + 1) * 2 * PAIRS - 1], out[:, 1]).then_inc(stored[1], 16)
                for b in range(2):
                    act.wait_ge(stored[b], 16 * PAIRS)

            @block.vector
            def _(dve):
                dve.wait_ge(landed, 16)
                dve.tensor_scalar(skip[:], skip[:], 1.0 / L, None, ALU.mult).then_inc(ready, 1)
                dve.wait_ge(ready, 1)
                for n in range(2 * PAIRS):
                    b, ch = n % 2, slice((n % 2) * BANK, (n % 2 + 1) * BANK)
                    dve.wait_ge(copied, n + 1)
                    if n >= 2:
                        dve.wait_ge(stored[b], 16 * (n // 2))
                    cos_odd, sin_odd = odd_lags[:, b, 0], odd_lags[:, b, 1]
                    dve.tensor_tensor(out[:, b, 0], ps[:, b, 0], cos_odd, ALU.add)
                    dve.tensor_tensor(out[:, b, 1], ps[:, b, 0], cos_odd, ALU.subtract)
                    dve.tensor_tensor(out[:, b, 2], sin_odd, ps[:, b, 2], ALU.add)
                    dve.tensor_tensor(out[:, b, 3], sin_odd, ps[:, b, 2], ALU.subtract).then_inc(emptied, 1)
                    dve.wait_ge(emptied, n + 3)
                    dve.tensor_tensor(out[:, b], out[:, b], spread(inverse[:, ch].unsqueeze(1), [P, 4, BANK]),
                                      ALU.mult).then_inc(step, 1)
                    dve.wait_ge(step, n + 1)
                    dve.tensor_tensor(out[:, b, 0:2], out[:, b, 0:2], spread(skip[:, ch].unsqueeze(1), [P, 2, BANK]),
                                      ALU.add).then_inc(finished, 1)


def hyena_filters(nc, A, ones):
    with ExitStack() as ctx:
        hid = ctx.enter_context(nc.sbuf_tensor("hy_hid", [FFN + 1, L], F32))
        plus = ctx.enter_context(nc.sbuf_tensor("hy_plus", [P, LT, D], F32))
        minus = ctx.enter_context(nc.sbuf_tensor("hy_minus", [P, LT, D], F32))
        inverse = ctx.enter_context(nc.sbuf_tensor("hy_inverse", [P, D], F32))
        filter_network(nc, A, hid)
        for order in range(2):
            filter_taps(nc, A, hid, order, plus, minus, inverse, ones)
            filter_spectrum(nc, A, order, plus, minus, inverse)


def project_conv(nc, tag, w, rhs, out, tiles, taps, first, before, after, func):
    width = before + 1 + after
    with Phase(nc, tag) as ph:
        kt = w.shape[2]
        wbuf = ph.sb("wbuf", [P, 2, kt, P])
        raw = ph.sb("raw", [P, 2, before + L + after])
        ps = ph.psum("ps", [P, 2, L])
        loaded = [ph.sem(f"loaded{b}") for b in range(2)]
        multiplied, emptied, padded, step, convolved = (
            ph.sem(s) for s in ("multiplied", "emptied", "padded", "step", "convolved"))
        with ph.block() as block:
            @block.sync
            def _(sp):
                load_weight_tiles(sp, w, wbuf, tiles, loaded, multiplied)

            @block.tensor
            def _(pe):
                multiply_weight_tiles(pe, wbuf, ps, rhs, L, tiles, loaded, multiplied, emptied)

            @block.scalar
            def _(act):
                act.wait_ge(padded, 1)
                for m in range(tiles):
                    act.wait_ge(multiplied, m + 3)
                    if m >= 2:
                        act.wait_ge(step, width * (m - 1))
                    act.activation(raw[:, m % 2, before:before + L], ps[:, m % 2], ACT.Copy).then_inc(emptied, 1)
                    if func is not None and m >= 1:
                        act.wait_ge(step, width * m)
                        act.activation(out[:, m - 1], out[:, m - 1], func)
                if func is not None:
                    act.wait_ge(step, width * tiles)
                    act.activation(out[:, tiles - 1], out[:, tiles - 1], func)

            @block.vector
            def _(dve):
                dve.memset(raw[:], 0.0).then_inc(padded, 1)
                for m in range(tiles):
                    t = taps[:, first + m]
                    dve.wait_ge(emptied, m + 3)
                    dve.tensor_scalar(out[:, m], raw[:, m % 2, 0:L], t[:, 0:1], t[:, width:width + 1],
                                      ALU.mult, ALU.add).then_inc(step, 1)
                    for j in range(1, width):
                        dve.wait_ge(step, width * m + j)
                        dve.scalar_tensor_tensor(out[:, m], raw[:, m % 2, j:j + L], t[:, j:j + 1], out[:, m],
                                                 ALU.mult, ALU.add).then_inc(step, 1)


def turn_tiles(nc, tag, src, dst, ident, keep=None):
    with Phase(nc, tag) as ph:
        ps = ph.psum("ps", [P, 2, L])
        turned, used, kept = ph.sem("turned"), ph.sem("used"), ph.sem("kept")
        with ph.block() as block:
            if keep is not None:
                @block.sync
                def _(sp):
                    for t in range(LT):
                        sp.wait_ge(used, t + 1)
                        sp.dma_start(keep[t], dst[:, t]).then_inc(kept, 16)
                    sp.wait_ge(kept, 16 * LT)

            @block.tensor
            def _(pe):
                for t in range(LT):
                    if t >= 2:
                        pe.wait_ge(used, t - 1)
                    first = t // 4 + 2 * P * (t % 4)
                    for c in range(DT):
                        tr = pe.transpose(ps[:, t % 2, c * P:(c + 1) * P], src[:, c, first:first + 2 * P - 1:2], ident)
                    tr.then_inc(turned, 1)

            @block.vector
            def _(dve):
                for t in range(LT):
                    dve.wait_ge(turned, t + 1)
                    dve.tensor_copy(dst[:, t], ps[:, t % 2]).then_inc(used, 1)


def turn_back(nc, tag, src, out, ident):
    with Phase(nc, tag) as ph:
        ps = ph.psum("ps", [P, 2, L])
        turned, used = ph.sem("turned"), ph.sem("used")
        with ph.block() as block:
            @block.tensor
            def _(pe):
                for c in range(DT):
                    if c >= 2:
                        pe.wait_ge(used, c - 1)
                    for t in range(LT):
                        tr = pe.transpose(ps[:, c % 2, t * P:(t + 1) * P], src[:, t, c * P:(c + 1) * P], ident)
                    tr.then_inc(turned, 1)

            @block.vector
            def _(dve):
                for c in range(DT):
                    by_parity = out[:, c].rearrange("p (n two) -> p two n", two=2)
                    dve.wait_ge(turned, c + 1)
                    dve.tensor_tensor(by_parity, ps[:, c % 2].rearrange("p (two n) -> p two n", two=2), by_parity,
                                      ALU.mult).then_inc(used, 1)


def long_conv(nc, A, order, z, spec, factor):
    with Phase(nc, f"fwd{order}") as ph:
        wbuf = ph.sb("wbuf", [P, 2, 4 * 4, P])
        filt = ph.sb("filt", [P, 2, 4, BANK])
        odd_tok = ph.sb("odd_tok", [P, 2, 2, BANK])
        sig = ph.sb("sig", [P, 4, BANK])
        prod = ph.sb("prod", [P, 4, BANK])
        res = ph.sb("res", [P, 2, 4, BANK])
        ps = ph.psum("ps", [P, 2, 4, BANK])
        loaded = [ph.sem(f"loaded{b}") for b in range(2)]
        filt_in = [ph.sem(f"filt_in{b}") for b in range(2)]
        multiplied, emptied, step, copied, filtered, folded = (
            ph.sem(s) for s in ("multiplied", "emptied", "step", "copied", "filtered", "folded"))
        with ph.block() as block:
            @block.sync
            def _(sp):
                load_tables(sp, A["hy_tables"], wbuf, loaded, multiplied)

            @block.tensor
            def _(pe):
                transform(pe, wbuf, ps, z, z, loaded, multiplied, emptied)

            @block.scalar
            def _(act):
                for n in range(2 * PAIRS):
                    if n >= 2:
                        act.wait_ge(filtered, n - 1)
                    act.dma_start(filt[:, n % 2], A["spectrum"][order * 2 * PAIRS + n]).then_inc(filt_in[n % 2], 16)
                    act.wait_ge(multiplied, n + 3)
                    if n >= 2:
                        act.wait_ge(emptied, n + 1)
                    act.activation(odd_tok[:, n % 2], ps[:, n % 2, 1::2], ACT.Copy).then_inc(copied, 1)

            @block.vector
            def _(dve):
                for n in range(2 * PAIRS):
                    b = n % 2
                    dve.wait_ge(copied, n + 1)
                    dve.tensor_tensor(sig[:, 0:2], ps[:, b, 0::2], odd_tok[:, b], ALU.add).then_inc(step, 1)
                    dve.tensor_tensor(sig[:, 3], ps[:, b, 0], odd_tok[:, b, 0], ALU.subtract).then_inc(step, 1)
                    dve.tensor_tensor(sig[:, 2], ps[:, b, 2], odd_tok[:, b, 1], ALU.subtract).then_inc(emptied, 1)
                    dve.wait_ge(emptied, n + 3)
                    dve.wait_ge(step, 6 * n + 2)
                    dve.wait_ge(filt_in[b], 16 * (n // 2 + 1))
                    if n >= 2:
                        dve.wait_ge(folded, 4 * (n - 1))
                    dve.tensor_tensor(prod[:, 0:2], sig[:, 2:4], filt[:, b, 2:4], ALU.mult).then_inc(step, 1)
                    dve.tensor_tensor(prod[:, 2:4], sig[:, 2:4], filt[:, b, 0:2], ALU.mult).then_inc(step, 1)
                    dve.tensor_tensor(res[:, b, 0:2], sig[:, 0:2], filt[:, b, 0:2], ALU.mult).then_inc(step, 1)
                    dve.tensor_tensor(res[:, b, 2:4], sig[:, 0:2], filt[:, b, 2:4], ALU.mult).then_inc(step, 1)
                    dve.wait_ge(step, 6 * n + 6)
                    dve.tensor_tensor(res[:, b, 0:2], res[:, b, 0:2], prod[:, 0:2], ALU.subtract)
                    dve.tensor_tensor(res[:, b, 2:4], res[:, b, 2:4], prod[:, 2:4], ALU.add).then_inc(filtered, 1)

            @block.gpsimd
            def _(pool):
                for n in range(2 * PAIRS):
                    b, f, ch = n % 2, n // 2, slice((n % 2) * BANK, (n % 2 + 1) * BANK)
                    pool.wait_ge(filtered, n + 1)
                    for j in range(2):
                        for sign, op in enumerate((ALU.add, ALU.subtract)):
                            pool.tensor_tensor(spec[:, sign, f + 4 * j, ch], res[:, b, j], res[:, b, 3 - j],
                                               op).then_inc(folded, 1)
    for parity in range(2):
        with Phase(nc, f"inv{order}{parity}") as ph:
            tiles = slice(4 * parity, 4 * parity + 4)
            wbuf = ph.sb("wbuf", [P, 2, LT, P])
            times = ph.sb("times", [P, 2, D])
            ps = ph.psum("ps", [P, 2, D])
            loaded = [ph.sem(f"loaded{b}") for b in range(2)]
            times_in = [ph.sem(f"times_in{b}") for b in range(2)]
            multiplied, emptied = (ph.sem(s) for s in ("multiplied", "emptied"))
            with ph.block() as block:
                @block.sync
                def _(sp):
                    load_weight_tiles(sp, A["hy_back_tables"][tiles], wbuf, 4, loaded, multiplied)

                @block.tensor
                def _(pe):
                    multiply_weight_tiles(pe, wbuf, ps, spec[:, parity], D, 4, loaded, multiplied, emptied)

                if factor is not None:
                    @block.scalar
                    def _(act):
                        for t in range(4):
                            act.wait_ge(emptied, t + 1)
                            act.dma_start(times[:, t % 2], factor[4 * parity + t]).then_inc(times_in[t % 2], 16)

                @block.vector
                def _(dve):
                    for t in range(4):
                        at = 4 * parity + t
                        dve.wait_ge(multiplied, t + 3)
                        if factor is None:
                            dve.tensor_copy(z[:, at], ps[:, t % 2]).then_inc(emptied, 1)
                        else:
                            dve.wait_ge(times_in[t % 2], 16 * (t // 2 + 1))
                            dve.tensor_tensor(z[:, at], ps[:, t % 2], times[:, t % 2], ALU.mult).then_inc(emptied, 1)


def multiply(nc, tag, out, a, b, tiles):
    with Phase(nc, tag) as ph:
        with ph.block() as block:
            @block.vector
            def _(dve):
                for t in range(tiles):
                    dve.tensor_tensor(out[:, t], a[:, t], b[:, t], ALU.mult)


def hyena_layer(nc, A, x_in, x_out, mod, one_plus, K):
    ones, ident = K[:, 0], K[:, 2]
    hyena_filters(nc, A, ones)
    with ExitStack() as ctx:
        def sb(name, shape):
            return ctx.enter_context(nc.sbuf_tensor(name, shape, F32))
        last = sb("hy_last", [P, DT, L])
        final_w = sb("hy_final_w", [P, DT])
        with ExitStack() as mid:
            z = mid.enter_context(nc.sbuf_tensor("hy_z", [P, LT, D], F32))
            with ExitStack() as inner:
                u = inner.enter_context(nc.sbuf_tensor("hy_u", [P, DT, L], F32))
                part1 = inner.enter_context(nc.sbuf_tensor("hy_part1", [P, LT, D], F32))
                h = inner.enter_context(nc.sbuf_tensor("hy_h", [P, DT, L], F32))
                taps = inner.enter_context(nc.sbuf_tensor("hy_taps", [P, 24, 4], F32))
                load(nc, "hy_load", [(u[:], x_in), (taps[:], A["hy_taps"]), (final_w[:], A["final_norm_w"])])
                rms_norm(nc, "hy_n", u, h, 1, DT, D, ones, one_plus[:, 1, 0], mod[:, 3 * DT:4 * DT, 0], L)
                w = A["hy_w_in"]
                project_conv(nc, "hy_c0", w[0:8], h, u, DT, taps, 0, 1, 1, None)
                turn_tiles(nc, "hy_t0", u, z, ident)
                project_conv(nc, "hy_c1", w[8:16], h, u, DT, taps, 8, 1, 1, None)
                turn_tiles(nc, "hy_t1", u, part1, ident, A["factor"])
                project_conv(nc, "hy_c2", w[16:24], h, u, DT, taps, 16, 1, 1, None)
                project(nc, "hy_g", w[24:32], h, last, DT, L, ACT.Silu)
                multiply(nc, "hy_m", last, last, u, DT)
            spec = mid.enter_context(nc.sbuf_tensor("hy_spec", [P, 2, DT, D], F32))
            long_conv(nc, A, 0, z, spec, A["factor"])
            long_conv(nc, A, 1, z, spec, None)
            turn_back(nc, "hy_t2", z, last, ident)
        x = sb("hy_x", [P, DT, L])
        project_residual(nc, "hy_out", A["hy_w_out"], last, mod[:, 5 * DT:6 * DT, 0], x, x_in)
        rms_norm(nc, "hy_fn", x, x, 1, DT, D, ones, final_w, None, L)
        store(nc, "hy_store", x_out, x)


KEY = 128
LEVELS = 7
SH = 8


def gated_tile(nc, tag, q, k, log_f, values, outs, scratch, masks, ident):
    H = len(values)
    rows = [slice(h * (P // H), (h + 1) * (P // H)) for h in range(H)]
    units = [(n, h) for n in range(LEVELS + 1) for h in range(H)]
    with Phase(nc, tag) as ph:
        cum = ph.sb("cum", [P, L])
        keep = ph.sb("keep", [P, LT, P])
        edge = ph.sb("edge", [P, 2, L])
        near_q, near_k = scratch[:, 0:2], scratch[:, 2:4]
        score = ph.sb("score", [P, H, L])
        spare = ph.sb("spare", [P, L])
        masked_part = [spare, keep[:].rearrange("p c t -> p (c t)")]
        key_tok = ph.sb("key_tok", [P, LT, P])
        state = ph.sb("state", [P, LT, P])
        ps = ph.psum("ps", [P, 2, L])
        ps_a = ph.psum("ps_a", [P, L])
        ps_b = ph.psum("ps_b", [P, L])
        cleared, setup, summed, edges, exped, factored, products, masked, added, turned, copied, updates, states, out_ready, out_copied = (
            ph.sem(s) for s in ("cleared", "setup", "summed", "edges", "exped", "factored", "products", "masked", "added", "turned",
                                "copied", "updates", "states", "out_ready", "out_copied"))

        def halves(ap, level):
            half = 2 ** level
            a = ap.rearrange("p (b s) -> p b s", s=2 * half)
            mid = a[:, :, half - 1:half]
            return a[:, :, 0:half], a[:, :, half:2 * half], spread(mid, [P, L // (2 * half), half])

        with ph.block() as block:
            @block.vector
            def _(dve):
                dve.memset(keep[:], 1.0).then_inc(setup, 1)
                dve.memset(state[:, 0], 0.0).then_inc(setup, 1)
                dve.wait_ge(setup, 2)
                dve.memset(keep[:, :, 0:1], 0.0).then_inc(setup, 1)
                dve.wait_ge(setup, 3)
                dve.tensor_tensor_scan(cum[:], keep[:].rearrange("p c t -> p (c t)"), log_f, 0.0, ALU.mult,
                                       ALU.add).then_inc(summed, 1)
                dve.wait_ge(summed, 1)

                def exponents(level):
                    b_left, b_right, mid = halves(cum[:], level)
                    left, right, _ = halves(edge[:, level % 2], level)
                    if level >= 2:
                        dve.wait_ge(factored, 2 * (level - 1))
                    dve.tensor_tensor(right, b_right, mid, ALU.subtract).then_inc(edges, 1)
                    dve.tensor_tensor(left, mid, b_left, ALU.subtract).then_inc(edges, 1)

                def factors(level):
                    left, right, _ = halves(edge[:, level % 2], level)
                    q_right, k_left = halves(q, level)[1], halves(k, level)[0]
                    if level >= 2:
                        dve.wait_ge(products, H * (level - 2 + 2))
                    else:
                        dve.wait_ge(cleared, 2 * level + 2)
                    dve.wait_ge(exped, level + 1)
                    dve.tensor_tensor(halves(near_q[:, level % 2], level)[1], q_right, right, ALU.mult).then_inc(factored, 1)
                    dve.tensor_tensor(halves(near_k[:, level % 2], level)[0], k_left, left, ALU.mult).then_inc(factored, 1)

                def accumulate(u):
                    n, h = units[u]
                    mask = spread(masks[:, n].unsqueeze(1), [P, LT, P])
                    part = ps[:, u % 2].rearrange("p (c t) -> p c t", t=P)
                    dve.wait_ge(products, u + 1)
                    if n == 0:
                        dve.tensor_tensor(score[:, h].rearrange("p (c t) -> p c t", t=P), part, mask,
                                          ALU.mult).then_inc(masked, 1)
                    else:
                        if u - H >= 2:
                            dve.wait_ge(added, u - H - 1)
                        dve.tensor_tensor(masked_part[u % 2][:].rearrange("p (c t) -> p c t", t=P), part, mask,
                                          ALU.mult).then_inc(masked, 1)

                exponents(0)
                for level in range(LEVELS):
                    if level + 1 < LEVELS:
                        exponents(level + 1)
                    factors(level)
                    for h in range(H):
                        accumulate(level * H + h)
                chunks = cum[:].rearrange("p (c t) -> p c t", t=P)
                last = spread(chunks[:, :, P - 1:P], [P, LT, P])
                dve.wait_ge(factored, 2 * LEVELS)
                dve.wait_ge(products, H * (LEVELS - 1))
                dve.tensor_tensor(edge[:, 1].rearrange("p (c t) -> p c t", t=P), last, chunks, ALU.subtract).then_inc(edges, 1)
                dve.wait_ge(exped, LEVELS + 2)
                dve.tensor_tensor(near_k[:, 1], k, edge[:, 1], ALU.mult).then_inc(factored, 1)
                dve.tensor_tensor(near_q[:, 1], q, edge[:, 0], ALU.mult).then_inc(factored, 1)
                for h in range(H):
                    accumulate(LEVELS * H + h)
                dve.wait_ge(updates, 1)
                for c in range(LT - 1):
                    if c:
                        dve.wait_ge(states, c)
                    dve.scalar_tensor_tensor(state[:, c + 1], state[:, c], edge[:, 0, (c + 1) * P - 1:(c + 1) * P],
                                             ps_b[:, c * P:(c + 1) * P], ALU.mult, ALU.add).then_inc(states, 1)

            @block.gpsimd
            def _(pool):
                for level in range(2):
                    pool.memset(near_q[:, level], 0.0).then_inc(cleared, 1)
                    pool.memset(near_k[:, level], 0.0).then_inc(cleared, 1)
                for u in range(H, len(units)):
                    pool.wait_ge(masked, u + 1)
                    if u >= 2 * H:
                        pool.wait_ge(added, u - 2 * H + 1)
                    score_h = score[:, units[u][1]]
                    pool.tensor_tensor(score_h, score_h, masked_part[u % 2][:], ALU.add).then_inc(added, 1)

            @block.scalar
            def _(act):
                for level in range(LEVELS):
                    act.wait_ge(edges, 2 * (level + 1))
                    act.activation(edge[:, level % 2], edge[:, level % 2], ACT.Exp).then_inc(exped, 1)
                act.wait_ge(factored, 2 * LEVELS)
                act.activation(edge[:, 0], cum[:], ACT.Exp).then_inc(exped, 1)
                act.wait_ge(edges, 2 * LEVELS + 1)
                act.activation(edge[:, 1], edge[:, 1], ACT.Exp).then_inc(exped, 1)
                act.wait_ge(turned, 1)
                act.activation(key_tok[:].rearrange("p c t -> p (c t)"), ps_a[:], ACT.Copy).then_inc(copied, 1)
                for h in range(H):
                    act.wait_ge(out_ready, h + 1)
                    act.activation(outs[h], (ps_a if h == 0 else ps_b)[:], ACT.Copy).then_inc(out_copied, 1)

            @block.tensor
            def _(pe):
                for u, (n, h) in enumerate(units):
                    if n == 0:
                        left, right = k, q
                    else:
                        left, right = near_k[:, (n - 1) % 2], near_q[:, (n - 1) % 2]
                        pe.wait_ge(factored, 2 * n)
                    if u >= 2:
                        pe.wait_ge(masked, u - 1)
                    for c in range(LT):
                        mm = pe.matmul(ps[:, u % 2, c * P:(c + 1) * P], left[rows[h], c * P:(c + 1) * P],
                                       right[rows[h], c * P:(c + 1) * P], start=True, stop=True)
                    mm.then_inc(products, 1)
                pe.wait_ge(factored, 2 * LEVELS + 2)
                for c in range(LT):
                    tr = pe.transpose(ps_a[:, c * P:(c + 1) * P], near_k[:, 1, c * P:(c + 1) * P], ident)
                tr.then_inc(turned, 1)
                pe.wait_ge(copied, 1)
                for h in range(H):
                    for c in range(LT):
                        mm = pe.matmul(ps_b[rows[h], c * P:(c + 1) * P], key_tok[:, c, rows[h]], values[h][:, c],
                                       start=True, stop=True)
                mm.then_inc(updates, 1)
                pe.wait_ge(states, LT - 1)
                pe.wait_ge(added, len(units) - H)
                for h in range(H):
                    out = (ps_a if h == 0 else ps_b)
                    for c in range(LT):
                        mm = pe.matmul(out[:, c * P:(c + 1) * P], values[h][:, c], score[:, h, c * P:(c + 1) * P],
                                       start=True, stop=(c == 0))
                        if c:
                            mm = pe.matmul(out[:, c * P:(c + 1) * P], state[rows[h], c],
                                           near_q[rows[h], 1, c * P:(c + 1) * P], start=False, stop=True)
                    mm.then_inc(out_ready, 1)


def soft(nc, tag, x, tmp, tiles, bias, scale, sign, rows=P):
    with Phase(nc, tag) as ph:
        biased, logged, done = (ph.sem(s) for s in ("biased", "logged", "done"))
        with ph.block() as block:
            @block.vector
            def _(dve):
                for t in range(tiles):
                    if bias is not None:
                        dve.tensor_scalar(x[:, t], x[:, t], bias[:, t:t + 1], None, ALU.add).then_inc(biased, 1)
                for t in range(tiles):
                    dve.wait_ge(logged, 3 * t + 3)
                    dve.scalar_tensor_tensor(x[:, t], x[:, t], 0.0, tmp[:, t], ALU.max if sign > 0 else ALU.min,
                                             ALU.add if sign > 0 else ALU.subtract).then_inc(done, 1)
                    if scale * sign != 1:
                        dve.wait_ge(done, t + 1)
                        dve.tensor_scalar(x[:, t], x[:, t], scale * sign, None, ALU.mult)

            @block.scalar
            def _(act):
                for t in range(tiles):
                    if bias is not None:
                        act.wait_ge(biased, t + 1)
                    for j, (src, func, s, b) in enumerate(((x, ACT.Abs, 1.0, 0.0), (tmp, ACT.Exp, -1.0, 0.0),
                                                           (tmp, ACT.Ln, 1.0, 1.0))):
                        act.activation(tmp[:, t], src[:, t], func, scale=s, bias=b).then_inc(logged, 1)
                        act.wait_ge(logged, 3 * t + j + 1)


def activate(nc, tag, out, x, tiles, func, scale=1.0):
    with Phase(nc, tag) as ph:
        with ph.block() as block:
            @block.scalar
            def _(act):
                for t in range(tiles):
                    act.activation(out[:, t], x[:, t], func, scale=scale)


def turn_rows(nc, tag, src, dst, tiles, ident):
    with Phase(nc, tag) as ph:
        ps = ph.psum("ps", [P, 2, BANK])
        turned, used = ph.sem("turned"), ph.sem("used")
        with ph.block() as block:
            @block.tensor
            def _(pe):
                for t in range(LT):
                    if t >= 2:
                        pe.wait_ge(used, t - 1)
                    for c in range(tiles):
                        tr = pe.transpose(ps[:, t % 2, c * P:(c + 1) * P], src[:, c, t * P:(t + 1) * P], ident)
                    tr.then_inc(turned, 1)

            @block.vector
            def _(dve):
                for t in range(LT):
                    dve.wait_ge(turned, t + 1)
                    dve.tensor_copy(dst[:, t, 0:tiles * P], ps[:, t % 2, 0:tiles * P]).then_inc(used, 1)


def hgrn_branch(nc, A, xn, out, work, small, masks, K):
    ones, ident = K[:, 0], K[:, 2]
    w = A["w_in_2"]
    with ExitStack() as ctx:
        q, f, key, v = (ctx.enter_context(nc.sbuf_tensor(f"hg_{n}", [P, 4, L], F32)) for n in ("q", "f", "key", "v"))
        v_tok = v[:].rearrange("p a (b c) -> p (a b) c", c=4 * P)
        project_each(nc, "hg_qfi", xn, L, [(w["hq"], q, 4, ACT.Silu), (w["hf"], f, 4, ACT.Copy),
                                           (w["hi"], work, 4, ACT.Copy)])
        turn_rows(nc, "hg_t", work, v_tok, 4, ident)
        activate(nc, "hg_k", key, f, 4, ACT.Sigmoid, -1.0)
        soft(nc, "hg_s", f, work, 4, None, -1.0, -1)
        for h in range(4):
            gated_tile(nc, f"hg{h}", q[:, h], key[:, h], f[:, h], [v_tok[:, :, h * P:(h + 1) * P]], [out[:, h]], work,
                       masks, ident)
        project(nc, "hg_g", w["hg"], xn, q, 4, L, ACT.Silu)
        rms_norm(nc, "hg_n", out, out, 4, 1, KEY, ones, small[:, 0:4], None, L)
        multiply(nc, "hg_m", out, out, q, 4)


def gla_branch(nc, A, xn, out, small, masks, K):
    ones, ident = K[:, 0], K[:, 2]
    w = A["w_in_2"]
    with ExitStack() as ctx:
        def sb(name, shape):
            return ctx.enter_context(nc.sbuf_tensor(name, shape, F32))
        q, k, f, tmp = (sb(f"gl_{n}", [P, 2, L]) for n in ("q", "k", "f", "tmp"))
        work, v = sb("gl_work", [P, 4, L]), sb("gl_v", [P, 4, L])
        gate_w = sb("gl_gate_w", [P, 2, P])
        v_tok = v[:].rearrange("p a (b c) -> p (a b) c", c=4 * P)
        project_each(nc, "gl_qki", xn, L, [(w["gq"], q, 2, ACT.Copy), (w["gk"], k, 2, ACT.Copy),
                                           (w["gv"], work, 4, ACT.Copy)])
        turn_rows(nc, "gl_t", work, v_tok, 4, ident)
        load(nc, "gl_load", [(gate_w[:], A["gla_gate_w"]), (tmp[:, 0], A["low_rank"])])
        with Phase(nc, "gl_f") as ph:
            ps = ph.psum("ps", [P, 2, L])
            multiplied = ph.sem("multiplied")
            with ph.block() as block:
                @block.tensor
                def _(pe):
                    for m in range(2):
                        for lo, hi in segments(L):
                            mm = pe.matmul(ps[:, m, lo:hi], gate_w[:, m], tmp[:, 0, lo:hi], start=True, stop=True)
                        mm.then_inc(multiplied, 1)

                @block.scalar
                def _(act):
                    for m in range(2):
                        act.wait_ge(multiplied, m + 1)
                        act.activation(f[:, m], ps[:, m], ACT.Copy)
                        act.activation(q[:, m], q[:, m], ACT.Copy, scale=64 ** -0.5)
        soft(nc, "gl_s", f, tmp, 2, small[:, 4:6], -1.0 / 16.0, -1)
        for m in range(2):
            gated_tile(nc, f"gl{m}", q[:, m], k[:, m], f[:, m], [v_tok[:, :, h * P:(h + 1) * P] for h in (2 * m, 2 * m + 1)],
                       [out[:, 2 * m], out[:, 2 * m + 1]], work, masks, ident)
        project(nc, "gl_g", w["gg"], xn, work, 4, L, ACT.Silu)
        rms_norm(nc, "gl_n", out, out, 4, 1, KEY, ones, small[:, 6:10], None, L)
        multiply(nc, "gl_m", out, out, work, 4)


def lru_branch(nc, A, xn, out, small, taps):
    w = A["w_in_2"]
    with ExitStack() as ctx:
        def sb(name, shape):
            return ctx.enter_context(nc.sbuf_tensor(name, shape, F32))
        u, r, i, gate = (sb(f"lr_{n}", [P, 4, L]) for n in ("u", "r", "i", "gate"))
        wa = sb("lr_w", [P, 2, 4, P])
        rate, tmp = sb("lr_rate", [P, 1, 4]), sb("lr_tmp", [P, 1, 4])
        project_conv(nc, "lr_x", w["lx"], xn, u, 4, taps, 6, 3, 0, None)
        project(nc, "lr_g", w["lg"], xn, gate, 4, L, ACT.Gelu_apprx_tanh)
        load(nc, "lr_load", [(wa[:], A["lru_w"]), (rate[:, 0], A["small_2"][:, 18:22])])
        soft(nc, "lr_s", rate, tmp, 1, None, -8.0, -1)
        with Phase(nc, "lr_r") as ph:
            ps = ph.psum("ps", [P, 2, 2, L])
            multiplied, emptied = ph.sem("multiplied"), ph.sem("emptied")
            with ph.block() as block:
                @block.tensor
                def _(pe):
                    for t in range(4):
                        if t >= 2:
                            pe.wait_ge(emptied, 2 * (t - 1))
                        for g in range(2):
                            for lo, hi in segments(L):
                                mm = pe.matmul(ps[:, t % 2, g, lo:hi], wa[:, g, t], u[:, t, lo:hi], start=True, stop=True)
                        mm.then_inc(multiplied, 1)

                @block.scalar
                def _(act):
                    for t in range(4):
                        act.wait_ge(multiplied, t + 1)
                        act.activation(r[:, t], ps[:, t % 2, 0], ACT.Sigmoid, bias=small[:, 10 + t:11 + t]).then_inc(emptied, 1)
                        act.activation(i[:, t], ps[:, t % 2, 1], ACT.Sigmoid, bias=small[:, 14 + t:15 + t]).then_inc(emptied, 1)
        with Phase(nc, "lr_scan") as ph:
            th, inv = ph.sb("th", [P, L]), ph.sb("inv", [P, L])
            step, lane, rooted = ph.sem("step"), ph.sem("lane"), ph.sem("rooted")
            with ph.block() as block:
                @block.vector
                def _(dve):
                    count = [0]
                    for t in range(4):
                        if t:
                            dve.wait_ge(lane, 3 * t)
                        chained(dve, dve.tensor_scalar(r[:, t], r[:, t], rate[:, 0, t:t + 1], None, ALU.mult), step, count)
                        dve.wait_ge(lane, 3 * t + 1)
                        chained(dve, dve.tensor_scalar(inv[:], th[:], -1.0, 1.0, ALU.mult, ALU.add), step, count)
                        chained(dve, dve.reciprocal(inv[:], inv[:]), step, count)
                        chained(dve, dve.scalar_tensor_tensor(inv[:], th[:], -2.0, inv[:], ALU.mult, ALU.mult), step, count)
                        chained(dve, dve.tensor_tensor(i[:, t], i[:, t], u[:, t], ALU.mult), step, count)
                        dve.wait_ge(lane, 3 * t + 3)
                        chained(dve, dve.tensor_tensor(i[:, t], i[:, t], inv[:], ALU.mult), step, count)
                        chained(dve, dve.tensor_tensor_scan(u[:, t], r[:, t], i[:, t], 0.0, ALU.mult, ALU.add), step, count)
                        chained(dve, dve.tensor_tensor(out[:, t], u[:, t], gate[:, t], ALU.mult), step, count)

                @block.scalar
                def _(act):
                    for t in range(4):
                        act.wait_ge(step, 8 * t + 1)
                        act.activation(th[:], r[:, t], ACT.Tanh).then_inc(lane, 1)
                        act.wait_ge(lane, 3 * t + 1)
                        act.activation(r[:, t], r[:, t], ACT.Exp).then_inc(lane, 1)
                        act.wait_ge(step, 8 * t + 4)
                        act.activation(inv[:], inv[:], ACT.Sqrt).then_inc(lane, 1)


def ssd_branch(nc, A, xn, out, scratch, small, taps, masks, K):
    ones, ident = K[:, 0], K[:, 2]
    w = A["w_in_2"]
    with ExitStack() as ctx:
        def sb(name, shape):
            return ctx.enter_context(nc.sbuf_tensor(name, shape, F32))
        xbc = sb("sd_xbc", [P, 6, L])
        dt = sb("sd_dt", [P, 2, L])
        cs, left = sb("sd_cs", [SH, L]), sb("sd_left", [SH, L])
        tok = sb("sd_tok", [P, LT, 5 * P])
        heads = sb("sd_heads", [P, LT, 2, SH])
        picks = sb("sd_picks", [SH, 2 * SH + 4, P])
        project_conv(nc, "sd_x", w["sxbc"], xn, xbc, 6, taps, 0, 3, 0, ACT.Silu)
        project(nc, "sd_d", w["glr_sdt"], xn, dt, 2, L)
        load(nc, "sd_load", [(picks[:], A["ssd_picks"]), (A["low_rank"], dt[:, 0])])
        with ExitStack() as inner:
            tmp = inner.enter_context(nc.sbuf_tensor("sd_tmp", [SH, 1, L], F32))
            soft(nc, "sd_s", dt[0:SH, 1:2], tmp, 1, small[0:SH, 22:23], 1.0, 1)
        with Phase(nc, "sd_cum") as ph:
            keep = ph.sb("keep", [SH, LT, P])
            rate = ph.sb("rate", [SH, 1])
            da = ph.sb("da", [SH, L])
            ps = ph.psum("ps", [P, LT, 2, SH])
            step, exped, turned = ph.sem("step"), ph.sem("exped"), ph.sem("turned")
            with ph.block() as block:
                @block.scalar
                def _(act):
                    act.activation(rate[:], small[0:SH, 23:24], ACT.Exp).then_inc(exped, 1)
                    act.wait_ge(step, 5)
                    act.activation(left[:], left[:], ACT.Exp).then_inc(exped, 1)

                @block.vector
                def _(dve):
                    count = [0]
                    chained(dve, dve.memset(keep[:], 1.0), step, count)
                    chained(dve, dve.memset(keep[:, :, 0:1], 0.0), step, count)
                    dve.wait_ge(exped, 1)
                    chained(dve, dve.tensor_scalar(da[:], dt[0:SH, 1], rate[:], -1.0, ALU.mult, ALU.mult), step, count)
                    chained(dve, dve.tensor_tensor_scan(cs[:], keep[:].rearrange("p c t -> p (c t)"), da[:], 0.0,
                                                        ALU.mult, ALU.add), step, count)
                    chunks = cs[:].rearrange("p (c t) -> p c t", t=P)
                    chained(dve, dve.tensor_tensor(left[:].rearrange("p (c t) -> p c t", t=P),
                                                   spread(chunks[:, :, P - 1:P], [SH, LT, P]), chunks, ALU.subtract),
                            step, count)
                    dve.wait_ge(exped, 2)
                    chained(dve, dve.tensor_tensor(left[:], left[:], dt[0:SH, 1], ALU.mult), step, count)
                    dve.wait_ge(turned, 1)
                    dve.tensor_copy(heads[:], ps[:])

                @block.tensor
                def _(pe):
                    pe.wait_ge(step, 6)
                    for c in range(LT):
                        pe.transpose(ps[:, c, 0], dt[0:SH, 1, c * P:(c + 1) * P], ident[0:SH, 0:SH])
                        tr = pe.transpose(ps[:, c, 1], left[:, c * P:(c + 1) * P], ident[0:SH, 0:SH])
                    tr.then_inc(turned, 1)
        turn_rows(nc, "sd_t", xbc, tok[:, :, 0:4 * P], 4, ident)
        turn_rows(nc, "sd_tb", xbc[:, 4:5], tok[:, :, 4 * P:5 * P], 1, ident)
        ssd_heads(nc, A, xbc, cs, tok, heads, picks, out, scratch, masks)
        skip_gate(nc, A, xn, xbc, out, small)
    rms_norm(nc, "sd_n", out, out, 2, 2, 256, ones, small[:, 28:32], None, L)


def ssd_heads(nc, A, xbc, cs, tok, heads, picks, out, scratch, masks):
    with Phase(nc, "sd_heads") as ph:
        both = scratch[:, 0:2]
        xdt, xw = ph.sb("xdt", [P, 2, LT, HD]), ph.sb("xw", [P, 2, LT, HD])
        score = scratch[:, 2:4]
        decay = ph.sb("decay", [P, L])
        c_dec = ph.sb("c_dec", [P, L])
        state = ph.sb("state", [P, LT, HD])
        causal = ph.sb("causal", [P, P])
        seg = ph.psum("seg", [P, 2, L])
        wide = ph.psum("wide", [P, L])
        upd = ph.psum("upd", [P, LT, HD])
        yp = ph.psum("yp", [P, BANK])
        landed, products, grouped, segs, low, exped, scored, widened, wide_exped, queried, xs, updates, states, outs, copied = (
            ph.sem(s) for s in ("landed", "products", "grouped", "segs", "low", "exped", "scored", "widened", "wide_exped",
                                "queried", "xs", "updates", "states", "outs", "copied"))
        with ph.block() as block:
            @block.sync
            def _(sp):
                sp.dma_start(causal[:], A["causal"]).then_inc(landed, 16)

            @block.tensor
            def _(pe):
                for g in range(2):
                    r = slice(64 * g, 64 * g + 64)
                    for c in range(LT):
                        at = slice(c * P, (c + 1) * P)
                        mm = pe.matmul(seg[:, g, at], xbc[r, 4, at], xbc[r, 5, at], start=True, stop=True)
                    mm.then_inc(products, 1)
                pe.wait_ge(grouped, 2)
                for m in range(4):
                    for e in range(2):
                        n, h = 2 * m + e, m + 4 * e
                        if n >= 2:
                            pe.wait_ge(low, n - 1)
                        for c in range(LT):
                            at = slice(c * P, (c + 1) * P)
                            pe.matmul(seg[:, e, at], picks[:, h], cs[:, at], start=True, stop=False)
                            mm = pe.matmul(seg[:, e, at], cs[:, at], picks[:, SH + h], start=False, stop=True)
                        mm.then_inc(segs, 1)
                    if m:
                        pe.wait_ge(wide_exped, m)
                    for lo, hi in segments(L):
                        mm = pe.matmul(wide[:, lo:hi], picks[:, 2 * SH + m], cs[:, lo:hi], start=True, stop=True)
                    mm.then_inc(widened, 1)
                    pe.wait_ge(xs, 4 * m + 4)
                    if m:
                        pe.wait_ge(states, (LT - 1) * m)
                    for e in range(2):
                        for c in range(LT):
                            mm = pe.matmul(upd[64 * e:64 * e + 64, c], tok[:, c, 4 * P + 64 * e:4 * P + 64 * e + 64],
                                           xw[:, e, c], start=True, stop=True)
                    mm.then_inc(updates, 1)
                    pe.wait_ge(queried, m + 1)
                    pe.wait_ge(states, (LT - 1) * (m + 1))
                    for e in range(2):
                        n, h = 2 * m + e, m + 4 * e
                        pe.wait_ge(scored, n + 1)
                        o = slice(64 * (h % 2), 64 * (h % 2) + 64)
                        r = slice(64 * e, 64 * e + 64)
                        for part in range(2):
                            if 2 * n + part:
                                pe.wait_ge(copied, 2 * n + part)
                            for c in range(4 * part, 4 * part + 4):
                                at, to = slice(c * P, (c + 1) * P), slice((c % 4) * P, (c % 4 + 1) * P)
                                mm = pe.matmul(yp[o, to], xdt[:, e, c], score[:, e, at], start=True, stop=(c == 0))
                                if c:
                                    mm = pe.matmul(yp[o, to], state[r, c], c_dec[r, at], start=False, stop=True)
                            mm.then_inc(outs, 1)

            @block.vector
            def _(dve):
                dve.wait_ge(landed, 16)
                dve.memset(state[:, 0], 0.0)
                for g in range(2):
                    dve.wait_ge(products, g + 1)
                    dve.tensor_tensor(both[:, g].rearrange("p (c t) -> p c t", t=P),
                                      seg[:, g].rearrange("p (c t) -> p c t", t=P),
                                      spread(causal[:].unsqueeze(1), [P, LT, P]), ALU.mult).then_inc(grouped, 1)
                dve.wait_ge(grouped, 2)
                for m in range(4):
                    if m:
                        dve.wait_ge(outs, 4 * m)
                    for e in range(2):
                        n, h = 2 * m + e, m + 4 * e
                        x = tok[:, :, h * HD:(h + 1) * HD]
                        for dst, which in ((xdt, 0), (xw, 1)):
                            dve.tensor_tensor(dst[:, e], x, spread(heads[:, :, which, h:h + 1], [P, LT, HD]),
                                              ALU.mult).then_inc(xs, 1)
                        dve.wait_ge(segs, n + 1)
                        dve.tensor_scalar(score[:, e], seg[:, e], 0.0, None, ALU.min).then_inc(low, 1)
                    dve.wait_ge(wide_exped, m + 1)
                    dve.tensor_tensor(c_dec[:], xbc[:, 5], decay[:], ALU.mult).then_inc(queried, 1)
                    for e in range(2):
                        dve.wait_ge(exped, 2 * m + e + 1)
                        dve.tensor_tensor(score[:, e], score[:, e], both[:, e], ALU.mult).then_inc(scored, 1)
                    dve.wait_ge(updates, m + 1)
                    for c in range(LT - 1):
                        if c or m:
                            dve.wait_ge(states, (LT - 1) * m + c)
                        dve.scalar_tensor_tensor(state[:, c + 1], state[:, c], decay[:, (c + 1) * P - 1:(c + 1) * P],
                                                 upd[:, c], ALU.mult, ALU.add).then_inc(states, 1)

            @block.scalar
            def _(act):
                for m in range(4):
                    for e in range(2):
                        act.wait_ge(low, 2 * m + e + 1)
                        act.activation(score[:, e], score[:, e], ACT.Exp).then_inc(exped, 1)
                    act.wait_ge(widened, m + 1)
                    if m:
                        act.wait_ge(queried, m)
                        act.wait_ge(states, (LT - 1) * m)
                    act.activation(decay[:], wide[:], ACT.Exp).then_inc(wide_exped, 1)
                    for e in range(2):
                        n, h = 2 * m + e, m + 4 * e
                        o = slice(64 * (h % 2), 64 * (h % 2) + 64)
                        for part in range(2):
                            act.wait_ge(outs, 2 * n + part + 1)
                            act.activation(out[o, h // 2, part * BANK:(part + 1) * BANK], yp[o, :],
                                           ACT.Copy).then_inc(copied, 1)


def skip_gate(nc, A, xn, xbc, out, small):
    z = xbc[:, 0:4]
    with Phase(nc, "sd_skip") as ph:
        with ph.block() as block:
            @block.vector
            def _(dve):
                for t in range(4):
                    dve.scalar_tensor_tensor(out[:, t], xbc[:, t], small[:, 24 + t:25 + t], out[:, t], ALU.mult, ALU.add)
    project(nc, "sd_z", A["w_in_2"]["sz"], xn, z, 4, L, ACT.Silu)
    multiply(nc, "sd_m", out, out, z, 4)


def merge(nc, A, xn, ys, merged):
    B = 4
    with Phase(nc, "merge") as ph:
        wgate = ph.sb("wgate", [P, 2, DT, P])
        wbr = ph.sb("wbr", [P, 2, 4, P])
        gates, part = ph.sb("gates", [P, 2, L]), ph.sb("part", [P, L])
        ps = ph.psum("ps", [P, 2, 2, L])
        gate_in = [ph.sem(f"gate_in{b}") for b in range(2)]
        branch_in = [ph.sem(f"branch_in{b}") for b in range(2)]
        gate_mul, branch_mul, gated, emptied, step = (ph.sem(s) for s in ("gate_mul", "branch_mul", "gated", "emptied", "step"))
        with ph.block() as block:
            @block.sync
            def _(sp):
                with sp.Fori(0, DT) as m:
                    for n in range(B):
                        b = n % 2
                        sp.wait_ge(gate_mul, m * B + (n + 1))
                        sp.dma_start(wgate[:, b], A["w_gates"][m * B + n]).then_inc(gate_in[b], 16)
                        sp.wait_ge(branch_mul, m * B + (n + 1))
                        sp.dma_start(wbr[:, b], A["w_branches"][m * B + n]).then_inc(branch_in[b], 16)

            @block.tensor
            def _(pe):
                pe.sem_inc(gate_mul, 2)
                pe.sem_inc(branch_mul, 2)
                pe.sem_inc(emptied, 2)
                pe.sem_inc(gated, 2)
                with pe.Fori(0, DT) as m:
                    for n in range(B):
                        b = n % 2
                        pe.wait_ge(gate_in[b], m * 32 + (16 * (n // 2) + 16))
                        pe.wait_ge(gated, m * B + (n + 1))
                        for k in range(DT):
                            for lo, hi in segments(L):
                                mm = pe.matmul(ps[:, b, 0, lo:hi], wgate[:, b, k], xn[:, k, lo:hi],
                                               start=(k == 0), stop=(k == DT - 1))
                        mm.then_inc(gate_mul, 1)
                        pe.wait_ge(branch_in[b], m * 32 + (16 * (n // 2) + 16))
                        pe.wait_ge(emptied, m * B + (n + 1))
                        for k in range(4):
                            for lo, hi in segments(L):
                                mm = pe.matmul(ps[:, b, 1, lo:hi], wbr[:, b, k], ys[:, 4 * n + k, lo:hi],
                                               start=(k == 0), stop=(k == 3))
                        mm.then_inc(branch_mul, 1)

            @block.scalar
            def _(act):
                with act.Fori(0, DT) as m:
                    for n in range(B):
                        act.wait_ge(gate_mul, m * B + (n + 3))
                        act.wait_ge(emptied, m * B + (n + 1))
                        act.activation(gates[:, n % 2], ps[:, n % 2, 0], ACT.Sigmoid).then_inc(gated, 1)

            @block.vector
            def _(dve):
                with dve.Fori(0, DT) as m:
                    for n in range(B):
                        dve.wait_ge(gated, m * B + (n + 3))
                        dve.wait_ge(branch_mul, m * B + (n + 3))
                        if n == 0:
                            dve.tensor_tensor(merged[:, m], ps[:, 0, 1], gates[:, 0], ALU.mult).then_inc(emptied, 1)
                        else:
                            dve.tensor_tensor(part[:], ps[:, n % 2, 1], gates[:, n % 2], ALU.mult).then_inc(emptied, 1)
                            dve.wait_ge(emptied, m * B + (n + 3))
                            dve.tensor_tensor(merged[:, m], merged[:, m], part[:], ALU.add).then_inc(step, 1)
                            dve.wait_ge(step, m * (B - 1) + n)


def mixer_layer(nc, A, x_in, x_out, K):
    ones = K[:, 0]
    with ExitStack() as ctx:
        def sb(name, shape):
            return ctx.enter_context(nc.sbuf_tensor(name, shape, F32))
        small = sb("m_small", [P, 48])
        taps = sb("m_taps", [P, 10, 5])
        masks = sb("m_masks", [P, LEVELS + 1, P])
        ys = sb("m_ys", [P, 16, L])
        xn = sb("m_xn", [P, DT, L])
        load(nc, "m_load", [(small[:], A["small_2"]), (taps[:], A["taps_2"]), (masks[:], A["level_masks"]),
                            (xn[:], x_in)])
        rms_norm(nc, "m_n", xn, xn, 1, DT, D, ones, small[:, 32:40], None, L)
        hgrn_branch(nc, A, xn, ys[:, 0:4], ys[:, 4:8], small, masks, K)
        ssd_branch(nc, A, xn, ys[:, 4:8], ys[:, 8:12], small, taps, masks, K)
        gla_branch(nc, A, xn, ys[:, 8:12], small, masks, K)
        lru_branch(nc, A, xn, ys[:, 12:16], small, taps)
        merged = sb("m_merged", [P, DT, L])
        merge(nc, A, xn, ys, merged)
        x = xn
        project_residual(nc, "m_out", A["w_out_2"], merged, None, x, x_in, x_out)


def ffn_layer(nc, A, x_in, out, K):
    FT = 22
    ones = K[:, 0]
    with ExitStack() as ctx:
        def sb(name, shape):
            return ctx.enter_context(nc.sbuf_tensor(name, shape, F32))
        small = sb("f_small", [P, 2, DT])
        x = sb("f_x", [P, DT, L])
        hidden = sb("f_hidden", [P, FT, L])
        with ExitStack() as inner:
            xn = inner.enter_context(nc.sbuf_tensor("f_xn", [P, DT, L], F32))
            load(nc, "f_load", [(x[:], x_in), (small[:], A["norms_2"])])
            rms_norm(nc, "f_n", x, xn, 1, DT, D, ones, small[:, 0], None, L)
            with Phase(nc, "f_in") as ph:
                wbuf = ph.sb("wbuf", [P, 2, 2 * DT, P])
                ps = ph.psum("ps", [P, 2, 2, L])
                act_out = ph.sb("act_out", [P, 2, L])
                loaded = [ph.sem(f"loaded{b}") for b in range(2)]
                multiplied, emptied, silued = (ph.sem(s) for s in ("multiplied", "emptied", "silued"))
                with ph.block() as block:
                    @block.sync
                    def _(sp):
                        load_weight_tiles(sp, A["w_ffn_in_2"], wbuf, FT, loaded, multiplied)

                    @block.tensor
                    def _(pe):
                        pe.sem_inc(multiplied, 2)
                        pe.sem_inc(emptied, 2)
                        with pe.Fori(0, FT // 2) as pair:
                            for b in range(2):
                                pe.wait_ge(loaded[b], pair * 16 + 16)
                                pe.wait_ge(emptied, pair * 2 + (b + 1))
                                for part in range(2):
                                    for k in range(DT):
                                        for lo, hi in segments(L):
                                            mm = pe.matmul(ps[:, b, part, lo:hi], wbuf[:, b, part * DT + k],
                                                           xn[:, k, lo:hi], start=(k == 0), stop=(k == DT - 1))
                                mm.then_inc(multiplied, 1)

                    @block.scalar
                    def _(act):
                        with act.Fori(0, FT // 2) as pair:
                            for b in range(2):
                                act.wait_ge(multiplied, pair * 2 + (b + 3))
                                act.wait_ge(emptied, pair * 2 + (b + 1))
                                act.activation(act_out[:, b], ps[:, b, 0], ACT.Silu).then_inc(silued, 1)

                    @block.vector
                    def _(dve):
                        with dve.Fori(0, FT // 2) as pair:
                            for b in range(2):
                                dve.wait_ge(silued, pair * 2 + (b + 1))
                                dve.tensor_tensor(hidden[:, pair * 2 + b], ps[:, b, 1], act_out[:, b],
                                                  ALU.mult).then_inc(emptied, 1)
        project_residual(nc, "f_out", A["w_ffn_out_2"], hidden, None, x)
        rms_norm(nc, "f_fn", x, x, 1, DT, D, ones, small[:, 1], None, L)
        store(nc, "f_store", out, x)


def weight_tiles(w):
    k, m = w.shape
    w = np.concatenate([w, np.zeros((k, -m % P), w.dtype)], axis=1)
    return w.reshape(k // P, P, -1, P).transpose(2, 1, 0, 3)


def channels(x):
    return x.T.reshape(-1, P, x.shape[0]).transpose(1, 0, 2)


def columns(v):
    return np.moveaxis(v.reshape(*v.shape[:-1], -1, P), -1, 0)


def swap_matrix(blocks):
    m = np.zeros((P, P), np.float32)
    for first, w in blocks:
        for half in range(2):
            for j in range(w):
                a = first + half * 2 * w + j
                m[a + w, a] = -1.0
                m[a, a + w] = 1.0
    return m


def rope_tables(blocks):
    cos, sin = np.ones((P, N), np.float32), np.zeros((P, N), np.float32)
    t = np.arange(L)
    for first, w in blocks:
        inv = np.float32(10000.0) ** (-np.arange(w, dtype=np.float32) / np.float32(w))
        for half, pos in enumerate((t // GRID, t % GRID)):
            angle = (pos.astype(np.float32)[None] * inv[:, None]).astype(np.float64)
            for part in range(2):
                rows = slice(first + half * 2 * w + part * w, first + half * 2 * w + (part + 1) * w)
                cos[rows, :L], sin[rows, :L] = np.cos(angle), np.sin(angle)
    return cos, sin


def attention_arrays(i):
    w = i["attn_w_in"][0]
    q, k, v, cq, ckv, kpe, gate = np.split(w, np.cumsum([512, 128, 128, 256, 128, 32]), axis=1)
    q = q.reshape(D, 2, 4, HD).transpose(0, 2, 1, 3).reshape(D, 512)
    kpe = np.concatenate([np.zeros((D, HD), w.dtype), kpe, np.zeros((D, P - HD - ROPE), w.dtype)], axis=1)
    uq = i["mla_w_uq"][0].reshape(256, QH, HD + ROPE)
    uq = np.concatenate([uq, np.zeros((256, QH, P - HD - ROPE), w.dtype)], axis=2).reshape(256, QH * P)
    ukv = i["mla_w_ukv"][0].reshape(P, QH, 2 * HD)
    wk = np.concatenate([ukv[:, :, :HD], np.zeros((P, QH, HD), w.dtype)], axis=2)
    qn, kn = i["attn_q_norm"][0], i["attn_k_norm"][0]
    qk = np.stack([np.tile(qn, 2)] * 4 + [np.tile(kn, 2)], axis=1)
    small = np.concatenate([qk, columns(i["mla_q_norm"][0]), columns(i["mla_kv_norm"][0])], axis=1)
    a_blocks, m_blocks = [(0, 16), (HD, 16)], [(HD, 8)]
    half = np.kron(np.eye(2), np.ones((HD, HD)))
    return {
        "x": channels(i["x"][0]), "ctx": channels(i["ctx"][0]),
        "c2": columns(np.stack([i["c"][0], i["c_ctx"]])).transpose(0, 2, 1),
        "ada_w": np.concatenate([weight_tiles(i["ada_w"][0]), weight_tiles(i["ada_w"][1])])
                   .reshape(-1, 4, P, DT, P).transpose(0, 2, 1, 3, 4).reshape(-1, P, 4 * DT, P),
        "ada_b": columns(i["ada_b"]).reshape(P, -1), "norm_w": columns(i["norm_w"]),
        "attn_w_lat": weight_tiles(np.concatenate([q, cq, gate], axis=1)),
        "attn_w_both": weight_tiles(np.concatenate([k, ckv, kpe, v], axis=1)),
        "attn_small": small, "mla_w_uq": weight_tiles(uq), "mla_wk": wk,
        "mla_wv": ukv[:, :, HD:].reshape(P, QH * HD), "attn_w_out": weight_tiles(i["attn_w_out"][0]),
        "rope": np.stack(rope_tables(a_blocks) + rope_tables(m_blocks)),
        "matrices": np.stack([np.ones((P, P)), half, np.eye(P), swap_matrix(a_blocks), swap_matrix(m_blocks)],
                             axis=1).astype(np.float32),
    }


def hyena_arrays(i):
    t = np.linspace(0.0, 1.0, L, dtype=np.float32)[:, None]
    w = (np.float32(2.0 * math.pi / L)) * np.arange(L, dtype=np.float32)[:, None]
    bands = np.linspace(1e-4, 15, 16, dtype=np.float32)
    angle = (w * bands).astype(np.float64)
    emb = np.concatenate([t, np.cos(angle), -np.sin(angle)], axis=-1).astype(np.float32)
    deltas = np.abs(np.linspace(math.log(1e-2) / 1.5, math.log(1e-2) / 0.3, D))
    decay = np.exp(-t.astype(np.float64) * deltas).astype(np.float32)
    parity = np.concatenate([np.arange(0, L, 2), np.arange(1, L, 2)])
    k = np.arange(L // 2)

    def angle_of(rows, frequencies):
        return np.pi / L * np.outer(rows, frequencies + 0.5)

    def pair_tables(first, second):
        return np.concatenate([weight_tiles(first), weight_tiles(second)], axis=2).astype(np.float32)

    lag_tables = pair_tables(np.cos(angle_of(parity, k)), np.sin(angle_of(parity, k)))
    tables = pair_tables(np.cos(angle_of(parity + 0.5, k)), np.cos(angle_of(parity + 0.5, L - 1 - k)))
    pairs = np.concatenate([k, L - 1 - k])
    back_tables = weight_tiles(np.cos(angle_of(parity + 0.5, pairs)).T).astype(np.float32)
    w3 = np.concatenate([i["hy_ffn_w3"][0], i["hy_ffn_b3"]], axis=0).reshape(65, 2, 2, D).transpose(1, 0, 2, 3)
    taps = np.concatenate([i["hy_conv_w"][0], i["hy_conv_b"]], axis=0)
    return {
        "hy_emb": emb[parity].T, "hy_w1": i["hy_ffn_w1"][0], "hy_w2": i["hy_ffn_w2"][0],
        "hy_small": np.stack([i["hy_ffn_b1"][0], i["hy_ffn_b2"][0], i["hy_freq"][0]], axis=1),
        "hy_w3": w3, "hy_decay": decay[parity].reshape(LT, P, D), "hy_lag_tables": lag_tables, "hy_tables": tables,
        "hy_back_tables": back_tables,
        "hy_skip": np.broadcast_to(i["hy_skip"][0][:, None], (2, P, D)),
        "hy_taps": columns(taps).transpose(0, 2, 1), "hy_w_in": weight_tiles(i["hy_w_in"][0]),
        "hy_w_out": weight_tiles(i["hy_w_out"][0]), "final_norm_w": columns(i["final_norm_w"]),
    }


def block_arrays(i):
    i = {k[:-2]: v for k, v in i.items() if k.endswith("_2")}
    w = i["w_in"][0]
    sizes = [512, 512, 512, 512, 512, 768, 8, 256, 256, 512, 512, 16, 512, 512, 4096]
    names = ["hq", "hf", "hi", "hg", "sz", "sxbc", "sdt", "gq", "gk", "gv", "gg", "glr", "lx", "lg", "mg"]
    parts = {n: weight_tiles(p) for n, p in zip(names, np.split(w, np.cumsum(sizes)[:-1], axis=1))}
    parts["glr_sdt"] = np.concatenate([parts.pop("glr"), parts.pop("sdt")])
    gates = parts.pop("mg").reshape(4, DT, P, DT, P).transpose(1, 0, 2, 3, 4).reshape(4 * DT, P, DT, P)
    branches = np.stack([weight_tiles(b) for b in i["w_branch"][0]], axis=1).reshape(4 * DT, P, 4, P)
    small = np.zeros((P, 48), np.float32)

    def put(at, cols):
        small[:cols.shape[0], at:at + cols.shape[1]] = cols

    put(0, np.tile(i["hgrn_norm_w"][0][:, None], (1, 4)))
    put(4, columns(i["gla_gate_b"][0]))
    put(6, np.tile(i["gla_norm_w"][0][:, None], (1, 4)))
    put(10, columns(i["lru_ba"][0]))
    put(14, columns(i["lru_bx"][0]))
    put(18, columns(i["lru_lambda"][0]))
    put(22, i["ssd_dt_bias"][0][:, None])
    put(23, i["ssd_a_log"][0][:, None])
    put(24, columns(np.repeat(i["ssd_d"][0], HD)))
    put(28, columns(i["ssd_norm_w"][0]))
    put(32, columns(i["norm_mix_w"][0]))
    taps = np.concatenate([np.concatenate([i["ssd_conv_w"][0], i["ssd_conv_b"]]),
                           np.concatenate([i["lru_conv_w"][0], i["lru_conv_b"]])], axis=1)
    gate_w = np.zeros((P, 2 * P), np.float32)
    gate_w[:16] = i["gla_gate_w"][0]
    lru = np.zeros((P, 2, 4, P), np.float32)
    for n, name in enumerate(("lru_wa", "lru_wx")):
        for b in range(8):
            r = slice(64 * (b % 2), 64 * (b % 2) + 64)
            lru[r, n, b // 2, r] = i[name][0][b]
    j, k = np.arange(P)[:, None], np.arange(P)[None]
    masks = [j == k]
    for level in range(LEVELS):
        half = 2 ** level
        masks.append((j // (2 * half) == k // (2 * half)) & (j // half % 2 == 0) & (k // half % 2 == 1))
    picks = np.zeros((SH, 2 * SH + 4, P), np.float32)
    for h in range(SH):
        picks[h, h], picks[h, SH + h] = 1.0, -1.0
    for m in range(4):
        picks[m, 2 * SH + m, :64], picks[4 + m, 2 * SH + m, 64:] = 1.0, 1.0
    ffn = i["w_ffn_in"][0]
    ffn = np.concatenate([weight_tiles(ffn[:, :2816]), weight_tiles(ffn[:, 2816:])], axis=2)
    out = {f"w_in_2_{n}": p for n, p in parts.items()}
    out.update({
        "w_gates": gates, "w_branches": branches, "small_2": small, "taps_2": columns(taps).transpose(0, 2, 1),
        "gla_gate_w": gate_w.reshape(P, 2, P), "lru_w": lru, "level_masks": np.stack(masks, axis=1).astype(np.float32),
        "causal": (j <= k).astype(np.float32), "ssd_picks": picks, "w_out_2": weight_tiles(i["w_out"][0]),
        "w_ffn_in_2": ffn, "w_ffn_out_2": weight_tiles(i["w_ffn_out"][0]),
        "norms_2": columns(np.stack([i["norm_ffn_w"][0], i["norm_f_w"]])),
    })
    return out


def build(nc, A):
    A["w_in_2"] = {name[7:]: ap for name, ap in A.items() if name.startswith("w_in_2_")}
    with ExitStack() as ctx:
        K = ctx.enter_context(nc.sbuf_tensor("matrices", [P, 5, P], F32))
        mod = ctx.enter_context(nc.sbuf_tensor("mod", [P, 6 * DT, 2], F32))
        one_plus = ctx.enter_context(nc.sbuf_tensor("one_plus", [P, 2, 2, DT], F32))
        load(nc, "load_matrices", [(K[:], A["matrices"])])
        modulation(nc, A, mod, one_plus)
        attention_layer(nc, A, A["x1"], mod, one_plus, K)
        hyena_layer(nc, A, A["x1"], A["x2"], mod, one_plus, K)
        mixer_layer(nc, A, A["x2"], A["x3"], K)
        ffn_layer(nc, A, A["x3"], A["out"], K)


def kernel(**inputs):
    import concourse.bacc as bacc
    from concourse.bass_utils import run_bass_kernel_spmd

    nc = bacc.Bacc("TRN2", target_bir_lowering=False, num_devices=1)
    i = {name: np.asarray(value) for name, value in inputs.items()}
    arrays = {**attention_arrays(i), **hyena_arrays(i), **block_arrays(i)}
    arrays = {name: np.ascontiguousarray(a) for name, a in arrays.items()}
    A = {name: nc.dram_tensor(f"in_{name}", a.shape, mybir.dt.from_np(a.dtype), kind="ExternalInput").ap()
         for name, a in arrays.items()}
    for name in ("x1", "x2", "x3"):
        A[name] = nc.dram_tensor(name, (P, DT, L), F32, kind="Internal").ap()
    A["spectrum"] = nc.dram_tensor("spectrum", (4 * PAIRS, P, 4, BANK), F32, kind="Internal").ap()
    A["low_rank"] = nc.dram_tensor("low_rank", (P, L), F32, kind="Internal").ap()
    A["factor"] = nc.dram_tensor("factor", (LT, P, D), F32, kind="Internal").ap()
    A["out"] = nc.dram_tensor("out", (P, DT, L), F32, kind="ExternalOutput").ap()
    build(nc, A)
    r = run_bass_kernel_spmd(nc, [{f"in_{name}": a for name, a in arrays.items()}], core_ids=[0])
    out = r.results[0]["out"]
    return out.transpose(2, 1, 0).reshape(1, L, D)
```
